# Optimizing a Trainium2 kernel written in Bass

```python
import math
import jax
import jax.numpy as jnp
from jax import lax
import numpy as np

D_MODEL = 1024
BATCH = 1
SEQ = 128
DEPTH = 2
DEC_BATCH = 1
DEC_SEQ = 256
PAST_LEN = 128

GRID_W = 64
CHUNK = 128
Q_BLOCK = 128
SGU_GROUPS = 4
SGU_WIDTH = 256
MLA_HEADS = 4
MLA_Q_LORA = 256
MLA_KV_LORA = 128
MLA_NOPE = 64
MLA_ROPE = 32
MLA_V = 64
NA_HEADS = 4
NA_HEAD_DIM = 64
NA_WIN_ROWS = 8
NA_WIN_COLS = 16
DIFF_HEADS = 4
DIFF_QK_DIM = 64
DIFF_V_DIM = 2 * DIFF_QK_DIM
N_BRANCHES = 4
PEER_HEADS = 8
PEER_N_KEYS = 128
PEER_N_EXPERTS = PEER_N_KEYS * PEER_N_KEYS
PEER_KEY_DIM = 256
PEER_TOPK = 16
PEER_TOKEN_BLOCK = 128

ROPE_THETA = 10000.0
LN_EPS = 1e-6
NEG_BIG = -1e30
DEEPNORM_ALPHA = (2 * DEPTH) ** 0.25
DEEPNORM_BETA = (8 * DEPTH) ** -0.25

SPLITS = (SGU_WIDTH, SGU_WIDTH,
          MLA_Q_LORA, MLA_KV_LORA, MLA_ROPE,
          NA_HEADS * NA_HEAD_DIM, NA_HEADS * NA_HEAD_DIM, NA_HEADS * NA_HEAD_DIM,
          DIFF_HEADS * 2 * DIFF_QK_DIM, DIFF_HEADS * 2 * DIFF_QK_DIM, DIFF_HEADS * DIFF_V_DIM)
IN_WIDTH = sum(SPLITS)
SPLIT_POINTS = tuple(sum(SPLITS[:i + 1]) for i in range(len(SPLITS) - 1))

kernel_name = 'hybrid_diffusion_prefix_trunk_step'

def layer_norm(x):
    xf = x.astype(jnp.float32)
    mu = jnp.mean(xf, axis=-1, keepdims=True)
    var = jnp.mean(jnp.square(xf - mu), axis=-1, keepdims=True)
    return ((xf - mu) * lax.rsqrt(var + LN_EPS)).astype(x.dtype)

def layer_norm_affine(x, g, b):
    return layer_norm(x) * g + b

def rms_norm(x, g):
    xf = x.astype(jnp.float32)
    y = xf * lax.rsqrt(jnp.mean(jnp.square(xf), axis=-1, keepdims=True) + LN_EPS)
    return y.astype(x.dtype) * g

def modulate(x, shift, scale):
    return layer_norm(x) * (1 + scale[:, None]) + shift[:, None]

def axial_rope_angles(n_tokens, rot_dim):
    t = jnp.arange(n_tokens)
    row = (t // GRID_W).astype(jnp.float32)
    col = (t % GRID_W).astype(jnp.float32)
    n_freq = rot_dim // 4
    inv_freq = ROPE_THETA ** (-jnp.arange(n_freq, dtype=jnp.float32) / n_freq)
    return jnp.concatenate([row[:, None] * inv_freq, col[:, None] * inv_freq], axis=-1)

def apply_rope(x, angles):
    d2 = x.shape[-1] // 2
    cos = jnp.cos(angles)[:, None, :].astype(x.dtype)
    sin = jnp.sin(angles)[:, None, :].astype(x.dtype)
    x1, x2 = x[..., :d2], x[..., d2:]
    return jnp.concatenate([x1 * cos - x2 * sin, x2 * cos + x1 * sin], axis=-1)

def rope_pair(x, angles):
    B, T, H, M, d = x.shape
    return apply_rope(x.reshape(B, T, H * M, d), angles).reshape(B, T, H, M, d)

def attend_blocks(q, k, v):
    B, T, H, dq = q.shape
    scale = dq ** -0.5
    qb = q.reshape(B, T // Q_BLOCK, Q_BLOCK, H, dq).swapaxes(0, 1)

    def one(q_blk):
        s = jnp.einsum('bqhd,bkhd->bhqk', q_blk, k).astype(jnp.float32) * scale
        p = jax.nn.softmax(s, axis=-1).astype(v.dtype)
        return jnp.einsum('bhqk,bkhd->bqhd', p, v)

    return lax.map(one, qb).swapaxes(0, 1).reshape(B, T, H, v.shape[-1])

def spatial_gating(u, v, norm_g, w_s, b_s):
    B, T, _ = v.shape
    vn = layer_norm(v) * norm_g
    vg = vn.reshape(B, T // CHUNK, CHUNK, SGU_GROUPS, SGU_WIDTH // SGU_GROUPS)
    mixed = jnp.einsum('gpq,bnqgc->bnpgc', w_s, vg) + b_s.T[None, None, :, :, None]
    return u * mixed.reshape(B, T, SGU_WIDTH)

def mla_keys(ckv_n, k_rope, w_ukv):
    B, L, _ = ckv_n.shape
    kv = (ckv_n @ w_ukv).reshape(B, L, MLA_HEADS, MLA_NOPE + MLA_V)
    k_nope, v = kv[..., :MLA_NOPE], kv[..., MLA_NOPE:]
    k = jnp.concatenate([k_nope, jnp.broadcast_to(k_rope, (B, L, MLA_HEADS, MLA_ROPE))], axis=-1)
    return k, v

def neighborhood_attend(q, k, v, k_ctx, v_ctx, rpb):
    B, T, H, d = q.shape
    rows = T // GRID_W
    wr = min(NA_WIN_ROWS, rows)
    scale = d ** -0.5
    qg = q.reshape(B, rows, GRID_W, H, d)
    kg = k.reshape(B, rows, GRID_W, H, d)
    vg = v.reshape(B, rows, GRID_W, H, d)
    col = jnp.arange(GRID_W)
    col_start = jnp.clip(col - NA_WIN_COLS // 2, 0, GRID_W - NA_WIN_COLS)
    col_in = (col[None, :] >= col_start[:, None]) & (col[None, :] < col_start[:, None] + NA_WIN_COLS)
    dc = jnp.clip(col[None, :] - col[:, None], -(NA_WIN_COLS - 1), NA_WIN_COLS - 1) + NA_WIN_COLS - 1
    rpb_cols = rpb[:, :, dc]

    def one_row(r):
        start = jnp.clip(r - wr // 2, 0, rows - wr)
        q_r = lax.dynamic_index_in_dim(qg, r, axis=1, keepdims=False)
        k_w = lax.dynamic_slice_in_dim(kg, start, wr, axis=1)
        v_w = lax.dynamic_slice_in_dim(vg, start, wr, axis=1)
        dr = start + jnp.arange(wr) - r + NA_WIN_ROWS - 1
        bias = rpb_cols[:, dr].transpose(0, 2, 1, 3)
        s_win = jnp.einsum('bqhd,bjkhd->bhqjk', q_r, k_w).astype(jnp.float32) * scale + bias[None]
        s_win = jnp.where(col_in[None, None, :, None, :], s_win, NEG_BIG)
        s_ctx = jnp.einsum('bqhd,blhd->bhql', q_r, k_ctx).astype(jnp.float32) * scale
        s = jnp.concatenate([s_win.reshape(B, H, GRID_W, wr * GRID_W), s_ctx], axis=-1)
        p = jax.nn.softmax(s, axis=-1).astype(v.dtype)
        p_win = p[..., :wr * GRID_W].reshape(B, H, GRID_W, wr, GRID_W)
        p_ctx = p[..., wr * GRID_W:]
        return (jnp.einsum('bhqjk,bjkhd->bqhd', p_win, v_w)
                + jnp.einsum('bhql,blhd->bqhd', p_ctx, v_ctx))

    out = lax.map(one_row, jnp.arange(rows))
    return out.transpose(1, 0, 2, 3, 4).reshape(B, T, H, d)

def differential_attend(q, k, v, p, lambda_init):
    B, T, H, _, d = q.shape
    lam = (jnp.exp(jnp.sum((p['diff_lambda_q1'] * p['diff_lambda_k1']).astype(jnp.float32)))
           - jnp.exp(jnp.sum((p['diff_lambda_q2'] * p['diff_lambda_k2']).astype(jnp.float32)))
           + lambda_init)
    scale = d ** -0.5
    qb = q.reshape(B, T // Q_BLOCK, Q_BLOCK, H, 2, d).swapaxes(0, 1)

    def one(q_blk):
        s = jnp.einsum('bqhmd,bkhmd->bhmqk', q_blk, k).astype(jnp.float32) * scale
        pr = jax.nn.softmax(s, axis=-1)
        w = (pr[:, :, 0] - lam * pr[:, :, 1]).astype(v.dtype)
        return jnp.einsum('bhqk,bkhd->bqhd', w, v)

    o = lax.map(one, qb).swapaxes(0, 1).reshape(B, T, H, DIFF_V_DIM)
    o = rms_norm(o, p['diff_norm_g']) * (1 - lambda_init)
    return o.reshape(B, T, H * DIFF_V_DIM)

def merge_branches(h, out_a, out_b, out_c, out_d, p):
    B, T, _ = h.shape
    g = jax.nn.sigmoid(h @ p['w_gate'] + p['b_gate']).reshape(B, T, N_BRANCHES, D_MODEL)
    merged = (g[:, :, 0] * (out_a.reshape(B, T, -1) @ p['w_branch_a'])
              + g[:, :, 1] * (out_b.reshape(B, T, -1) @ p['w_branch_b'])
              + g[:, :, 2] * (out_c.reshape(B, T, -1) @ p['w_branch_c'])
              + g[:, :, 3] * (out_d.reshape(B, T, -1) @ p['w_branch_d']))
    return merged @ p['w_out']

def token_mixing(h, p, lambda_init, cache):
    B, T, _ = h.shape
    (a_u, a_v, m_cq, m_ckv, m_krope, n_q, n_k, n_v,
     d_q, d_k, d_v) = jnp.split(h @ p['w_in'], SPLIT_POINTS, axis=-1)
    out_a = spatial_gating(jax.nn.gelu(a_u, approximate=False), jax.nn.gelu(a_v, approximate=False),
                           p['sgu_norm_g'], p['sgu_w'], p['sgu_b'])
    m_q = (rms_norm(m_cq, p['mla_q_norm_g']) @ p['mla_w_uq']).reshape(B, T, MLA_HEADS, MLA_NOPE + MLA_ROPE)
    m_ckv = rms_norm(m_ckv, p['mla_kv_norm_g'])
    m_kr = m_krope[:, :, None, :]
    n_q = n_q.reshape(B, T, NA_HEADS, NA_HEAD_DIM)
    n_k = n_k.reshape(B, T, NA_HEADS, NA_HEAD_DIM)
    n_v = n_v.reshape(B, T, NA_HEADS, NA_HEAD_DIM)
    d_q = d_q.reshape(B, T, DIFF_HEADS, 2, DIFF_QK_DIM)
    d_k = d_k.reshape(B, T, DIFF_HEADS, 2, DIFF_QK_DIM)
    d_v = d_v.reshape(B, T, DIFF_HEADS, DIFF_V_DIM)
    if cache is None:
        k_b, v_b = mla_keys(m_ckv, m_kr, p['mla_w_ukv'])
        out_b = attend_blocks(m_q, k_b, v_b)
        out_c = attend_blocks(n_q, n_k, n_v)
        out_d = differential_attend(d_q, d_k, d_v, p, lambda_init)
        ctx_tensors = (m_ckv, m_krope, n_k, n_v, d_k.reshape(B, T, DIFF_HEADS, 2 * DIFF_QK_DIM), d_v)
    else:
        ckv_c, kr_c, nk_c, nv_c, dk_c, dv_c = cache
        L = ckv_c.shape[1]
        ang_b = axial_rope_angles(T, MLA_ROPE)
        ang_d = axial_rope_angles(T, DIFF_QK_DIM)
        m_q = jnp.concatenate([m_q[..., :MLA_NOPE], apply_rope(m_q[..., MLA_NOPE:], ang_b)], axis=-1)
        k_lat, v_lat = mla_keys(m_ckv, apply_rope(m_kr, ang_b), p['mla_w_ukv'])
        k_ctx, v_ctx = mla_keys(ckv_c, kr_c[:, :, None, :], p['mla_w_ukv'])
        out_b = attend_blocks(m_q, jnp.concatenate([k_lat, k_ctx], axis=1),
                              jnp.concatenate([v_lat, v_ctx], axis=1))
        out_c = neighborhood_attend(n_q, n_k, n_v, nk_c, nv_c, p['na_rpb'])
        d_k_all = jnp.concatenate([rope_pair(d_k, ang_d),
                                   dk_c.reshape(B, L, DIFF_HEADS, 2, DIFF_QK_DIM)], axis=1)
        d_v_all = jnp.concatenate([d_v, dv_c], axis=1)
        out_d = differential_attend(rope_pair(d_q, ang_d), d_k_all, d_v_all, p, lambda_init)
        ctx_tensors = None
    return merge_branches(h, out_a, out_b, out_c, out_d, p), ctx_tensors

def peer_ffn(h, w_q, subkeys, u_tab, v_tab):
    B, T, D = h.shape
    n_tok = B * T
    n_blk = n_tok // PEER_TOKEN_BLOCK
    x = h.reshape(n_tok, D)
    q = (x @ w_q).reshape(n_tok, PEER_HEADS, 2, PEER_KEY_DIM // 2)
    s = jnp.einsum('thpd,hpnd->thpn', q, subkeys).astype(jnp.float32)
    half_s, half_i = lax.top_k(s, PEER_TOPK)
    cand = half_s[:, :, 0, :, None] + half_s[:, :, 1, None, :]
    best_s, best_i = lax.top_k(cand.reshape(n_tok, PEER_HEADS, PEER_TOPK * PEER_TOPK), PEER_TOPK)
    i1 = jnp.take_along_axis(half_i[:, :, 0], best_i // PEER_TOPK, axis=-1)
    i2 = jnp.take_along_axis(half_i[:, :, 1], best_i % PEER_TOPK, axis=-1)
    experts = (i1 * PEER_N_KEYS + i2).reshape(n_blk, PEER_TOKEN_BLOCK, PEER_HEADS * PEER_TOPK)
    gates = jax.nn.softmax(best_s, axis=-1).astype(h.dtype).reshape(n_blk, PEER_TOKEN_BLOCK, PEER_HEADS * PEER_TOPK)
    xb = x.reshape(n_blk, PEER_TOKEN_BLOCK, D)

    def expert_block(args):
        xt, e, g = args
        act = jax.nn.gelu(jnp.einsum('td,tkd->tk', xt, jnp.take(u_tab, e, axis=0)), approximate=False) * g
        return jnp.einsum('tk,tkd->td', act, jnp.take(v_tab, e, axis=0))

    return lax.map(expert_block, (xb, experts, gates)).reshape(B, T, D)

def trunk_layer(x, cond, p, lambda_init, cache):
    sh1, sc1, g1, sh2, sc2, g2 = jnp.split(jax.nn.silu(cond) @ p['w_mod'] + p['b_mod'], 6, axis=-1)
    mix, ctx_tensors = token_mixing(modulate(x, sh1, sc1), p, lambda_init, cache)
    x = layer_norm_affine(DEEPNORM_ALPHA * x + g1[:, None] * mix, p['ln1_g'], p['ln1_b'])
    ffn = peer_ffn(modulate(x, sh2, sc2), p['peer_w_q'], p['peer_subkeys'], p['peer_u'], p['peer_v'])
    x = layer_norm_affine(DEEPNORM_ALPHA * x + g2[:, None] * ffn, p['ln2_g'], p['ln2_b'])
    return x, ctx_tensors

def setup_inputs(seed: int = 0) -> dict:
    key = jax.random.key(seed)
    ks = iter(jax.random.split(key, 64))

    def nrm(shape, scale=1.0):
        return scale * jax.random.normal(next(ks), shape, jnp.float32)

    def gain(shape):
        return 1.0 + nrm(shape, 0.01)

    D = D_MODEL
    return {
        'x_prompt': nrm((BATCH, SEQ, D)),
        'x_sample': nrm((DEC_BATCH, DEC_SEQ, D)),
        'cache_mla_ckv': nrm((DEC_BATCH, DEPTH, PAST_LEN, MLA_KV_LORA)),
        'cache_mla_krope': nrm((DEC_BATCH, DEPTH, PAST_LEN, MLA_ROPE)),
        'cache_na_k': nrm((DEC_BATCH, DEPTH, PAST_LEN, NA_HEADS, NA_HEAD_DIM)),
        'cache_na_v': nrm((DEC_BATCH, DEPTH, PAST_LEN, NA_HEADS, NA_HEAD_DIM)),
        'cache_diff_k': nrm((DEC_BATCH, DEPTH, PAST_LEN, DIFF_HEADS, 2 * DIFF_QK_DIM)),
        'cache_diff_v': nrm((DEC_BATCH, DEPTH, PAST_LEN, DIFF_HEADS, DIFF_V_DIM)),
        'c': nrm((DEC_BATCH, D)),
        'c_ctx': nrm((D,)),
        'w_mod': nrm((DEPTH, D, 6 * D), D ** -0.5),
        'b_mod': nrm((DEPTH, 6 * D), 0.01),
        'w_in': nrm((DEPTH, D, IN_WIDTH), D ** -0.5),
        'sgu_norm_g': gain((DEPTH, SGU_WIDTH)),
        'sgu_w': nrm((DEPTH, SGU_GROUPS, CHUNK, CHUNK), CHUNK ** -0.5),
        'sgu_b': gain((DEPTH, SGU_GROUPS, CHUNK)),
        'mla_q_norm_g': gain((DEPTH, MLA_Q_LORA)),
        'mla_w_uq': nrm((DEPTH, MLA_Q_LORA, MLA_HEADS * (MLA_NOPE + MLA_ROPE)), MLA_Q_LORA ** -0.5),
        'mla_kv_norm_g': gain((DEPTH, MLA_KV_LORA)),
        'mla_w_ukv': nrm((DEPTH, MLA_KV_LORA, MLA_HEADS * (MLA_NOPE + MLA_V)), MLA_KV_LORA ** -0.5),
        'na_rpb': nrm((DEPTH, NA_HEADS, 2 * NA_WIN_ROWS - 1, 2 * NA_WIN_COLS - 1), 0.1),
        'diff_lambda_q1': nrm((DEPTH, DIFF_QK_DIM), 0.1),
        'diff_lambda_k1': nrm((DEPTH, DIFF_QK_DIM), 0.1),
        'diff_lambda_q2': nrm((DEPTH, DIFF_QK_DIM), 0.1),
        'diff_lambda_k2': nrm((DEPTH, DIFF_QK_DIM), 0.1),
        'diff_norm_g': gain((DEPTH, DIFF_V_DIM)),
        'w_branch_a': nrm((DEPTH, SGU_WIDTH, D), SGU_WIDTH ** -0.5),
        'w_branch_b': nrm((DEPTH, MLA_HEADS * MLA_V, D), (MLA_HEADS * MLA_V) ** -0.5),
        'w_branch_c': nrm((DEPTH, NA_HEADS * NA_HEAD_DIM, D), (NA_HEADS * NA_HEAD_DIM) ** -0.5),
        'w_branch_d': nrm((DEPTH, DIFF_HEADS * DIFF_V_DIM, D), (DIFF_HEADS * DIFF_V_DIM) ** -0.5),
        'w_gate': nrm((DEPTH, D, N_BRANCHES * D), D ** -0.5),
        'b_gate': nrm((DEPTH, N_BRANCHES * D), 0.01),
        'w_out': nrm((DEPTH, D, D), DEEPNORM_BETA * D ** -0.5),
        'ln1_g': gain((DEPTH, D)),
        'ln1_b': nrm((DEPTH, D), 0.01),
        'peer_w_q': nrm((DEPTH, D, PEER_HEADS * PEER_KEY_DIM), D ** -0.5),
        'peer_subkeys': nrm((DEPTH, PEER_HEADS, 2, PEER_N_KEYS, PEER_KEY_DIM // 2), (PEER_KEY_DIM // 2) ** -0.5),
        'peer_u': nrm((DEPTH, PEER_N_EXPERTS, D), D ** -0.5),
        'peer_v': nrm((DEPTH, PEER_N_EXPERTS, D), DEEPNORM_BETA),
        'ln2_g': gain((DEPTH, D)),
        'ln2_b': nrm((DEPTH, D), 0.01),
    }

def reference(x_prompt, x_sample, cache_mla_ckv, cache_mla_krope, cache_na_k, cache_na_v,
              cache_diff_k, cache_diff_v, c, c_ctx,
              w_mod, b_mod, w_in, sgu_norm_g, sgu_w, sgu_b,
              mla_q_norm_g, mla_w_uq, mla_kv_norm_g, mla_w_ukv, na_rpb,
              diff_lambda_q1, diff_lambda_k1, diff_lambda_q2, diff_lambda_k2, diff_norm_g,
              w_branch_a, w_branch_b, w_branch_c, w_branch_d, w_gate, b_gate, w_out,
              ln1_g, ln1_b, peer_w_q, peer_subkeys, peer_u, peer_v, ln2_g, ln2_b):
    params = dict(w_mod=w_mod, b_mod=b_mod, w_in=w_in, sgu_norm_g=sgu_norm_g, sgu_w=sgu_w, sgu_b=sgu_b,
                  mla_q_norm_g=mla_q_norm_g, mla_w_uq=mla_w_uq, mla_kv_norm_g=mla_kv_norm_g,
                  mla_w_ukv=mla_w_ukv, na_rpb=na_rpb,
                  diff_lambda_q1=diff_lambda_q1, diff_lambda_k1=diff_lambda_k1,
                  diff_lambda_q2=diff_lambda_q2, diff_lambda_k2=diff_lambda_k2, diff_norm_g=diff_norm_g,
                  w_branch_a=w_branch_a, w_branch_b=w_branch_b, w_branch_c=w_branch_c, w_branch_d=w_branch_d,
                  w_gate=w_gate, b_gate=b_gate, w_out=w_out, ln1_g=ln1_g, ln1_b=ln1_b,
                  peer_w_q=peer_w_q, peer_subkeys=peer_subkeys, peer_u=peer_u, peer_v=peer_v,
                  ln2_g=ln2_g, ln2_b=ln2_b)
    y_prompt = x_prompt
    ctx_layers = []
    for l in range(DEPTH):
        p = {name: arr[l] for name, arr in params.items()}
        lambda_init = 0.8 - 0.6 * math.exp(-0.3 * l)
        y_prompt, ctx_tensors = trunk_layer(y_prompt, c_ctx[None], p, lambda_init, None)
        ctx_layers.append(ctx_tensors)
    new_mla_ckv = jnp.stack([t[0] for t in ctx_layers], axis=1)
    new_mla_krope = jnp.stack([t[1] for t in ctx_layers], axis=1)
    new_na_k = jnp.stack([t[2] for t in ctx_layers], axis=1)
    new_na_v = jnp.stack([t[3] for t in ctx_layers], axis=1)
    new_diff_k = jnp.stack([t[4] for t in ctx_layers], axis=1)
    new_diff_v = jnp.stack([t[5] for t in ctx_layers], axis=1)
    y_sample = x_sample
    for l in range(DEPTH):
        p = {name: arr[l] for name, arr in params.items()}
        lambda_init = 0.8 - 0.6 * math.exp(-0.3 * l)
        cache = (cache_mla_ckv[:, l], cache_mla_krope[:, l], cache_na_k[:, l], cache_na_v[:, l],
                 cache_diff_k[:, l], cache_diff_v[:, l])
        y_sample, _ = trunk_layer(y_sample, c, p, lambda_init, cache)
    return (y_prompt, y_sample, new_mla_ckv, new_mla_krope, new_na_k, new_na_v, new_diff_k, new_diff_v)


_drawn_inputs = setup_inputs


def setup_inputs(seed=0):
    import zlib

    import numpy as np

    out = dict(_drawn_inputs(seed))
    spreads = {}
    factors = {'cache_mla_ckv': 3.226,
     'cache_mla_krope': 4.198,
     'sgu_norm_g': 20.008,
     'sgu_b': 21.061,
     'mla_q_norm_g': 8.0,
     'mla_kv_norm_g': 5.513,
     'na_rpb': 16.111,
     'diff_lambda_q1': 3.791,
     'diff_lambda_k1': 3.593,
     'diff_lambda_k2': 3.794,
     'diff_norm_g': 22.633,
     'b_gate': 8.0,
     'ln2_g': 2.845,
     'ln2_b': 2.724,
     'cache_na_k': 3.805,
     'cache_na_v': 4.174}
    for name, (base, spread) in spreads.items():
        noise = np.random.default_rng([zlib.crc32(name.encode()), seed]).standard_normal(out[name].shape)
        drawn = base * np.exp(spread * noise) if base else spread * noise
        out[name] = jnp.asarray(drawn.astype(out[name].dtype))
    for name, factor in factors.items():
        out[name] = (out[name] * factor).astype(out[name].dtype)
    return out
```

```python
from contextlib import ExitStack
import math

import numpy as np
import concourse.bass as bass
from concourse import mybir

F32 = mybir.dt.float32
I32 = mybir.dt.int32
U32 = mybir.dt.uint32
ALU = mybir.AluOpType
ACT = mybir.ActivationFunctionType
AX = mybir.AxisListType

P = 128
D = 1024
KD = D // P
DEPTH = 2
NT = 3
NTOK = NT * P
GRID_W = 64
EPS = 1e-6
ALPHA = (2 * DEPTH) ** 0.25
HEADS = 4
NOPE, ROPE, MV = 64, 32, 64
MQK = NOPE + ROPE
NA_D = 64
DQK, DV = 64, 128
PH, TOPK, NKEYS = 8, 16, 128
NEXP = NKEYS * NKEYS
KSEL = PH * TOPK
GROUP = 4
STEPS = KSEL // (2 * GROUP)
NEG_BIG = -1e30
LOWEST = -3.0e38

IN_W = 3232
AU, AV, CQ, CKV, KR, NQ, NK, NV, DQ, DK, DVO = 0, 256, 512, 768, 896, 928, 1184, 1440, 1696, 2208, 2720
C_CKV, C_KR, C_NK, C_NV, C_DK, C_DV, C_W = 0, 128, 160, 416, 672, 1184, 1696
OUT_A, OUT_B, OUT_C, OUT_D, OUT_W = 0, 256, 512, 768, 1280
R_SG, R_KVG, R_DG, R_LAM, R_L1G, R_L1B, R_L2G, R_L2B, R_W = 0, 256, 384, 512, 768, 1792, 2816, 3840, 4864
C_BM, C_BG, C_SB, C_QG, C_LI, C_EO, C_LO, COLS = 0, 48, 80, 84, 86, 88, 89, 90
K_ID, K_ON, K_MA, K_IO, K_C16, K_S16, K_C32, K_S32, K_W = 0, 128, 256, 512, 528, 560, 592, 656, 720

W_SLOT = 4 * 512
W_RING = 4

TT_SRC = [[CQ, CQ + 128, CKV], [NQ, NQ + 128, NK, NK + 128],
          [DQ + 128 * i for i in range(4)], [DK + 128 * i for i in range(4)]]
TT_CACHE = {0: [(2, C_CKV)], 1: [(2, C_NK), (3, C_NK + 128)], 3: [(i, C_DK + 128 * i) for i in range(4)]}

HEAD_LIST = [(t, kind, h) for t in range(NT) for kind in "BCD" for h in range(HEADS)]
ROWS = [(w, m) for w, (t, kind, h) in enumerate(HEAD_LIST) for m in range(2 if kind == "D" else 1)]
ROW_OF = {wm: r for r, wm in enumerate(ROWS)}
P_BUFS = 6
HEAD_LAG = 2


def key_blocks(t):
    return [0] if t == 0 else [1, 2, 3]


def spread(ap, axis, n):
    shape = list(ap.shape)
    shape[axis] = n
    return ap.broadcast_to(shape)


def head_order():
    for w in range(len(HEAD_LIST) + HEAD_LAG + 1):
        if w < len(HEAD_LIST):
            for m in range(2 if HEAD_LIST[w][1] == "D" else 1):
                yield ("s", w, m)
        if 0 <= w - HEAD_LAG < len(HEAD_LIST):
            yield ("pt", w - HEAD_LAG)
        if 0 <= w - HEAD_LAG - 1:
            yield ("o", w - HEAD_LAG - 1)


def plan_items():
    out = [(("mod", j), "v") for j in range(12)]
    out += [(("gb", i, q), "a") for i in range(2) for q in range(2)]
    out += [(("hT", t, q), "av"[q]) for t in range(NT) for q in range(2)]
    out += [(("proj", j, t), "a" if j == 0 or (j + t) % 2 else "v") for j in range(7) for t in range(NT)]
    out += [(("sgu", t), "v") for t in range(NT)]
    out += [(("tt", t, g), "v" if g == 0 else "a") for t in range(4) for g in range(4) if t < NT or g in TT_CACHE]
    out += [(("mq", t), "v") for t in range(NT)]
    out += [(("kv", b), "a") for b in range(4)]
    out += [(("mqt", t), "v") for t in range(NT)]
    out += [(("mkt", b), "a") for b in range(4)]
    for it in head_order():
        t, kind, h = HEAD_LIST[it[1]]
        if it[0] == "s":
            out.append((it, "v" if kind == "C" and t else "p"))
        else:
            out.append((it, "v" if it[0] == "o" else "a"))
    out += [(("ot", t, g), "av"[g % 2]) for t in range(NT) for g in range(3)]
    for b in range(4):
        for half in range(2):
            out += [(("gate", b, 4 * half + n), "a") for n in range(4)]
            out += [(("br", b, 4 * half + n), "v") for n in range(4)]
    out += [(("mix", j, t), "v") for j in range(2) for t in range(NT)]
    out += [(("gb", i, q), "a") for i in (2, 3) for q in range(2)]
    out += [(("h2T", t, q), "av"[q]) for t in range(NT) for q in range(2)]
    out += [(("h2", t, q), "av"[q]) for t in range(NT) for q in range(2)]
    out += [(("pq", c), "av"[c % 2]) for c in range(16)]
    out += [(("ps", t, q), "av"[q % 2]) for t in range(NT) for q in range(4)]
    return out


ITEMS = plan_items()
INDEX = {name: n for n, (name, _) in enumerate(ITEMS)}
EVAC_BY = [who for _, who in ITEMS]
EVAC_COUNT = [sum(w == who for w in EVAC_BY[:n + 1]) for n, who in enumerate(EVAC_BY)]

SLOTS = ([("mod", j, k) for j in range(12) for k in range(2)] + [("in", j, k) for j in range(7) for k in range(2)]
         + [("small",)])
SLOTS += [s for b in range(4) for j in range(2) for s in (("gate", b, j, 0), ("gate", b, j, 1), ("branch", b, j))]
SLOTS += [("out", j, k) for j in range(2) for k in range(2)]
SLOTS += [("pq", j, k) for j in range(4) for k in range(2)] + [("sub",)]
SLOT_OF = {s: n for n, s in enumerate(SLOTS)}
BRANCH_K = [2, 2, 2, 4]


def last_item(s):
    return {"mod": lambda: ("mod", s[1]), "in": lambda: ("proj", s[1], NT - 1), "small": lambda: ("kv", 3),
            "gate": lambda: ("gate", s[1], 4 * s[2] + 3), "branch": lambda: ("br", s[1], 4 * s[2] + 3),
            "out": lambda: ("mix", s[1], NT - 1), "pq": lambda: ("pq", 4 * s[1] + 3), "sub": lambda: ("ps", NT - 1, 3)}[s[0]]()


S_UQ, S_UKV, S_SW, S_W = 0, 768, 1280, 1792


def build(nc, a, outs):
    with ExitStack() as ctx:
        def sb(name, words, dt=F32):
            return ctx.enter_context(nc.sbuf_tensor(name, [P, words], dt))

        def sem(name):
            s = ctx.enter_context(nc.semaphore(name))
            return s

        x = sb("x", NT * D)[:, :].rearrange("p (t d) -> p t d", t=NT)
        hT = sb("hT", KD * NTOK)[:, :].rearrange("p (k n) -> p k n", k=KD)
        rows = sb("rows", R_L2G)
        gains = sb("gains", 2 * D)[:, :].rearrange("p (i d) -> p i d", i=2)
        bias = sb("bias", 2 * HEADS * 256)[:, :].rearrange("p (t h n) -> p t h n", t=2, h=HEADS)
        cols = sb("cols", COLS)
        consts = sb("consts", K_W)
        diag = sb("diag", 512)
        modT = sb("modT", 96)[:, :].rearrange("p (n c) -> p n c", c=2)
        silu = sb("silu", 16)[:, :].rearrange("p (k c) -> p k c", c=2)
        wring = sb("wring", W_RING * W_SLOT)
        stat = sb("stat", 256)
        psum = ctx.enter_context(nc.psum_tensor("psum", [P, 8, 512], F32))
        ident = consts[:, K_ID:K_ID + P]
        ones = consts[:, K_ON:K_ON + P]

        WORK = 27700
        work = sb("work", WORK)

        def region(at, words):
            assert at + words <= WORK
            return work[:, at:at + words]

        proj = region(0, NT * IN_W).rearrange("p (t n) -> p t n", t=NT)
        TTO = NT * IN_W
        TT = region(TTO, 16 * 512).rearrange("p (b n) -> p b n", b=16)
        xn = region(TTO, NT * D).rearrange("p (t d) -> p t d", t=NT)
        outT = region(TTO, 10 * NTOK).rearrange("p (k n) -> p k n", k=10)
        mergedT = region(TTO + 10 * NTOK, KD * NTOK).rearrange("p (k n) -> p k n", k=KD)
        o = TTO + 16 * 512
        VB = region(o, 4 * 256).rearrange("p (b n) -> p b n", b=4)
        o += 4 * 256
        MQT = region(o, HEADS * NTOK).rearrange("p (h n) -> p h n", h=HEADS)
        sg = region(o, 4 * NTOK).rearrange("p (n q) -> p n q", n=4)
        o += HEADS * NTOK
        MKT = region(o, HEADS * 512).rearrange("p (h n) -> p h n", h=HEADS)
        tmp = region(o, 2 * 512).rearrange("p (n q) -> p n q", n=2)
        o += HEADS * 512
        cache = region(o, C_W)
        o += C_W
        MQ = region(o, NT * 384).rearrange("p (t n) -> p t n", t=NT)
        KB = region(o + NT * 384, 4 * 384).rearrange("p (b h n) -> p b h n", b=4, h=HEADS)
        PB = region(o, P_BUFS * 384).rearrange("p (r n) -> p r n", r=P_BUFS)
        o += P_BUFS * 384
        o += (NT + 4 - P_BUFS) * 384
        PT = region(o, 2 * 384).rearrange("p (r b n) -> p r b n", r=2, b=3)
        nbs = sb("nbs", 2 * 384)[:, :].rearrange("p (r n) -> p r n", r=2)

        ringU = region(0, 8 * D).rearrange("p (r d) -> p r d", r=8)
        ringV = region(8 * D, 8 * D).rearrange("p (r d) -> p r d", r=8)
        S = region(0, NT * 2048).rearrange("p (t c n) -> p t c n", t=NT, c=16)
        qT = region(8 * D, 16 * NTOK).rearrange("p (c n) -> p c n", c=16)
        o = 16 * D
        h2 = region(o, NT * D).rearrange("p (t d) -> p t d", t=NT)
        o += NT * D
        y = region(o, 2 * D).rearrange("p (r d) -> p r d", r=2)
        o += 2 * D
        cand = region(14 * D, 2048)
        eq = region(o - 2 * D, 2048)
        xn2 = region(0, NT * D).rearrange("p (t d) -> p t d", t=NT)
        v16 = region(o, 256).rearrange("p (c k) -> p c k", c=16)
        i16f = region(o + 256, 256).rearrange("p (c k) -> p c k", c=16)
        best = region(o + 512, 128).rearrange("p (h k) -> p h k", h=PH)
        selA = region(o + 640, 128)
        selB = region(o + 768, 128)
        i16 = sb("i16", 256, U32)[:, :].rearrange("p (c k) -> p c k", c=16)
        bi = sb("bi", 256, U32)[:, :].rearrange("p (r n) -> p r n", r=2)
        gates = sb("gates", NT * KSEL)
        experts = sb("experts", NT * KSEL + 8, I32)
        exslot = sb("exslot", 8, I32)
        dots = sb("dots", 8)
        acts = sb("acts", 8)
        wts = sb("wts", 8)

        names = ["loaded", "psum_full", "dve_evac", "act_evac", "dve_step", "ln1_done",
                 "diag_ready", "xn_ready", "norms_ready", "kb_ready",
                 "negmax_ready", "probs_ready", "nbs_ready", "weights_ready", "outs_ready", "merged_ready",
                 "h2_ready", "best_ready", "gate_exp", "experts_ready", "dots_ready", "gelu_ready", "stored",
                 "new_ready", "x_ready", "sqin", "sqout", "mod_ready", "lam_in", "lam_out", "acc_done"]
        sems = {n: sem(n) for n in names}
        w_ready = [sem(f"w_ready{i}") for i in range(W_RING)]
        gotU = [sem(f"gotU{i}") for i in range(8)]
        gotV = [sem(f"gotV{i}") for i in range(8)]
        setup_loaded = sem("setup_loaded")
        setup_done = sem("setup_done")
        gather_gate = sem("gather_gate")
        loaded, psum_full, dve_evac, act_evac = (sems[n] for n in names[:4])

        def bank(name):
            return psum[:, INDEX[name] % 8, :]

        def full(eng, name):
            eng.wait_ge(psum_full, INDEX[name] + 1)

        def evacuated(eng, name):
            n = INDEX[name]
            if EVAC_BY[n] == "p":
                eng.wait_ge(sems["probs_ready"], ROW_OF[name[1:]] + 1)
            else:
                eng.wait_ge(dve_evac if EVAC_BY[n] == "v" else act_evac, EVAC_COUNT[n])

        def all_evacuated(eng, names_):
            for who in "va":
                last = [n for n in names_ if EVAC_BY[INDEX[n]] == who]
                if last:
                    evacuated(eng, max(last, key=lambda n: INDEX[n]))

        with nc.Block() as block:
            @block.sync
            def _(sp):
                for t in range(NT):
                    src = a["x_prompt"][0] if t == 0 else a["x_sample"][0, (t - 1) * P:t * P, :]
                    sp.dma_start(x[:, t, :], src).then_inc(setup_loaded, 16)
                sp.dma_start(consts[:, :], a["consts"]).then_inc(setup_loaded, 16)
                sp.dma_start(silu, a["cond"]).then_inc(setup_loaded, 16)
                sp.wait_ge(setup_loaded, 80)

            @block.scalar
            def _(act):
                act.wait_ge(setup_loaded, 80)
                nc.scalar.activation(silu, silu, ACT.Silu).then_inc(setup_done, 1)

            @block.tensor
            def _(pe):
                pe.wait_ge(setup_done, 2)

            @block.vector
            def _(dve):
                nc.vector.memset(experts[:, NT * KSEL:], 0).then_inc(setup_done, 1)
                dve.wait_ge(setup_done, 2)

            @block.gpsimd
            def _(pool):
                pool.wait_ge(setup_done, 2)
        nc.all_engine_barrier()

        with nc.Fori(0, DEPTH) as l:
            with nc.Block() as block:
                @block.sync
                def _(sp):
                    lay = bass.ds(l, 1)
                    sp.dma_start(cols[:, :], a["cols"][lay].rearrange("a p n -> p (a n)")).then_inc(loaded, 16)
                    sp.dma_start(rows[:, :], a["rows"][lay, 0:R_L2G].broadcast_to([P, R_L2G])).then_inc(loaded, 16)
                    sp.dma_start(cache, a["cache"][lay].rearrange("a p n -> p (a n)")).then_inc(loaded, 16)
                    sp.dma_start(bias.rearrange("p t h n -> p (t h n)"),
                                 a["rpb"][lay].rearrange("a p n -> p (a n)")).then_inc(loaded, 16)

                    def cols_of(name, j, width, k0, nk):
                        w = a[name][lay].rearrange("a (k p) n -> p (a k) n", p=P)
                        return w[:, k0:k0 + nk, j:j + width]

                    for n, s in enumerate(SLOTS):
                        if n >= W_RING:
                            full(sp, last_item(SLOTS[n - W_RING]))
                        base = (n % W_RING) * W_SLOT
                        ready = w_ready[n % W_RING]
                        kind = s[0]
                        if kind == "small":
                            sp.dma_start(wring[:, base:base + S_W],
                                         a["small"][lay].rearrange("a p n -> p (a n)")).then_inc(ready, 16)
                        elif kind == "sub":
                            sp.dma_start(wring[:, base:base + W_SLOT],
                                         a["subT"][lay].rearrange("a p n -> p (a n)")).then_inc(ready, 16)
                        elif kind == "branch":
                            dst = wring[:, base:base + W_SLOT].rearrange("p (k n) -> p k n", k=4)[:, 0:BRANCH_K[s[1]], :]
                            sp.dma_start(dst, cols_of("w_branch_" + "abcd"[s[1]], 512 * s[2], 512, 0, BRANCH_K[s[1]])).then_inc(ready, 16)
                        else:
                            name = {"mod": "w_mod", "in": "w_in", "gate": "w_gate", "out": "w_out", "pq": "peer_w_q"}[kind]
                            col = (s[1] * 2 + s[2]) * 512 if kind == "gate" else s[1] * 512
                            width = min(512, IN_W - col) if kind == "in" else 512
                            dst = wring[:, base:base + W_SLOT].rearrange("p (k n) -> p k n", k=4)[:, :, 0:width]
                            sp.dma_start(dst, cols_of(name, col, width, 4 * s[-1], 4)).then_inc(ready, 16)
                    sp.wait_ge(sems["ln1_done"], 1)
                    sp.dma_start(rows[:, R_L1G:R_L2G], a["rows"][lay, R_L2G:R_W].broadcast_to([P, 2 * D])).then_inc(loaded, 16)
                    for t in range(NT):
                        sp.wait_ge(sems["x_ready"], t + 1)
                        dst = outs[0][0] if t == 0 else outs[1][0, (t - 1) * P:t * P, :]
                        sp.dma_start(dst, x[:, t, :]).then_inc(sems["stored"], 16)
                    sp.wait_ge(sems["stored"], 16 * (NT + 6))

                @block.tensor
                def _(pe):
                    def slot(s, k):
                        n = SLOT_OF[s]
                        pe.wait_ge(w_ready[n % W_RING], 16 * (n // W_RING + 1))
                        base = (n % W_RING) * W_SLOT
                        return wring[:, base:base + W_SLOT].rearrange("p (k n) -> p k n", k=k)

                    def room(name):
                        if INDEX[name] >= 8:
                            evacuated(pe, ITEMS[INDEX[name] - 8][0])
                        return bank(name)

                    pe.wait_ge(loaded, 64)
                    for j in range(12):
                        out = room(("mod", j))
                        w = [slot(("mod", j, k), 4) for k in range(2)]
                        for n in range(4):
                            for k in range(KD):
                                last = nc.tensor.matmul(out[:, 2 * n:2 * n + 2], w[k // 4][:, k % 4, n * P:(n + 1) * P],
                                                        silu[:, k, :], start=(k == 0), stop=(k == KD - 1))
                        last.then_inc(psum_full, 1)
                    def spread_gains(pair):
                        for i in pair:
                            for q in range(2):
                                out = room(("gb", i, q))
                                pe.wait_ge(sems["diag_ready"], 2 * i + q + 1)
                                nc.tensor.matmul(out, ones, diag[:, :], start=True, stop=True).then_inc(psum_full, 1)

                    spread_gains((0, 1))

                    def transposed(kind, src, ready, count):
                        for t in range(NT):
                            pe.wait_ge(ready, count + t)
                            for q in range(2):
                                out = room((kind, t, q))
                                for k in range(4):
                                    last = nc.tensor.transpose(out[:, k * P:(k + 1) * P],
                                                               src[:, t, (4 * q + k) * P:(4 * q + k + 1) * P], ident)
                                last.then_inc(psum_full, 1)

                    transposed("hT", xn, sems["xn_ready"], 1)

                    all_evacuated(pe, [("hT", t, q) for t in range(NT) for q in range(2)])
                    for j in range(7):
                        width = min(512, IN_W - 512 * j)
                        outb = [room(("proj", j, t)) for t in range(NT)]
                        for half in range(2):
                            w = slot(("in", j, half), 4)
                            for t in range(NT):
                                for k in range(4):
                                    kk = 4 * half + k
                                    last = nc.tensor.matmul(outb[t][:, 0:width], hT[:, kk, t * P:(t + 1) * P],
                                                            w[:, k, 0:width], start=(kk == 0), stop=(kk == KD - 1))
                                if half == 1:
                                    last.then_inc(psum_full, 1)

                    small = slot(("small",), 1)[:, 0, :]
                    pe.wait_ge(sems["norms_ready"], 1)
                    for t in range(NT):
                        out = room(("sgu", t))
                        for g in range(4):
                            last = nc.tensor.matmul(out[:, g * 64:(g + 1) * 64], small[:, S_SW + g * P:S_SW + (g + 1) * P],
                                                    proj[:, t, AV + 64 * g:AV + 64 * (g + 1)], start=True, stop=True)
                        last.then_inc(psum_full, 1)
                    for t in range(4):
                        for g in range(4):
                            if t == NT and g not in TT_CACHE:
                                continue
                            out = room(("tt", t, g))
                            blocks = TT_CACHE[g] if t == NT else list(enumerate(TT_SRC[g]))
                            for i, c in blocks:
                                src = cache[:, c:c + P] if t == NT else proj[:, t, c:c + P]
                                last = nc.tensor.transpose(out[:, i * P:(i + 1) * P], src, ident)
                            last.then_inc(psum_full, 1)
                    all_evacuated(pe, [("tt", 3, 0), ("tt", 2, 0)])
                    for t in range(NT):
                        out = room(("mq", t))
                        for k in range(2):
                            last = nc.tensor.matmul(out[:, 0:384], TT[:, k, t * P:(t + 1) * P],
                                                    small[:, S_UQ + 384 * k:S_UQ + 384 * (k + 1)],
                                                    start=(k == 0), stop=(k == 1))
                        last.then_inc(psum_full, 1)
                    for b in range(4):
                        nc.tensor.matmul(room(("kv", b)), TT[:, 2, b * P:(b + 1) * P], small[:, S_UKV:S_UKV + 512],
                                         start=True, stop=True).then_inc(psum_full, 1)
                    for t in range(NT):
                        out = room(("mqt", t))
                        evacuated(pe, ("mq", t))
                        for h in range(HEADS):
                            last = nc.tensor.transpose(out[0:MQK, h * P:(h + 1) * P], MQ[:, t, h * MQK:(h + 1) * MQK], ident)
                        last.then_inc(psum_full, 1)
                    for b in range(4):
                        out = room(("mkt", b))
                        evacuated(pe, ("kv", b))
                        pe.wait_ge(sems["kb_ready"], 1)
                        for h in range(HEADS):
                            last = nc.tensor.transpose(out[0:MQK, h * P:(h + 1) * P], KB[:, b, h, :], ident)
                        last.then_inc(psum_full, 1)

                    all_evacuated(pe, [("mqt", 2), ("mkt", 3)])
                    all_evacuated(pe, [("tt", t, g) for t in range(4) for g in range(4) if t < NT or g in TT_CACHE])
                    for it in head_order():
                        w = it[1]
                        t, kind, h = HEAD_LIST[w]
                        out = room(it)
                        blocks = key_blocks(t)
                        nk = P * len(blocks)
                        k0 = P * blocks[0]
                        if it[0] == "s":
                            if kind == "B":
                                q, k = MQT[0:MQK, h, t * P:(t + 1) * P], MKT[0:MQK, h, k0:k0 + nk]
                            elif kind == "C":
                                lo = 64 * (h % 2)
                                q, k = TT[lo:lo + 64, 4 + h // 2, t * P:(t + 1) * P], TT[lo:lo + 64, 6 + h // 2, k0:k0 + nk]
                            else:
                                lo = 64 * it[2]
                                q, k = TT[lo:lo + 64, 8 + h, t * P:(t + 1) * P], TT[lo:lo + 64, 12 + h, k0:k0 + nk]
                            nc.tensor.matmul(out[:, 0:nk], q, k, start=True, stop=True).then_inc(psum_full, 1)
                        elif it[0] == "pt":
                            r = ROW_OF[(w, 0)]
                            if kind == "D":
                                pe.wait_ge(sems["weights_ready"], sum(1 for q_ in HEAD_LIST[:w + 1] if q_[1] == "D"))
                            else:
                                pe.wait_ge(sems["probs_ready"], r + 1)
                            for i in range(len(blocks)):
                                last = nc.tensor.transpose(out[:, i * P:(i + 1) * P], PB[:, r % P_BUFS, i * P:(i + 1) * P], ident)
                            last.then_inc(psum_full, 1)
                        else:
                            evacuated(pe, ("pt", w))
                            for i, b in enumerate(blocks):
                                if kind == "B":
                                    v = VB[:, b, 64 * h:64 * (h + 1)]
                                elif kind == "C":
                                    v = proj[:, b, NV + 64 * h:NV + 64 * (h + 1)] if b < NT else cache[:, C_NV + 64 * h:C_NV + 64 * (h + 1)]
                                else:
                                    v = proj[:, b, DVO + P * h:DVO + P * (h + 1)] if b < NT else cache[:, C_DV + P * h:C_DV + P * (h + 1)]
                                last = nc.tensor.matmul(out[:, 0:P if kind == "D" else 64], PT[:, w % 2, i, :], v,
                                                        start=(i == 0), stop=(i == len(blocks) - 1))
                            last.then_inc(psum_full, 1)

                    pe.wait_ge(sems["outs_ready"], 1)
                    for t in range(NT):
                        for g in range(3):
                            out = room(("ot", t, g))
                            for i in range(4 if g < 2 else 2):
                                c = (4 * g + i) * P
                                last = nc.tensor.transpose(out[:, i * P:(i + 1) * P], proj[:, t, c:c + P], ident)
                            last.then_inc(psum_full, 1)
                    all_evacuated(pe, [("ot", t, g) for t in range(NT) for g in range(3)])
                    for b in range(4):
                        kb0, nkb = 2 * b, BRANCH_K[b]
                        for half in range(2):
                            outb = [room(("gate", b, 4 * half + n)) for n in range(4)]
                            for kh in range(2):
                                w = slot(("gate", b, half, kh), 4)
                                for n in range(4):
                                    for k in range(4):
                                        kk = 4 * kh + k
                                        last = nc.tensor.matmul(outb[n][:, 0:NTOK], w[:, k, n * P:(n + 1) * P], hT[:, kk, :],
                                                                start=(kk == 0), stop=(kk == KD - 1))
                                    if kh == 1:
                                        last.then_inc(psum_full, 1)
                            wb = slot(("branch", b, half), 4)
                            for n in range(4):
                                nn = 4 * half + n
                                out = room(("br", b, nn))
                                for k in range(nkb):
                                    last = nc.tensor.matmul(out[:, 0:NTOK], wb[:, k, n * P:(n + 1) * P],
                                                            outT[:, kb0 + k, :], start=(k == 0), stop=(k == nkb - 1))
                                last.then_inc(psum_full, 1)
                    pe.wait_ge(sems["merged_ready"], 1)
                    for j in range(2):
                        outb = [room(("mix", j, t)) for t in range(NT)]
                        for half in range(2):
                            w = slot(("out", j, half), 4)
                            for t in range(NT):
                                for k in range(4):
                                    kk = 4 * half + k
                                    last = nc.tensor.matmul(outb[t], mergedT[:, kk, t * P:(t + 1) * P], w[:, k, :],
                                                            start=(kk == 0), stop=(kk == KD - 1))
                                if half == 1:
                                    last.then_inc(psum_full, 1)
                    spread_gains((2, 3))
                    transposed("h2T", xn2, sems["xn_ready"], NT + 1)
                    for t in range(NT):
                        all_evacuated(pe, [("h2T", t, 0), ("h2T", t, 1)])
                        for q in range(2):
                            out = room(("h2", t, q))
                            for k in range(4):
                                last = nc.tensor.transpose(out[:, k * P:(k + 1) * P], hT[:, 4 * q + k, t * P:(t + 1) * P], ident)
                            last.then_inc(psum_full, 1)
                    for j in range(4):
                        outb = [room(("pq", 4 * j + n)) for n in range(4)]
                        for kh in range(2):
                            w = slot(("pq", j, kh), 4)
                            for n in range(4):
                                for k in range(4):
                                    kk = 4 * kh + k
                                    last = nc.tensor.matmul(outb[n][:, 0:NTOK], w[:, k, n * P:(n + 1) * P], hT[:, kk, :],
                                                            start=(kk == 0), stop=(kk == KD - 1))
                                if kh == 1:
                                    last.then_inc(psum_full, 1)
                    sub = slot(("sub",), 16)
                    all_evacuated(pe, [("pq", c) for c in range(16)])
                    for t in range(NT):
                        for q in range(4):
                            out = room(("ps", t, q))
                            for i in range(4):
                                c = 4 * q + i
                                last = nc.tensor.matmul(out[:, i * P:(i + 1) * P], qT[:, c, t * P:(t + 1) * P], sub[:, c, :],
                                                        start=True, stop=True)
                            last.then_inc(psum_full, 1)

                @block.scalar
                def _(act):
                    cond = [0, 1, 1]

                    def taken(ins):
                        return ins.then_inc(act_evac, 1)

                    act.wait_ge(loaded, 64)
                    def take_gains(pair):
                        for i in pair:
                            for q in range(2):
                                full(act, ("gb", i, q))
                                taken(nc.scalar.copy(gains[:, i % 2, q * 512:(q + 1) * 512], bank(("gb", i, q))))

                    take_gains((0, 1))

                    def shift_scale(kind, t, q, sh, sc):
                        full(act, (kind, t, q))
                        for k in range(4):
                            n = 4 * q + k
                            last = nc.scalar.activation(hT[:, n, t * P:(t + 1) * P], bank((kind, t, q))[:, k * P:(k + 1) * P],
                                                        ACT.Identity, bias=modT[:, sh + n, cond[t]:cond[t] + 1],
                                                        scale=modT[:, sc + n, cond[t]:cond[t] + 1])
                        taken(last)

                    sq = [0]

                    def square_roots(width, scale):
                        sq[0] += 1
                        act.wait_ge(sems["sqin"], sq[0])
                        nc.scalar.activation(stat[:, 16:16 + width], stat[:, 0:width], ACT.Sqrt,
                                             bias=cols[:, C_EO:C_EO + 1], scale=scale).then_inc(sems["sqout"], 1)

                    square_roots(NT, 1.0)
                    act.wait_ge(sems["mod_ready"], 1)
                    for t in range(NT):
                        shift_scale("hT", t, 0, 0, 8)
                    for j in range(7):
                        width = min(512, IN_W - 512 * j)
                        for t in range(NT):
                            name = ("proj", j, t)
                            if EVAC_BY[INDEX[name]] != "a":
                                continue
                            full(act, name)
                            taken(nc.scalar.activation(proj[:, t, 512 * j:512 * j + width], bank(name)[:, 0:width],
                                                       ACT.Gelu if j == 0 else ACT.Copy))
                    square_roots(3 * NT, 1.0)
                    act.wait_ge(sems["lam_in"], 1)
                    nc.scalar.activation(stat[:, 48:50], stat[:, 46:48], ACT.Exp).then_inc(sems["lam_out"], 1)
                    act.wait_ge(sems["new_ready"], 1)
                    lay = bass.ds(l, 1)
                    for i, (c, width) in enumerate([(CKV, 128), (KR, 32), (NK, 256), (NV, 256), (DK, 512), (DVO, 512)]):
                        act.dma_start(outs[2 + i][lay].rearrange("a p n -> p (a n)"), proj[:, 0, c:c + width])\
                           .then_inc(sems["stored"], 16)
                    for t in range(4):
                        for g in range(1, 4):
                            if t == NT and g not in TT_CACHE:
                                continue
                            name = ("tt", t, g)
                            full(act, name)
                            lo = 2 if (t == NT and g == 1) else 0
                            taken(nc.scalar.copy(TT[:, 4 * g + lo:4 * g + 4, t * P:(t + 1) * P],
                                                 bank(name)[:, lo * P:512].rearrange("p (b n) -> p b n", n=P)))
                    for b in range(4):
                        full(act, ("kv", b))
                        src = bank(("kv", b)).rearrange("p (h n) -> p h n", h=HEADS)
                        nc.scalar.copy(KB[:, b, :, 0:NOPE], src[:, :, 0:NOPE])
                        taken(nc.scalar.copy(VB[:, b, :].rearrange("p (h n) -> p h n", h=HEADS), src[:, :, NOPE:NOPE + MV]))
                    for b in range(4):
                        full(act, ("mkt", b))
                        taken(nc.scalar.copy(MKT[0:MQK, :, b * P:(b + 1) * P],
                                             bank(("mkt", b))[0:MQK, :].rearrange("p (h n) -> p h n", h=HEADS)))
                    for it in head_order():
                        w = it[1]
                        t, kind, h = HEAD_LIST[w]
                        nk = P * len(key_blocks(t))
                        if it[0] == "s":
                            r = ROW_OF[(w, it[2])]
                            if r >= P_BUFS:
                                full(act, ("pt", ROWS[r - P_BUFS][0]))
                            act.wait_ge(sems["negmax_ready"], r + 1)
                            if kind == "C" and t:
                                c = sum(1 for q_ in HEAD_LIST[:w] if q_[1] == "C" and q_[0])
                                src, scale = nbs[:, c % 2, 0:nk], 1.0
                            else:
                                src, scale = bank(it)[:, 0:nk], (MQK if kind == "B" else 64) ** -0.5
                            ins = nc.scalar.activation(PB[:, r % P_BUFS, 0:nk], src, ACT.Exp, bias=stat[:, 64 + r:65 + r],
                                                       scale=scale, accum_out=stat[:, 112 + r:113 + r])
                            ins.then_inc(sems["probs_ready"], 1)
                        elif it[0] == "pt":
                            full(act, it)
                            if w >= 2:
                                full(act, ("o", w - 2))
                            taken(nc.scalar.copy(PT[:, w % 2, 0:nk // P, :],
                                                 bank(it)[:, 0:nk].rearrange("p (b n) -> p b n", n=P)))
                    square_roots(NT * HEADS, 1.0 / DV)
                    for t in range(NT):
                        for g in (0, 2):
                            full(act, ("ot", t, g))
                            nb = 4 if g < 2 else 2
                            taken(nc.scalar.copy(outT[:, 4 * g:4 * g + nb, t * P:(t + 1) * P],
                                                 bank(("ot", t, g))[:, 0:nb * P].rearrange("p (b n) -> p b n", n=P)))
                    for b in range(4):
                        for n in range(KD):
                            full(act, ("gate", b, n))
                            i = 8 * b + n
                            if i >= 4:
                                evacuated(act, ("br", (i - 4) // 8, (i - 4) % 8))
                            else:
                                full(act, ("s", len(HEAD_LIST) - 1, 1))
                            taken(nc.scalar.activation(sg[:, n % 4, :], bank(("gate", b, n))[:, 0:NTOK], ACT.Sigmoid,
                                                       bias=cols[:, C_BG + 8 * b + n:C_BG + 8 * b + n + 1]))
                    take_gains((2, 3))
                    square_roots(NT, 1.0)
                    square_roots(NT, 1.0)
                    for t in range(NT):
                        shift_scale("h2T", t, 0, 24, 32)
                    for t in range(NT):
                        full(act, ("h2", t, 0))
                        taken(nc.scalar.copy(h2[:, t, 0:512], bank(("h2", t, 0))))
                    for c in range(0, 16, 2):
                        full(act, ("pq", c))
                        taken(nc.scalar.copy(qT[:, c, :], bank(("pq", c))[:, 0:NTOK]))
                    for t in range(NT):
                        for q in (0, 2):
                            full(act, ("ps", t, q))
                            taken(nc.scalar.copy(S[:, t, 4 * q:4 * q + 4, :],
                                                 bank(("ps", t, q)).rearrange("p (c n) -> p c n", n=P)))
                    for t in range(NT):
                        act.wait_ge(sems["best_ready"], t + 1)
                        gt = gates[:, t * KSEL:(t + 1) * KSEL]
                        nc.scalar.activation(gt, gt, ACT.Exp).then_inc(sems["gate_exp"], 1)
                    for t in range(NT):
                        with act.Fori(0, STEPS) as i:
                            for g in range(2):
                                act.wait_ge(sems["dots_ready"], GROUP * (i * 2 + (2 * STEPS * t + g + 1)))
                                nc.scalar.activation(acts[:, GROUP * g:GROUP * (g + 1)], dots[:, GROUP * g:GROUP * (g + 1)],
                                                     ACT.Gelu).then_inc(sems["gelu_ready"], 1)
                        square_roots(1, 1.0)

                @block.vector
                def _(dve):
                    cond = [0, 1, 1]
                    steps = [0]
                    dve_step = sems["dve_step"]

                    def step(ins):
                        steps[0] += 1
                        ins.then_inc(dve_step, 1)

                    def sync():
                        dve.wait_ge(dve_step, steps[0])

                    def link(ins):
                        step(ins)
                        sync()

                    def taken(ins):
                        return ins.then_inc(dve_evac, 1)

                    sq = [0]

                    def roots(width):
                        sync()
                        sq[0] += 1
                        dve.sem_inc(sems["sqin"], 1)
                        dve.wait_ge(sems["sqout"], sq[0])
                        link(nc.vector.reciprocal(stat[:, 32:32 + width], stat[:, 16:16 + width]))

                    bn = stat[:, 160:256]

                    def mean_var(slot_, src, width):
                        nb = (width + 511) // 512
                        part = bn[:, 12 * (slot_ % 3):12 * (slot_ % 3) + 6 * nb]
                        for i in range(nb):
                            step(nc.vector.bn_stats(part[:, 6 * i:6 * i + 6], src[:, i * (width // nb):(i + 1) * (width // nb)]))
                        sync()
                        link(nc.vector.bn_aggr(bn[:, 36 + 2 * slot_:38 + 2 * slot_], part))
                        step(nc.vector.tensor_copy(stat[:, slot_:slot_ + 1], bn[:, 37 + 2 * slot_:38 + 2 * slot_]))

                    def normalised(dst, ready):
                        for t in range(NT):
                            nc.vector.tensor_scalar(dst[:, t, :], x[:, t, :], bn[:, 36 + 2 * t:37 + 2 * t], stat[:, 32 + t:33 + t],
                                                    ALU.subtract, ALU.mult).then_inc(ready, 1)

                    dve.wait_ge(loaded, 64)
                    for j in range(12):
                        full(dve, ("mod", j))
                        taken(nc.vector.tensor_tensor(modT[:, 4 * j:4 * j + 4, :],
                                                      bank(("mod", j))[:, 0:8].rearrange("p (n c) -> p n c", c=2),
                                                      spread(cols[:, C_BM + 4 * j:C_BM + 4 * j + 4].unsqueeze(2), 2, 2), ALU.add))
                    evacuated(dve, ("mod", 11))
                    step(nc.vector.tensor_scalar(modT[:, 8:16, :], modT[:, 8:16, :], 1.0, None, ALU.add))
                    nc.vector.tensor_scalar(modT[:, 32:40, :], modT[:, 32:40, :], 1.0, None, ALU.add).then_inc(sems["mod_ready"], 1)
                    def diagonals(pair):
                        for i in pair:
                            for q in range(2):
                                if i or q:
                                    full(dve, ("gb", (2 * i + q - 1) // 2, (2 * i + q - 1) % 2))
                                base = 16 if i < 2 else 40
                                for k in range(4):
                                    last = nc.vector.tensor_scalar(diag[:, k * P:(k + 1) * P], ident,
                                                                   modT[:, base + 4 * q + k, i % 2:i % 2 + 1], None, ALU.mult)
                                last.then_inc(sems["diag_ready"], 1)

                    diagonals((0, 1))
                    for t in range(2):
                        for h in range(HEADS):
                            step(nc.vector.tensor_tensor(bias[:, t, h, :], bias[:, t, h, :], consts[:, K_MA:K_MA + 256], ALU.add))
                    for t in range(NT):
                        mean_var(t, x[:, t, :], D)
                    roots(NT)
                    normalised(xn, sems["xn_ready"])

                    def shift_scale(kind, t, sh, sc):
                        full(dve, (kind, t, 1))
                        dve.wait_ge(sems["mod_ready"], 1)
                        for k in range(4):
                            n = 4 + k
                            last = nc.vector.tensor_scalar(hT[:, n, t * P:(t + 1) * P], bank((kind, t, 1))[:, k * P:(k + 1) * P],
                                                           modT[:, sc + n, cond[t]:cond[t] + 1],
                                                           modT[:, sh + n, cond[t]:cond[t] + 1], ALU.mult, ALU.add)
                        taken(last)

                    for t in range(NT):
                        shift_scale("hT", t, 0, 8)
                    for j in range(7):
                        width = min(512, IN_W - 512 * j)
                        for t in range(NT):
                            name = ("proj", j, t)
                            if EVAC_BY[INDEX[name]] == "v":
                                full(dve, name)
                                taken(nc.vector.tensor_copy(proj[:, t, 512 * j:512 * j + width], bank(name)[:, 0:width]))
                    all_evacuated(dve, [("proj", j, t) for j in range(7) for t in range(NT)])
                    for t in range(NT):
                        mean_var(t, proj[:, t, AV:AV + 256], 256)
                        for i, (c, width) in enumerate([(CQ, 256), (CKV, 128)]):
                            n = 3 + 3 * i + t
                            mean_var(n, proj[:, t, c:c + width], width)
                            sync()
                            link(nc.vector.scalar_tensor_tensor(out=stat[:, n:n + 1], in0=bn[:, 36 + 2 * n:37 + 2 * n],
                                                                scalar=bn[:, 36 + 2 * n:37 + 2 * n],
                                                                in1=bn[:, 37 + 2 * n:38 + 2 * n], op0=ALU.mult, op1=ALU.add))
                    roots(3 * NT)
                    for t in range(NT):
                        av = proj[:, t, AV:AV + 256]
                        step(nc.vector.tensor_scalar(av, av, bn[:, 36 + 2 * t:37 + 2 * t], stat[:, 32 + t:33 + t], ALU.subtract, ALU.mult))
                        cq = proj[:, t, CQ:CQ + 256]
                        step(nc.vector.tensor_scalar(cq, cq, stat[:, 35 + t:36 + t], None, ALU.mult))
                        ck = proj[:, t, CKV:CKV + P]
                        step(nc.vector.scalar_tensor_tensor(out=ck, in0=ck, scalar=stat[:, 38 + t:39 + t],
                                                            in1=rows[:, R_KVG:R_KVG + P], op0=ALU.mult, op1=ALU.mult))
                    sync()
                    for t in range(NT):
                        av = proj[:, t, AV:AV + 256]
                        step(nc.vector.tensor_tensor(av, av, rows[:, R_SG:R_SG + 256], ALU.mult))
                    sync()
                    dve.sem_inc(sems["new_ready"], 1)

                    def rotate(dst, src, t, groups, half, kc, ks):
                        cs = spread(consts[:, kc + (t - 1) * half:kc + t * half].unsqueeze(1), 1, groups)
                        sn = spread(consts[:, ks + (t - 1) * half:ks + t * half].unsqueeze(1), 1, groups)
                        x1, x2 = src[:, :, 0:half], src[:, :, half:2 * half]
                        bufs = [hold[:, i * groups * half:(i + 1) * groups * half].rearrange("p (g n) -> p g n", g=groups)
                                for i in range(4)]
                        for b_, (u, v) in zip(bufs, [(x1, cs), (x2, sn), (x2, cs), (x1, sn)]):
                            step(nc.vector.tensor_tensor(b_, u, v, ALU.mult))
                        sync()
                        step(nc.vector.tensor_tensor(dst[:, :, 0:half], bufs[0], bufs[1], ALU.subtract))
                        return nc.vector.tensor_tensor(dst[:, :, half:2 * half], bufs[2], bufs[3], ALU.add)

                    hold = TT[:, 8:12, :].rearrange("p b n -> p (b n)")
                    for t in (1, 2):
                        step(rotate(proj[:, t, DQ:DQ + 1024].rearrange("p (g n) -> p g n", g=16),
                                    proj[:, t, DQ:DQ + 1024].rearrange("p (g n) -> p g n", g=16), t, 16, 32, K_C32, K_S32))
                        sync()
                        step(rotate(proj[:, t, KR:KR + 32].rearrange("p (g n) -> p g n", g=1),
                                    proj[:, t, KR:KR + 32].rearrange("p (g n) -> p g n", g=1), t, 1, 16, K_C16, K_S16))
                        sync()
                    dve.sem_inc(sems["norms_ready"], 1)
                    for i in range(2):
                        q1 = rows[:, R_LAM + 128 * i:R_LAM + 128 * i + 64]
                        k1 = rows[:, R_LAM + 128 * i + 64:R_LAM + 128 * i + 128]
                        step(nc.vector.tensor_tensor(q1, q1, k1, ALU.mult))
                    sync()
                    step(nc.vector.tensor_reduce(stat[:, 46:48], rows[:, R_LAM:R_LAM + 256].rearrange("p (i n) -> p i n", i=2)[:, :, 0:64],
                                                 AX.X, ALU.add))
                    sync()
                    dve.sem_inc(sems["lam_in"], 1)
                    dve.wait_ge(sems["lam_out"], 1)
                    link(nc.vector.tensor_tensor(stat[:, 50:51], stat[:, 49:50], stat[:, 48:49], ALU.subtract))
                    link(nc.vector.tensor_tensor(stat[:, 51:52], stat[:, 50:51], cols[:, C_LI:C_LI + 1], ALU.subtract))
                    step(nc.vector.tensor_scalar(rows[:, R_DG:R_DG + P], rows[:, R_DG:R_DG + P], cols[:, C_LI + 1:C_LI + 2], None, ALU.mult))
                    neglam = stat[:, 51:52]
                    for t in range(NT):
                        full(dve, ("sgu", t))
                        for g in range(4):
                            u = proj[:, t, AU + 64 * g:AU + 64 * (g + 1)]
                            last = nc.vector.scalar_tensor_tensor(out=u, in0=bank(("sgu", t))[:, 64 * g:64 * (g + 1)],
                                                                  scalar=cols[:, C_SB + g:C_SB + g + 1], in1=u,
                                                                  op0=ALU.add, op1=ALU.mult)
                        taken(last)
                    for t in range(4):
                        name = ("tt", t, 0)
                        full(dve, name)
                        if t < NT:
                            for k in range(2):
                                nc.vector.tensor_scalar(TT[:, k, t * P:(t + 1) * P], bank(name)[:, k * P:(k + 1) * P],
                                                        cols[:, C_QG + k:C_QG + k + 1], None, ALU.mult)
                        taken(nc.vector.tensor_copy(TT[:, 2, t * P:(t + 1) * P], bank(name)[:, 2 * P:3 * P]))
                    for b in range(4):
                        src = spread((cache[:, C_KR:C_KR + 32] if b == NT else proj[:, b, KR:KR + 32]).unsqueeze(1), 1, HEADS)
                        step(nc.vector.tensor_copy(KB[:, b, :, NOPE:MQK], src))
                    sync()
                    dve.sem_inc(sems["kb_ready"], 1)
                    hold = nbs.rearrange("p r n -> p (r n)")
                    for t in range(NT):
                        full(dve, ("mq", t))
                        src = bank(("mq", t))[:, 0:384].rearrange("p (h n) -> p h n", h=HEADS)
                        dst = MQ[:, t, :].rearrange("p (h n) -> p h n", h=HEADS)
                        if t == 0:
                            taken(nc.vector.tensor_copy(dst, src))
                        else:
                            sync()
                            step(nc.vector.tensor_copy(dst[:, :, 0:NOPE], src[:, :, 0:NOPE]))
                            taken(rotate(dst[:, :, NOPE:MQK], src[:, :, NOPE:MQK], t, HEADS, 16, K_C16, K_S16))
                            evacuated(dve, ("mq", t))
                    for t in range(NT):
                        full(dve, ("mqt", t))
                        taken(nc.vector.tensor_copy(MQT[0:MQK, :, t * P:(t + 1) * P],
                                                    bank(("mqt", t))[0:MQK, :].rearrange("p (h n) -> p h n", h=HEADS)))

                    negmax = sems["negmax_ready"]
                    for it in head_order():
                        w = it[1]
                        t, kind, h = HEAD_LIST[w]
                        nk = P * len(key_blocks(t))
                        if it[0] == "s":
                            r = ROW_OF[(w, it[2])]
                            full(dve, it)
                            nm = stat[:, 64 + r:65 + r]
                            if kind == "C" and t:
                                c = sum(1 for q_ in HEAD_LIST[:w] if q_[1] == "C" and q_[0])
                                if c >= 2:
                                    dve.wait_ge(sems["probs_ready"], ROW_OF[(HEAD_LIST.index((1 + (c - 2) // 4, "C", (c - 2) % 4)), 0)] + 1)
                                step(nc.vector.scalar_tensor_tensor(out=nbs[:, c % 2, 0:256], in0=bank(it)[:, 0:256], scalar=NA_D ** -0.5,
                                                                    in1=bias[:, t - 1, h, :], op0=ALU.mult, op1=ALU.add))
                                taken(nc.vector.tensor_scalar(nbs[:, c % 2, 256:384], bank(it)[:, 256:384], NA_D ** -0.5, None, ALU.mult))
                                evacuated(dve, it)
                                nc.vector.tensor_reduce(nm, nbs[:, c % 2, :], AX.X, ALU.max, negate=True).then_inc(negmax, 1)
                            else:
                                link(nc.vector.tensor_reduce(nm, bank(it)[:, 0:nk], AX.X, ALU.max, negate=True))
                                nc.vector.tensor_scalar(nm, nm, (MQK if kind == "B" else 64) ** -0.5, None, ALU.mult).then_inc(negmax, 1)
                        elif it[0] == "pt":
                            r = ROW_OF[(w, 0)]
                            nr = 2 if kind == "D" else 1
                            dve.wait_ge(sems["probs_ready"], r + nr)
                            rr = stat[:, 112 + r:112 + r + nr]
                            link(nc.vector.reciprocal(rr, rr))
                            if kind == "D":
                                link(nc.vector.tensor_tensor(stat[:, 113 + r:114 + r], stat[:, 113 + r:114 + r], neglam, ALU.mult))
                                p1, p2 = PB[:, r % P_BUFS, 0:nk], PB[:, (r + 1) % P_BUFS, 0:nk]
                                link(nc.vector.tensor_scalar(p2, p2, stat[:, 113 + r:114 + r], None, ALU.mult))
                                nc.vector.scalar_tensor_tensor(out=p1, in0=p1, scalar=stat[:, 112 + r:113 + r], in1=p2,
                                                               op0=ALU.mult, op1=ALU.add).then_inc(sems["weights_ready"], 1)
                        else:
                            r = ROW_OF[(w, 0)]
                            full(dve, it)
                            if w == 0:
                                dve.wait_ge(sems["stored"], 16 * 6)
                            if kind == "D":
                                taken(nc.vector.tensor_copy(proj[:, t, OUT_D + P * h:OUT_D + P * (h + 1)], bank(it)[:, 0:P]))
                            else:
                                c = (OUT_B if kind == "B" else OUT_C) + 64 * h
                                taken(nc.vector.tensor_scalar(proj[:, t, c:c + 64], bank(it)[:, 0:64], stat[:, 112 + r:113 + r], None, ALU.mult))
                    evacuated(dve, ("o", len(HEAD_LIST) - 1))
                    full(dve, ("o", len(HEAD_LIST) - 1))
                    for t in range(NT):
                        for h in range(HEADS):
                            n = HEADS * t + h
                            od = proj[:, t, OUT_D + P * h:OUT_D + P * (h + 1)]
                            step(nc.vector.tensor_tensor_reduce(TT[:, n % 16, 0:P], od, od, 1.0, 0.0, ALU.mult, ALU.add, stat[:, n:n + 1]))
                    roots(NT * HEADS)
                    for t in range(NT):
                        for h in range(HEADS):
                            n = HEADS * t + h
                            od = proj[:, t, OUT_D + P * h:OUT_D + P * (h + 1)]
                            step(nc.vector.scalar_tensor_tensor(out=od, in0=od, scalar=stat[:, 32 + n:33 + n], in1=rows[:, R_DG:R_DG + P],
                                                                op0=ALU.mult, op1=ALU.mult))
                    sync()
                    dve.sem_inc(sems["outs_ready"], 1)
                    for t in range(NT):
                        full(dve, ("ot", t, 1))
                        taken(nc.vector.tensor_copy(outT[:, 4:8, t * P:(t + 1) * P],
                                                    bank(("ot", t, 1)).rearrange("p (b n) -> p b n", n=P)))
                    for b in range(4):
                        for n in range(KD):
                            full(dve, ("br", b, n))
                            evacuated(dve, ("gate", b, n))
                            br = bank(("br", b, n))[:, 0:NTOK]
                            if b == 0:
                                taken(nc.vector.tensor_tensor(mergedT[:, n, :], br, sg[:, n % 4, :], ALU.mult))
                            else:
                                dve.wait_ge(dve_evac, EVAC_COUNT[INDEX[("br", b - 1, n)]])
                                sync()
                                tb = tmp[:, n % 2, 0:NTOK]
                                taken(nc.vector.tensor_tensor(tb, br, sg[:, n % 4, :], ALU.mult))
                                evacuated(dve, ("br", b, n))
                                step(nc.vector.tensor_tensor(mergedT[:, n, :], mergedT[:, n, :], tb, ALU.add))
                    sync()
                    dve.sem_inc(sems["merged_ready"], 1)

                    def residual(t, j, src, gain):
                        xs = x[:, t, 512 * j:512 * (j + 1)]
                        tb = tmp[:, 0, :] if gain < 2 else y[:, 1, 512 * j:512 * (j + 1)]
                        first = nc.vector.tensor_tensor(tb, src, gains[:, gain % 2, 512 * j:512 * (j + 1)], ALU.mult)
                        return first, (lambda: nc.vector.scalar_tensor_tensor(out=xs, in0=xs, scalar=ALPHA, in1=tb,
                                                                              op0=ALU.mult, op1=ALU.add))

                    for j in range(2):
                        for t in range(NT):
                            full(dve, ("mix", j, t))
                            first, second = residual(t, j, bank(("mix", j, t)), cond[t])
                            taken(first)
                            evacuated(dve, ("mix", j, t))
                            link(second())

                    diagonals((2, 3))

                    def affine(ts, g, b_, ready):
                        for t in ts:
                            step(nc.vector.tensor_tensor(x[:, t, :], x[:, t, :], rows[:, g:g + D], ALU.mult))
                        sync()
                        for t in ts:
                            ins = nc.vector.tensor_tensor(x[:, t, :], x[:, t, :], rows[:, b_:b_ + D], ALU.add)
                            if ready is None:
                                step(ins)
                            else:
                                ins.then_inc(ready, 1)

                    def layer_norm(ts):
                        for i, t in enumerate(ts):
                            mean_var(i, x[:, t, :], D)
                        roots(len(ts))
                        for i, t in enumerate(ts):
                            step(nc.vector.tensor_scalar(x[:, t, :], x[:, t, :], bn[:, 36 + 2 * i:37 + 2 * i], stat[:, 32 + i:33 + i],
                                                         ALU.subtract, ALU.mult))
                        sync()

                    layer_norm(range(NT))
                    affine(range(NT), R_L1G, R_L1B, None)
                    sync()
                    dve.sem_inc(sems["ln1_done"], 1)
                    for t in range(NT):
                        mean_var(t, x[:, t, :], D)
                    roots(NT)
                    normalised(xn2, sems["xn_ready"])
                    for t in range(NT):
                        shift_scale("h2T", t, 24, 32)
                    for t in range(NT):
                        full(dve, ("h2", t, 1))
                        taken(nc.vector.tensor_copy(h2[:, t, 512:1024], bank(("h2", t, 1))))
                    for c in range(1, 16, 2):
                        full(dve, ("pq", c))
                        taken(nc.vector.tensor_copy(qT[:, c, :], bank(("pq", c))[:, 0:NTOK]))
                    for t in range(NT):
                        for q in (1, 3):
                            full(dve, ("ps", t, q))
                            taken(nc.vector.tensor_copy(S[:, t, 4 * q:4 * q + 4, :],
                                                        bank(("ps", t, q)).rearrange("p (c n) -> p c n", n=P)))

                    def top16(n, src, vals, idxs):
                        for c in range(n):
                            step(nc.vector.max(vals(c)[:, 0:8], src(c)))
                        sync()
                        for c in range(n):
                            step(nc.vector.max_index(idxs(c)[:, 0:8], vals(c)[:, 0:8], src(c)))
                        sync()
                        for c in range(n):
                            step(nc.vector.match_replace(src(c), vals(c)[:, 0:8], src(c), LOWEST))
                        sync()
                        for c in range(n):
                            step(nc.vector.max(vals(c)[:, 8:16], src(c)))
                        sync()
                        for c in range(n):
                            step(nc.vector.max_index(idxs(c)[:, 8:16], vals(c)[:, 8:16], src(c)))
                        sync()

                    for t in range(NT):
                        all_evacuated(dve, [("ps", t, q) for q in range(4)])
                        top16(16, lambda c: S[:, t, c, :], lambda c: v16[:, c, :], lambda c: i16[:, c, :])
                        step(nc.vector.tensor_copy(i16f, i16))
                        vv = v16.rearrange("p (h m) k -> p h m k", m=2)
                        for h in range(PH):
                            step(nc.vector.tensor_tensor(cand[:, 256 * h:256 * (h + 1)].rearrange("p (a b) -> p a b", a=16),
                                                         spread(vv[:, h, 0, :].unsqueeze(2), 2, 16),
                                                         spread(vv[:, h, 1, :].unsqueeze(1), 1, 16), ALU.add))
                        sync()
                        bv = bi[:, 0, :].rearrange("p (h k) -> p h k", h=PH)
                        top16(PH, lambda h: cand[:, 256 * h:256 * (h + 1)], lambda h: best[:, h, :], lambda h: bv[:, h, :])
                        gt = gates[:, t * KSEL:(t + 1) * KSEL].rearrange("p (h k) -> p h k", h=PH)
                        nc.vector.tensor_tensor(gt, best, spread(best[:, :, 0:1], 2, TOPK), ALU.subtract)\
                            .then_inc(sems["best_ready"], 1)
                        step(nc.vector.tensor_scalar(bi[:, 1, :], bi[:, 0, :], 4, None, ALU.logical_shift_right))
                        sync()
                        step(nc.vector.tensor_copy(selA, bi[:, 1, :]))
                        sync()
                        step(nc.vector.tensor_scalar(bi[:, 1, :], bi[:, 0, :], 15, None, ALU.bitwise_and))
                        sync()
                        step(nc.vector.tensor_copy(selB, bi[:, 1, :]))
                        sync()
                        iota = spread(consts[:, K_IO:K_IO + 16].unsqueeze(1), 1, KSEL)
                        ii = i16f.rearrange("p (h m) k -> p h m k", m=2)
                        for m, sel in ((0, selA), (1, selB)):
                            e3 = eq.rearrange("p (n k) -> p n k", n=KSEL)
                            step(nc.vector.tensor_tensor(e3, spread(sel.unsqueeze(2), 2, 16), iota, ALU.is_equal))
                            sync()
                            for h in range(PH):
                                eh = eq[:, 256 * h:256 * (h + 1)].rearrange("p (n k) -> p n k", n=TOPK)
                                step(nc.vector.tensor_tensor(eh, eh, spread(ii[:, h, m, :].unsqueeze(1), 1, TOPK), ALU.mult))
                            sync()
                            step(nc.vector.tensor_reduce(sel, e3, AX.X, ALU.add))
                            sync()
                        step(nc.vector.scalar_tensor_tensor(out=selA, in0=selA, scalar=float(NKEYS), in1=selB, op0=ALU.mult, op1=ALU.add))
                        sync()
                        step(nc.vector.tensor_scalar(selA, selA, cols[:, C_LO:C_LO + 1], None, ALU.add))
                        sync()
                        step(nc.vector.tensor_copy(experts[:, t * KSEL:(t + 1) * KSEL], selA))
                        dve.wait_ge(sems["gate_exp"], t + 1)
                        step(nc.vector.tensor_reduce(stat[:, 0:PH], gt, AX.X, ALU.add))
                        sync()
                        step(nc.vector.reciprocal(stat[:, 32:32 + PH], stat[:, 0:PH]))
                        sync()
                        step(nc.vector.tensor_tensor(gt, gt, spread(stat[:, 32:32 + PH].unsqueeze(2), 2, TOPK), ALU.mult))
                        sync()

                    for g in range(2):
                        nc.vector.tensor_copy(exslot[:, GROUP * g:GROUP * (g + 1)], experts[:, GROUP * g:GROUP * (g + 1)])\
                            .then_inc(sems["experts_ready"], 1)
                    per_layer = 16 * NT * STEPS
                    acc_done = sems["acc_done"]
                    for t in range(NT):
                        step(nc.vector.memset(y.rearrange("p r d -> p (r d)"), 0.0))
                        sync()
                        with dve.Fori(0, STEPS) as i:
                            for g in range(2):
                                for j in range(GROUP * g, GROUP * (g + 1)):
                                    dve.wait_ge(gotU[j], l * per_layer + i * 16 + 16 * (STEPS * t + 1))
                                    nc.vector.tensor_tensor_reduce(ringU[:, j, :], ringU[:, j, :], h2[:, t, :], 1.0, 0.0,
                                                                   ALU.mult, ALU.add, dots[:, j:j + 1]).then_inc(sems["dots_ready"], 1)
                            for g in range(2):
                                dve.wait_ge(sems["gelu_ready"], i * 2 + (2 * STEPS * t + g + 1))
                                nc.vector.tensor_tensor(wts[:, GROUP * g:GROUP * (g + 1)], acts[:, GROUP * g:GROUP * (g + 1)],
                                                        gates[:, bass.ds(i * 2 * GROUP + (t * KSEL + GROUP * g), GROUP)],
                                                        ALU.mult).then_inc(acc_done, 1)
                                for j in range(GROUP * g, GROUP * (g + 1)):
                                    dve.wait_ge(acc_done, i * 10 + (10 * STEPS * t + 5 * g + 1 + j - GROUP * g))
                                    dve.wait_ge(gotV[j], l * per_layer + i * 16 + 16 * (STEPS * t + 1))
                                    nc.vector.scalar_tensor_tensor(out=y[:, 0, :], in0=ringV[:, j, :], scalar=wts[:, j:j + 1],
                                                                   in1=y[:, 0, :], op0=ALU.mult, op1=ALU.add).then_inc(acc_done, 1)
                                dve.wait_ge(acc_done, i * 10 + (10 * STEPS * t + 5 * g + 5))
                                nc.vector.tensor_copy(exslot[:, GROUP * g:GROUP * (g + 1)],
                                                      experts[:, bass.ds(i * 2 * GROUP + (t * KSEL + 2 * GROUP + GROUP * g), GROUP)])\
                                    .then_inc(sems["experts_ready"], 1)
                        dve.wait_ge(acc_done, 10 * STEPS * (t + 1))
                        for j in range(2):
                            first, second = residual(t, j, y[:, 0, 512 * j:512 * (j + 1)], 2 + cond[t])
                            link(first)
                            link(second())
                        layer_norm([t])
                        dve.wait_ge(loaded, 80)
                        affine([t], R_L1G, R_L1B, sems["x_ready"])
                    dve.wait_ge(sems["x_ready"], NT)

                @block.gpsimd
                def _(pool):
                    for t in range(NT):
                        with pool.Fori(0, STEPS) as i:
                            for g in range(2):
                                pool.wait_ge(sems["experts_ready"], i * 2 + (2 * STEPS * t + g + 1))
                                pool.sem_inc(gather_gate, 1)
                                for ring, table, got in ((ringU, "peer_u", gotU), (ringV, "peer_v", gotV)):
                                    for j in range(GROUP * g, GROUP * (g + 1)):
                                        pool.indirect_dma_start(ring[:, j, :], None, a[table],
                                                                bass.IndirectOffsetOnAxis(ap=exslot[:, j:j + 1], axis=0))\
                                            .then_inc(got[j], 16)
            nc.all_engine_barrier()
            for s in list(sems.values()) + w_ready:
                nc.gpsimd.sem_clear(s)
            nc.all_engine_barrier()


_OUTS = [(1, 128, 1024), (1, 256, 1024), (2, 128, 128), (2, 128, 32), (2, 128, 256), (2, 128, 256), (2, 128, 512), (2, 128, 512)]
_SHAPES = [(1, 128, 1024), (1, 256, 1024), (1, 2, 128, 128), (1, 2, 128, 32), (1, 2, 128, 4, 64), (1, 2, 128, 4, 64),
           (1, 2, 128, 4, 128), (1, 2, 128, 4, 128)]


def shape_constants():
    c = np.zeros((P, K_W), np.float32)
    c[:, K_ID:K_ID + P] = np.eye(P)
    c[:, K_ON:K_ON + P] = 1
    col = np.arange(GRID_W)
    start = np.clip(col - 8, 0, GRID_W - 16)
    inside = (col[None] >= start[:, None]) & (col[None] < start[:, None] + 16)
    c[:, K_MA:K_MA + 256] = np.tile(np.where(inside, 0.0, NEG_BIG), (2, 4))
    c[:, K_IO:K_IO + 16] = np.arange(16)
    tok = np.arange(256)
    for half, kc, ks in ((16, K_C16, K_S16), (32, K_C32, K_S32)):
        nf = half // 2
        inv = (np.float32(10000.0) ** (-np.arange(nf, dtype=np.float32) / nf)).astype(np.float32)
        row, cc = (tok // GRID_W).astype(np.float32), (tok % GRID_W).astype(np.float32)
        ang = np.concatenate([row[:, None] * inv, cc[:, None] * inv], 1).astype(np.float32)
        for t in range(2):
            c[:, kc + t * half:kc + (t + 1) * half] = np.cos(ang[t * P:(t + 1) * P])
            c[:, ks + t * half:ks + (t + 1) * half] = np.sin(ang[t * P:(t + 1) * P])
    return c


def layouts(v):
    cat = np.concatenate
    lam = cat([v[n] for n in ("diff_lambda_q1", "diff_lambda_k1", "diff_lambda_q2", "diff_lambda_k2")], 1)
    rows = cat([v["sgu_norm_g"], v["mla_kv_norm_g"], v["diff_norm_g"], lam, v["ln1_g"], v["ln1_b"], v["ln2_g"], v["ln2_b"]], 1)
    colT = lambda w, n: w.reshape(DEPTH, n, P).transpose(0, 2, 1)
    init = [0.8 - 0.6 * math.exp(-0.3 * l) for l in range(DEPTH)]
    fixed = np.zeros((DEPTH, P, 4), np.float32)
    for l in range(DEPTH):
        fixed[l] = [init[l], 1 - init[l], EPS, l * NEXP]
    cols = cat([colT(v["b_mod"], 48), colT(v["b_gate"], 32), v["sgu_b"].transpose(0, 2, 1), colT(v["mla_q_norm_g"], 2), fixed], 2)
    flat = lambda w: w[0].reshape(DEPTH, P, -1)
    cache = cat([flat(v[n]) for n in ("cache_mla_ckv", "cache_mla_krope", "cache_na_k", "cache_na_v", "cache_diff_k", "cache_diff_v")], 2)
    q = np.arange(2 * P)
    r, c = q // GRID_W, q % GRID_W
    dr = r[None, :] - r[:, None] + 7
    dc = np.clip(c[None, :] - c[:, None], -15, 15) + 15
    rpb = v["na_rpb"][:, :, dr, dc].reshape(DEPTH, HEADS, 2, P, 256).transpose(0, 3, 2, 1, 4).reshape(DEPTH, P, -1)
    uq = v["mla_w_uq"].reshape(DEPTH, 2, P, 384).transpose(0, 2, 1, 3).reshape(DEPTH, P, 768)
    sgw = v["sgu_w"].transpose(0, 3, 1, 2).reshape(DEPTH, P, 512)
    small = cat([uq, v["mla_w_ukv"], sgw], 2)
    subT = v["peer_subkeys"].reshape(DEPTH, 16, P, P).transpose(0, 3, 1, 2).reshape(DEPTH, P, 2048)
    cond = np.stack([v["c_ctx"].reshape(KD, P).T, v["c"][0].reshape(KD, P).T], 2)
    out = dict(rows=rows, cols=cols, cache=cache, rpb=rpb, small=small, subT=subT, cond=cond, consts=shape_constants())
    for n in ("x_prompt", "x_sample", "w_mod", "w_in", "w_gate", "w_out", "peer_w_q", "w_branch_a", "w_branch_b", "w_branch_c", "w_branch_d"):
        out[n] = v[n]
    for n in ("peer_u", "peer_v"):
        out[n] = v[n].reshape(DEPTH * NEXP, D)
    return {n: np.ascontiguousarray(w) for n, w in out.items()}


def kernel(**inputs):
    import concourse.bacc as _bacc
    from concourse.bass_utils import run_bass_kernel_spmd as _run

    nc = _bacc.Bacc("TRN2", target_bir_lowering=False, num_devices=1)
    arrays = {f"in_{n}": w for n, w in layouts({k: np.asarray(w) for k, w in inputs.items()}).items()}
    a = {n[3:]: nc.dram_tensor(n, w.shape, F32, kind="ExternalInput").ap() for n, w in arrays.items()}
    outs = [nc.dram_tensor(f"out_{i}", s, F32, kind="ExternalOutput").ap() for i, s in enumerate(_OUTS)]
    build(nc, a, outs)
    r = _run(nc, [arrays], core_ids=[0])
    return tuple(r.results[0][f"out_{i}"].reshape(s) for i, s in enumerate(_SHAPES))
```

```python
from contextlib import ExitStack
import math

import numpy as np
import concourse.bass as bass
from concourse import mybir

F32 = mybir.dt.float32
I32 = mybir.dt.int32
U32 = mybir.dt.uint32
ALU = mybir.AluOpType
ACT = mybir.ActivationFunctionType
AX = mybir.AxisListType

P = 128
D = 1024
KD = D // P
DEPTH = 2
NT = 3
NTOK = NT * P
GRID_W = 64
EPS = 1e-6
ALPHA = (2 * DEPTH) ** 0.25
HEADS = 4
NOPE, ROPE, MV = 64, 32, 64
MQK = NOPE + ROPE
NA_D = 64
DQK, DV = 64, 128
PH, TOPK, NKEYS = 8, 16, 128
NEXP = NKEYS * NKEYS
KSEL = PH * TOPK
GROUP = 4
STEPS = KSEL // (2 * GROUP)
NEG_BIG = -1e30
LOWEST = -3.0e38

IN_W = 3232
AU, AV, CQ, CKV, KR, NQ, NK, NV, DQ, DK, DVO = 0, 256, 512, 768, 896, 928, 1184, 1440, 1696, 2208, 2720
C_CKV, C_KR, C_NK, C_NV, C_DK, C_DV, C_W = 0, 128, 160, 416, 672, 1184, 1696
OUT_A, OUT_B, OUT_C, OUT_D, OUT_W = 0, 256, 512, 768, 1280
R_SG, R_KVG, R_DG, R_LAM, R_L1G, R_L1B, R_L2G, R_L2B, R_W = 0, 256, 384, 512, 768, 1792, 2816, 3840, 4864
C_BM, C_BG, C_SB, C_QG, C_LI, C_EO, C_LO, COLS = 0, 48, 80, 84, 86, 88, 89, 90
K_ID, K_ON, K_MA, K_IO, K_C16, K_S16, K_C32, K_S32, K_W = 0, 128, 256, 512, 528, 560, 592, 656, 720

W_SLOT = 4 * 512
W_RING = 4

TT_FIRST = [0, 3, 7, 11]
B_NQ, B_NK, B_DQ, B_DK, TT_BLOCKS = 3, 5, 7, 11, 15
TT_SRC = [[CQ, CQ + 128, CKV], [NQ, NQ + 128, NK, NK + 128],
          [DQ + 128 * i for i in range(4)], [DK + 128 * i for i in range(4)]]
TT_CACHE = {0: [(2, C_CKV)], 1: [(2, C_NK), (3, C_NK + 128)], 3: [(i, C_DK + 128 * i) for i in range(4)]}

HEAD_LIST = [(t, kind, h) for kind in "BCD" for t in range(NT) for h in range(HEADS)]
BRANCH_K = [2, 2, 2, 4]
ROWS = [(w, m) for w, (t, kind, h) in enumerate(HEAD_LIST) for m in range(2 if kind == "D" else 1)]
ROW_OF = {wm: r for r, wm in enumerate(ROWS)}
P_BUFS = 6
HEAD_LAG = 2


def key_blocks(t):
    return [0] if t == 0 else [1, 2, 3]


def spread(ap, axis, n):
    shape = list(ap.shape)
    shape[axis] = n
    return ap.broadcast_to(shape)


def head_step(w):
    scores = [("s", w, m) for m in range(2 if HEAD_LIST[w][1] == "D" else 1)] if w < len(HEAD_LIST) else []
    pt = [("pt", w - HEAD_LAG)] if 0 <= w - HEAD_LAG < len(HEAD_LIST) else []
    o = [("o", w - HEAD_LAG - 1)] if w > HEAD_LAG else []
    return scores, pt + o


def branch_items(b):
    out = [("ot", b, k) for k in range(BRANCH_K[b])]
    for half in range(2):
        out += [("gate", b, 4 * half + n) for n in range(4)] + [("br", b, 4 * half + n) for n in range(4)]
    return out


def middle_order():
    per = len(HEAD_LIST) // 3
    mods = [[4, 5], [6, 7, 8], [9, 10, 11]]
    last = 0
    for w in range(len(HEAD_LIST) + HEAD_LAG + 1):
        p = min(w // per, 2)
        i = w - p * per
        scores, rest = head_step(w)
        if i == 0:
            wait = HEAD_LAG + 1 if p else 0
            steps = per if p < 2 else per + HEAD_LAG + 1
            late = branch_items(p)
            pending = [x for j in mods[p] for x in (("mod", j), ("modt", j))]
            share = [[] for _ in range(steps)]
            for n, x in enumerate(pending):
                share[min((n + 1) // 2 if p else n, steps - 1)].append(x)
            for n, x in enumerate(late):
                share[wait + n * (steps - wait) // len(late)].append(x)
        yield from scores
        yield from share[i]
        yield from rest


MOD_FIRST = [("mod", 0)] + [x for j in range(1, 4) for x in (("mod", j), ("modt", j - 1))] + [("modt", 3)]


def plan_items():
    out = [(x, "v") for x in MOD_FIRST]
    out += [(("hT", t, q), "av"[q]) for t in range(NT) for q in range(2)]
    out += [(("proj", j, t), "a" if j == 0 or (j + t) % 2 else "v") for j in range(7) for t in range(NT)]
    out += [(("sgu", t), "v") for t in range(NT)]
    out += [(("tt", t, g), "v" if g == 0 else "a") for t in range(4) for g in range(4) if t < NT or g in TT_CACHE]
    out += [(("mq", t), "v") for t in range(NT)]
    out += [(("kv", b), "a") for b in range(4)]
    out += [(("mqt", t), "v") for t in range(NT)]
    out += [(("mkt", b), "a") for b in range(4)]
    for it in list(middle_order()) + branch_items(3):
        if it[0] == "s":
            t, kind, h = HEAD_LIST[it[1]]
            out.append((it, "v" if kind == "C" and t else "p"))
        else:
            out.append((it, "v" if it[0] in ("o", "br", "mod", "modt") else "a"))
    out += [(("gb", i, q), "a") for i in (0, 1) for q in range(2)]
    out += [(("mix", j, t), "v") for j in range(2) for t in range(NT)]
    out += [(("gb", i, q), "a") for i in (2, 3) for q in range(2)]
    out += [(("h2T", t, q), "av"[q]) for t in range(NT) for q in range(2)]
    out += [(("h2", t, q), "av"[q]) for t in range(NT) for q in range(2)]
    out += [(("pq", c), "av"[c % 2]) for c in range(16)]
    out += [(("ps", t, q), "av"[q % 2]) for t in range(NT) for q in range(4)]
    return out


ITEMS = plan_items()
INDEX = {name: n for n, (name, _) in enumerate(ITEMS)}
EVAC_BY = [who for _, who in ITEMS]
EVAC_COUNT = [sum(w == who for w in EVAC_BY[:n + 1]) for n, who in enumerate(EVAC_BY)]

SLOTS = []
for _name, _ in ITEMS:
    if _name[0] == "mod":
        SLOTS += [("mod", _name[1], k) for k in range(2)]
    elif _name[0] == "proj" and _name[2] == 0:
        SLOTS += [("in", _name[1], k) for k in range(2)]
    elif _name == ("sgu", 0):
        SLOTS += [("small",)]
    elif _name[0] == "gate" and _name[2] % 4 == 0:
        SLOTS += [("gate", _name[1], _name[2] // 4, k) for k in range(2)]
    elif _name[0] == "br" and _name[2] % 4 == 0:
        SLOTS += [("branch", _name[1], _name[2] // 4)]
SLOTS += [("out", j, k) for j in range(2) for k in range(2)]
SLOTS += [("pq", j, k) for j in range(4) for k in range(2)] + [("sub",)]
SLOT_OF = {s: n for n, s in enumerate(SLOTS)}
def last_item(s):
    return {"mod": lambda: ("mod", s[1]), "in": lambda: ("proj", s[1], NT - 1), "small": lambda: ("kv", 3),
            "gate": lambda: ("gate", s[1], 4 * s[2] + 3), "branch": lambda: ("br", s[1], 4 * s[2] + 3),
            "out": lambda: ("mix", s[1], NT - 1), "pq": lambda: ("pq", 4 * s[1] + 3), "sub": lambda: ("ps", NT - 1, 3)}[s[0]]()


S_UQ, S_UKV, S_SW, S_W = 0, 768, 1280, 1792


def build(nc, a, outs):
    with ExitStack() as ctx:
        def sb(name, words, dt=F32):
            return ctx.enter_context(nc.sbuf_tensor(name, [P, words], dt))

        def sem(name):
            s = ctx.enter_context(nc.semaphore(name))
            return s

        x = sb("x", NT * D)[:, :].rearrange("p (t d) -> p t d", t=NT)
        hT = sb("hT", KD * NTOK)[:, :].rearrange("p (k n) -> p k n", k=KD)
        rows = sb("rows", R_L1G)
        bias = sb("bias", 2 * HEADS * 256)[:, :].rearrange("p (t h n) -> p t h n", t=2, h=HEADS)
        cols = sb("cols", COLS)
        consts = sb("consts", K_W)
        diag = sb("diag", 512)
        modT = sb("modT", 96)[:, :].rearrange("p (n c) -> p n c", c=2)
        silu = sb("silu", 16)[:, :].rearrange("p (k c) -> p k c", c=2)
        wring = sb("wring", W_RING * W_SLOT)
        stat = sb("stat", 256)
        psum = ctx.enter_context(nc.psum_tensor("psum", [P, 8, 512], F32))
        ident = consts[:, K_ID:K_ID + P]
        ones = consts[:, K_ON:K_ON + P]

        WORK = 31744
        work = sb("work", WORK)

        def region(at, words):
            assert at + words <= WORK
            return work[:, at:at + words]

        proj = region(0, NT * IN_W).rearrange("p (t n) -> p t n", t=NT)
        TTO = NT * IN_W
        TT = region(TTO, TT_BLOCKS * 512).rearrange("p (b n) -> p b n", b=TT_BLOCKS)
        outT = [region(TTO + at, n * NTOK).rearrange("p (k n) -> p k n", k=n)
                for at, n in ((0, 2), (2 * NTOK, 2), (B_NQ * 512, 2), (B_DQ * 512, 4))]
        o = TTO + TT_BLOCKS * 512
        VB = region(o, 4 * 256).rearrange("p (b n) -> p b n", b=4)
        o += 4 * 256
        MQT = region(o, HEADS * NTOK).rearrange("p (h n) -> p h n", h=HEADS)
        o += HEADS * NTOK
        MKT = region(o, HEADS * 512).rearrange("p (h n) -> p h n", h=HEADS)
        o += HEADS * 512
        cache = region(o, C_W)
        o += C_W
        MQ = region(o, NT * 384).rearrange("p (t n) -> p t n", t=NT)
        KB = region(o + NT * 384, 4 * 384).rearrange("p (b h n) -> p b h n", b=4, h=HEADS)
        PB = region(o, P_BUFS * 384).rearrange("p (r n) -> p r n", r=P_BUFS)
        o += (NT + 4) * 384
        PT = region(o, 2 * 384).rearrange("p (r b n) -> p r b n", r=2, b=3)
        o += 2 * 384
        xn = region(o, NT * D).rearrange("p (t d) -> p t d", t=NT)
        mergedT = region(o, KD * NTOK).rearrange("p (k n) -> p k n", k=KD)
        o += KD * NTOK
        sg = region(o, 4 * NTOK).rearrange("p (n q) -> p n q", n=4)
        tmp = region(o, 512)
        nbs = sb("nbs", 2 * 384)[:, :].rearrange("p (r n) -> p r n", r=2)

        ringU = region(0, 8 * D).rearrange("p (r d) -> p r d", r=8)
        ringV = region(8 * D, 8 * D).rearrange("p (r d) -> p r d", r=8)
        S = region(0, NT * 2048).rearrange("p (t c n) -> p t c n", t=NT, c=16)
        qT = region(8 * D, 16 * NTOK).rearrange("p (c n) -> p c n", c=16)
        o = 16 * D
        h2 = region(o, NT * D).rearrange("p (t d) -> p t d", t=NT)
        o += NT * D
        y = region(o, 2 * D).rearrange("p (r d) -> p r d", r=2)
        o += 2 * D
        cand = region(14 * D, 2048)
        eq = region(o - 2 * D, 2048)
        xn2 = region(0, NT * D).rearrange("p (t d) -> p t d", t=NT)
        v16 = region(o, 256).rearrange("p (c k) -> p c k", c=16)
        i16f = region(o + 256, 256).rearrange("p (c k) -> p c k", c=16)
        best = region(o + 512, 128).rearrange("p (h k) -> p h k", h=PH)
        selA = region(o + 640, 128)
        selB = region(o + 768, 128)
        o += 896
        lnrows = region(o, 2 * D)
        gains = region(o + 2 * D, 2 * D).rearrange("p (i d) -> p i d", i=2)
        i16 = sb("i16", 256, U32)[:, :].rearrange("p (c k) -> p c k", c=16)
        bi = sb("bi", 256, U32)[:, :].rearrange("p (r n) -> p r n", r=2)
        gates = sb("gates", NT * KSEL)
        experts = sb("experts", NT * KSEL + 8, I32)
        exslot = sb("exslot", 8, I32)
        dots = sb("dots", 8)
        acts = sb("acts", 8)
        wts = sb("wts", 8)

        names = ["loaded", "psum_full", "dve_evac", "act_evac", "dve_step", "ln1_done", "merge_done",
                 "diag_ready", "bias_ready", "sigmoid_exp", "xn_ready", "norms_ready", "kb_ready",
                 "negmax_ready", "probs_ready", "nbs_ready", "weights_ready", "outs_ready", "merged_ready",
                 "h2_ready", "best_ready", "gate_exp", "experts_ready", "dots_ready", "gelu_ready", "stored",
                 "new_ready", "x_ready", "sqin", "sqout", "lam_in", "lam_out", "acc_done"]
        sems = {n: sem(n) for n in names}
        w_ready = [sem(f"w_ready{i}") for i in range(W_RING)]
        gotU = [sem(f"gotU{i}") for i in range(8)]
        gotV = [sem(f"gotV{i}") for i in range(8)]
        setup_loaded = sem("setup_loaded")
        setup_done = sem("setup_done")
        gather_gate = sem("gather_gate")
        loaded, psum_full, dve_evac, act_evac = (sems[n] for n in names[:4])

        def bank(name):
            return psum[:, INDEX[name] % 8, :]

        def full(eng, name):
            eng.wait_ge(psum_full, INDEX[name] + 1)

        def evacuated(eng, name):
            n = INDEX[name]
            if EVAC_BY[n] == "p":
                eng.wait_ge(sems["probs_ready"], ROW_OF[name[1:]] + 1)
            else:
                eng.wait_ge(dve_evac if EVAC_BY[n] == "v" else act_evac, EVAC_COUNT[n])

        def all_evacuated(eng, names_):
            for who in "va":
                last = [n for n in names_ if EVAC_BY[INDEX[n]] == who]
                if last:
                    evacuated(eng, max(last, key=lambda n: INDEX[n]))

        with nc.Block() as block:
            @block.sync
            def _(sp):
                for t in range(NT):
                    src = a["x_prompt"][0] if t == 0 else a["x_sample"][0, (t - 1) * P:t * P, :]
                    sp.dma_start(x[:, t, :], src).then_inc(setup_loaded, 16)
                sp.dma_start(consts[:, :], a["consts"]).then_inc(setup_loaded, 16)
                sp.dma_start(silu, a["cond"]).then_inc(setup_loaded, 16)
                sp.wait_ge(setup_loaded, 80)

            @block.scalar
            def _(act):
                act.wait_ge(setup_loaded, 80)
                nc.scalar.activation(silu, silu, ACT.Silu).then_inc(setup_done, 1)

            @block.tensor
            def _(pe):
                pe.wait_ge(setup_done, 2)

            @block.vector
            def _(dve):
                nc.vector.memset(experts[:, NT * KSEL:], 0).then_inc(setup_done, 1)
                dve.wait_ge(setup_done, 2)

            @block.gpsimd
            def _(pool):
                pool.wait_ge(setup_done, 2)
        nc.all_engine_barrier()

        with nc.Fori(0, DEPTH) as l:
            with nc.Block() as block:
                @block.sync
                def _(sp):
                    lay = bass.ds(l, 1)
                    sp.dma_start(cols[:, :], a["cols"][lay].rearrange("a p n -> p (a n)")).then_inc(loaded, 16)
                    sp.dma_start(rows[:, :], a["rows"][lay, 0:R_L1G].broadcast_to([P, R_L1G])).then_inc(loaded, 16)
                    sp.dma_start(cache, a["cache"][lay].rearrange("a p n -> p (a n)")).then_inc(loaded, 16)
                    sp.dma_start(bias.rearrange("p t h n -> p (t h n)"),
                                 a["rpb"][lay].rearrange("a p n -> p (a n)")).then_inc(loaded, 16)

                    def cols_of(name, j, width, k0, nk):
                        w = a[name][lay].rearrange("a (k p) n -> p (a k) n", p=P)
                        return w[:, k0:k0 + nk, j:j + width]

                    for n, s in enumerate(SLOTS):
                        if n >= W_RING:
                            full(sp, last_item(SLOTS[n - W_RING]))
                        base = (n % W_RING) * W_SLOT
                        ready = w_ready[n % W_RING]
                        kind = s[0]
                        if kind == "small":
                            sp.dma_start(wring[:, base:base + S_W],
                                         a["small"][lay].rearrange("a p n -> p (a n)")).then_inc(ready, 16)
                        elif kind == "sub":
                            sp.dma_start(wring[:, base:base + W_SLOT],
                                         a["subT"][lay].rearrange("a p n -> p (a n)")).then_inc(ready, 16)
                        elif kind == "branch":
                            dst = wring[:, base:base + W_SLOT].rearrange("p (k n) -> p k n", k=4)[:, 0:BRANCH_K[s[1]], :]
                            sp.dma_start(dst, cols_of("w_branch_" + "abcd"[s[1]], 512 * s[2], 512, 0, BRANCH_K[s[1]])).then_inc(ready, 16)
                        else:
                            name = {"mod": "w_mod", "in": "w_in", "gate": "w_gate", "out": "w_out", "pq": "peer_w_q"}[kind]
                            col = (s[1] * 2 + s[2]) * 512 if kind == "gate" else s[1] * 512
                            width = min(512, IN_W - col) if kind == "in" else 512
                            dst = wring[:, base:base + W_SLOT].rearrange("p (k n) -> p k n", k=4)[:, :, 0:width]
                            sp.dma_start(dst, cols_of(name, col, width, 4 * s[-1], 4)).then_inc(ready, 16)
                    sp.wait_ge(sems["ln1_done"], 1)
                    sp.dma_start(lnrows, a["rows"][lay, R_L2G:R_W].broadcast_to([P, 2 * D])).then_inc(loaded, 16)
                    for t in range(NT):
                        sp.wait_ge(sems["x_ready"], t + 1)
                        dst = outs[0][0] if t == 0 else outs[1][0, (t - 1) * P:t * P, :]
                        sp.dma_start(dst, x[:, t, :]).then_inc(sems["stored"], 16)
                    sp.wait_ge(sems["stored"], 16 * (NT + 6))

                @block.tensor
                def _(pe):
                    def slot(s, k):
                        n = SLOT_OF[s]
                        pe.wait_ge(w_ready[n % W_RING], 16 * (n // W_RING + 1))
                        base = (n % W_RING) * W_SLOT
                        return wring[:, base:base + W_SLOT].rearrange("p (k n) -> p k n", k=k)

                    def room(name):
                        if INDEX[name] >= 8:
                            evacuated(pe, ITEMS[INDEX[name] - 8][0])
                        return bank(name)

                    def mod_item(it):
                        j = it[1]
                        out = room(it)
                        if it[0] == "mod":
                            w = [slot(("mod", j, k), 4) for k in range(2)]
                            for k in range(KD):
                                last = nc.tensor.matmul(out[0:2, :], silu[:, k, :], w[k // 4][:, k % 4, :],
                                                        start=(k == 0), stop=(k == KD - 1))
                        else:
                            evacuated(pe, ("mod", j))
                            for n in range(4):
                                last = nc.tensor.transpose(out[:, 2 * n:2 * n + 2], diag[0:2, n * P:(n + 1) * P], ident[0:2, 0:2])
                        last.then_inc(psum_full, 1)

                    pe.wait_ge(loaded, 64)
                    for it in MOD_FIRST:
                        mod_item(it)

                    def spread_gains(pair):
                        for i in pair:
                            for q in range(2):
                                out = room(("gb", i, q))
                                pe.wait_ge(sems["diag_ready"], 2 * i + q + 1)
                                nc.tensor.matmul(out, ones, diag[:, :], start=True, stop=True).then_inc(psum_full, 1)

                    def transposed(kind, src, ready, count):
                        for t in range(NT):
                            pe.wait_ge(ready, count + t)
                            for q in range(2):
                                out = room((kind, t, q))
                                for k in range(4):
                                    last = nc.tensor.transpose(out[:, k * P:(k + 1) * P],
                                                               src[:, t, (4 * q + k) * P:(4 * q + k + 1) * P], ident)
                                last.then_inc(psum_full, 1)

                    transposed("hT", xn, sems["xn_ready"], 1)

                    all_evacuated(pe, [("hT", t, q) for t in range(NT) for q in range(2)])
                    for j in range(7):
                        width = min(512, IN_W - 512 * j)
                        outb = [room(("proj", j, t)) for t in range(NT)]
                        for half in range(2):
                            w = slot(("in", j, half), 4)
                            for t in range(NT):
                                for k in range(4):
                                    kk = 4 * half + k
                                    last = nc.tensor.matmul(outb[t][:, 0:width], hT[:, kk, t * P:(t + 1) * P],
                                                            w[:, k, 0:width], start=(kk == 0), stop=(kk == KD - 1))
                                if half == 1:
                                    last.then_inc(psum_full, 1)

                    small = slot(("small",), 1)[:, 0, :]
                    pe.wait_ge(sems["norms_ready"], 1)
                    for t in range(NT):
                        out = room(("sgu", t))
                        for g in range(4):
                            last = nc.tensor.matmul(out[:, g * 64:(g + 1) * 64], small[:, S_SW + g * P:S_SW + (g + 1) * P],
                                                    proj[:, t, AV + 64 * g:AV + 64 * (g + 1)], start=True, stop=True)
                        last.then_inc(psum_full, 1)
                    for t in range(4):
                        for g in range(4):
                            if t == NT and g not in TT_CACHE:
                                continue
                            out = room(("tt", t, g))
                            blocks = TT_CACHE[g] if t == NT else list(enumerate(TT_SRC[g]))
                            for i, c in blocks:
                                src = cache[:, c:c + P] if t == NT else proj[:, t, c:c + P]
                                last = nc.tensor.transpose(out[:, i * P:(i + 1) * P], src, ident)
                            last.then_inc(psum_full, 1)
                    all_evacuated(pe, [("tt", 3, 0), ("tt", 2, 0)])
                    for t in range(NT):
                        out = room(("mq", t))
                        for k in range(2):
                            last = nc.tensor.matmul(out[:, 0:384], TT[:, k, t * P:(t + 1) * P],
                                                    small[:, S_UQ + 384 * k:S_UQ + 384 * (k + 1)],
                                                    start=(k == 0), stop=(k == 1))
                        last.then_inc(psum_full, 1)
                    for b in range(4):
                        nc.tensor.matmul(room(("kv", b)), TT[:, 2, b * P:(b + 1) * P], small[:, S_UKV:S_UKV + 512],
                                         start=True, stop=True).then_inc(psum_full, 1)
                    for t in range(NT):
                        out = room(("mqt", t))
                        evacuated(pe, ("mq", t))
                        for h in range(HEADS):
                            last = nc.tensor.transpose(out[0:MQK, h * P:(h + 1) * P], MQ[:, t, h * MQK:(h + 1) * MQK], ident)
                        last.then_inc(psum_full, 1)
                    for b in range(4):
                        out = room(("mkt", b))
                        evacuated(pe, ("kv", b))
                        pe.wait_ge(sems["kb_ready"], 1)
                        for h in range(HEADS):
                            last = nc.tensor.transpose(out[0:MQK, h * P:(h + 1) * P], KB[:, b, h, :], ident)
                        last.then_inc(psum_full, 1)

                    all_evacuated(pe, [("mqt", 2), ("mkt", 3)])
                    all_evacuated(pe, [("tt", t, g) for t in range(4) for g in range(4) if t < NT or g in TT_CACHE])
                    def branch_item(it):
                        b, n = it[1:]
                        out = room(it)
                        if it[0] == "ot":
                            if b in (1, 2):
                                evacuated(pe, ("o", 12 * b - 1))
                            elif b == 3:
                                pe.wait_ge(sems["outs_ready"], 1)
                            else:
                                evacuated(pe, ("sgu", NT - 1))
                            c = [OUT_A, OUT_B, OUT_C, OUT_D][b] + n * P
                            for t in range(NT):
                                last = nc.tensor.transpose(out[:, t * P:(t + 1) * P], proj[:, t, c:c + P], ident)
                        elif it[0] == "gate":
                            w = [slot(("gate", b, n // 4, k), 4) for k in range(2)]
                            for k in range(KD):
                                last = nc.tensor.matmul(out[:, 0:NTOK], w[k // 4][:, k % 4, n % 4 * P:(n % 4 + 1) * P], hT[:, k, :],
                                                        start=(k == 0), stop=(k == KD - 1))
                        else:
                            w = slot(("branch", b, n // 4), 4)
                            all_evacuated(pe, [("ot", b, k) for k in range(BRANCH_K[b])])
                            for k in range(BRANCH_K[b]):
                                last = nc.tensor.matmul(out[:, 0:NTOK], w[:, k, n % 4 * P:(n % 4 + 1) * P], outT[b][:, k, :],
                                                        start=(k == 0), stop=(k == BRANCH_K[b] - 1))
                        last.then_inc(psum_full, 1)

                    for it in middle_order():
                        if it[0] in ("mod", "modt"):
                            mod_item(it)
                            continue
                        if it[0] in ("ot", "gate", "br"):
                            branch_item(it)
                            continue
                        w = it[1]
                        t, kind, h = HEAD_LIST[w]
                        out = room(it)
                        blocks = key_blocks(t)
                        nk = P * len(blocks)
                        k0 = P * blocks[0]
                        if it[0] == "s":
                            if kind == "B":
                                q, k = MQT[0:MQK, h, t * P:(t + 1) * P], MKT[0:MQK, h, k0:k0 + nk]
                            elif kind == "C":
                                lo = 64 * (h % 2)
                                q, k = TT[lo:lo + 64, B_NQ + h // 2, t * P:(t + 1) * P], TT[lo:lo + 64, B_NK + h // 2, k0:k0 + nk]
                            else:
                                lo = 64 * it[2]
                                q, k = TT[lo:lo + 64, B_DQ + h, t * P:(t + 1) * P], TT[lo:lo + 64, B_DK + h, k0:k0 + nk]
                            nc.tensor.matmul(out[:, 0:nk], q, k, start=True, stop=True).then_inc(psum_full, 1)
                        elif it[0] == "pt":
                            r = ROW_OF[(w, 0)]
                            if kind == "D":
                                pe.wait_ge(sems["weights_ready"], sum(1 for q_ in HEAD_LIST[:w + 1] if q_[1] == "D"))
                            else:
                                pe.wait_ge(sems["probs_ready"], r + 1)
                            for i in range(len(blocks)):
                                last = nc.tensor.transpose(out[:, i * P:(i + 1) * P], PB[:, r % P_BUFS, i * P:(i + 1) * P], ident)
                            last.then_inc(psum_full, 1)
                        else:
                            evacuated(pe, ("pt", w))
                            for i, b in enumerate(blocks):
                                if kind == "B":
                                    v = VB[:, b, 64 * h:64 * (h + 1)]
                                elif kind == "C":
                                    v = proj[:, b, NV + 64 * h:NV + 64 * (h + 1)] if b < NT else cache[:, C_NV + 64 * h:C_NV + 64 * (h + 1)]
                                else:
                                    v = proj[:, b, DVO + P * h:DVO + P * (h + 1)] if b < NT else cache[:, C_DV + P * h:C_DV + P * (h + 1)]
                                last = nc.tensor.matmul(out[:, 0:P if kind == "D" else 64], PT[:, w % 2, i, :], v,
                                                        start=(i == 0), stop=(i == len(blocks) - 1))
                            last.then_inc(psum_full, 1)

                    for it in branch_items(3):
                        branch_item(it)
                    spread_gains((0, 1))
                    pe.wait_ge(sems["merged_ready"], 1)
                    for j in range(2):
                        outb = [room(("mix", j, t)) for t in range(NT)]
                        for half in range(2):
                            w = slot(("out", j, half), 4)
                            for t in range(NT):
                                for k in range(4):
                                    kk = 4 * half + k
                                    last = nc.tensor.matmul(outb[t], mergedT[:, kk, t * P:(t + 1) * P], w[:, k, :],
                                                            start=(kk == 0), stop=(kk == KD - 1))
                                if half == 1:
                                    last.then_inc(psum_full, 1)
                    spread_gains((2, 3))
                    transposed("h2T", xn2, sems["xn_ready"], NT + 1)
                    for t in range(NT):
                        all_evacuated(pe, [("h2T", t, 0), ("h2T", t, 1)])
                        for q in range(2):
                            out = room(("h2", t, q))
                            for k in range(4):
                                last = nc.tensor.transpose(out[:, k * P:(k + 1) * P], hT[:, 4 * q + k, t * P:(t + 1) * P], ident)
                            last.then_inc(psum_full, 1)
                    for j in range(4):
                        outb = [room(("pq", 4 * j + n)) for n in range(4)]
                        for kh in range(2):
                            w = slot(("pq", j, kh), 4)
                            for n in range(4):
                                for k in range(4):
                                    kk = 4 * kh + k
                                    last = nc.tensor.matmul(outb[n][:, 0:NTOK], w[:, k, n * P:(n + 1) * P], hT[:, kk, :],
                                                            start=(kk == 0), stop=(kk == KD - 1))
                                if kh == 1:
                                    last.then_inc(psum_full, 1)
                    sub = slot(("sub",), 16)
                    all_evacuated(pe, [("pq", c) for c in range(16)])
                    for t in range(NT):
                        for q in range(4):
                            out = room(("ps", t, q))
                            for i in range(4):
                                c = 4 * q + i
                                last = nc.tensor.matmul(out[:, i * P:(i + 1) * P], qT[:, c, t * P:(t + 1) * P], sub[:, c, :],
                                                        start=True, stop=True)
                            last.then_inc(psum_full, 1)

                @block.scalar
                def _(act):
                    cond = [0, 1, 1]

                    def taken(ins):
                        return ins.then_inc(act_evac, 1)

                    act.wait_ge(loaded, 64)
                    def take_gains(pair):
                        for i in pair:
                            for q in range(2):
                                full(act, ("gb", i, q))
                                taken(nc.scalar.copy(gains[:, i % 2, q * 512:(q + 1) * 512], bank(("gb", i, q))))


                    def shift_scale(kind, t, q, sh, sc):
                        full(act, (kind, t, q))
                        evacuated(act, ("modt", 3 if kind == "hT" else 11))
                        for k in range(4):
                            n = 4 * q + k
                            last = nc.scalar.activation(hT[:, n, t * P:(t + 1) * P], bank((kind, t, q))[:, k * P:(k + 1) * P],
                                                        ACT.Identity, bias=modT[:, sh + n, cond[t]:cond[t] + 1],
                                                        scale=modT[:, sc + n, cond[t]:cond[t] + 1])
                        taken(last)

                    sq = [0]

                    def square_roots(width, scale):
                        sq[0] += 1
                        act.wait_ge(sems["sqin"], sq[0])
                        nc.scalar.activation(stat[:, 16:16 + width], stat[:, 0:width], ACT.Sqrt,
                                             bias=cols[:, C_EO:C_EO + 1], scale=scale).then_inc(sems["sqout"], 1)

                    square_roots(NT, 1.0)
                    for t in range(NT):
                        shift_scale("hT", t, 0, 0, 8)
                    for j in range(7):
                        width = min(512, IN_W - 512 * j)
                        for t in range(NT):
                            name = ("proj", j, t)
                            if EVAC_BY[INDEX[name]] != "a":
                                continue
                            full(act, name)
                            taken(nc.scalar.activation(proj[:, t, 512 * j:512 * j + width], bank(name)[:, 0:width],
                                                       ACT.Gelu if j == 0 else ACT.Copy))
                    square_roots(3 * NT, 1.0)
                    act.wait_ge(sems["lam_in"], 1)
                    nc.scalar.activation(stat[:, 48:50], stat[:, 46:48], ACT.Exp).then_inc(sems["lam_out"], 1)
                    act.wait_ge(sems["new_ready"], 1)
                    lay = bass.ds(l, 1)
                    for i, (c, width) in enumerate([(CKV, 128), (KR, 32), (NK, 256), (NV, 256), (DK, 512), (DVO, 512)]):
                        act.dma_start(outs[2 + i][lay].rearrange("a p n -> p (a n)"), proj[:, 0, c:c + width])\
                           .then_inc(sems["stored"], 16)
                    for t in range(4):
                        for g in range(1, 4):
                            if t == NT and g not in TT_CACHE:
                                continue
                            name = ("tt", t, g)
                            full(act, name)
                            lo = 2 if (t == NT and g == 1) else 0
                            b0 = TT_FIRST[g]
                            taken(nc.scalar.copy(TT[:, b0 + lo:b0 + 4, t * P:(t + 1) * P],
                                                 bank(name)[:, lo * P:512].rearrange("p (b n) -> p b n", n=P)))
                    for b in range(4):
                        full(act, ("kv", b))
                        src = bank(("kv", b)).rearrange("p (h n) -> p h n", h=HEADS)
                        nc.scalar.copy(KB[:, b, :, 0:NOPE], src[:, :, 0:NOPE])
                        taken(nc.scalar.copy(VB[:, b, :].rearrange("p (h n) -> p h n", h=HEADS), src[:, :, NOPE:NOPE + MV]))
                    for b in range(4):
                        full(act, ("mkt", b))
                        taken(nc.scalar.copy(MKT[0:MQK, :, b * P:(b + 1) * P],
                                             bank(("mkt", b))[0:MQK, :].rearrange("p (h n) -> p h n", h=HEADS)))
                    def branch_item(it):
                        b, n = it[1:]
                        full(act, it)
                        if it[0] == "ot":
                            if n == 0 and b >= 2:
                                full(act, ("o", 12 * b - 1))
                            taken(nc.scalar.copy(outT[b][:, n, :], bank(it)[:, 0:NTOK]))
                        elif it[0] == "gate":
                            i = 8 * b + n
                            if 4 <= i < 12:
                                evacuated(act, ("br", 0, i - 4))
                            elif i >= 12:
                                act.wait_ge(sems["merge_done"], i - 11)
                            else:
                                act.wait_ge(sems["bias_ready"], 1)
                            nc.scalar.activation(sg[:, n % 4, :], bank(it)[:, 0:NTOK], ACT.Exp, scale=-1.0,
                                                 bias=cols[:, C_BG + i:C_BG + i + 1]).then_inc(sems["sigmoid_exp"], 1)
                            act.wait_ge(sems["sigmoid_exp"], i + 1)
                            taken(nc.scalar.add(sg[:, n % 4, :], sg[:, n % 4, :], 1.0))

                    for it in middle_order():
                        if it[0] in ("mod", "modt", "br"):
                            continue
                        if it[0] in ("ot", "gate"):
                            branch_item(it)
                            continue
                        w = it[1]
                        t, kind, h = HEAD_LIST[w]
                        nk = P * len(key_blocks(t))
                        if it[0] == "s":
                            r = ROW_OF[(w, it[2])]
                            if r >= P_BUFS:
                                full(act, ("pt", ROWS[r - P_BUFS][0]))
                            act.wait_ge(sems["negmax_ready"], r + 1)
                            if kind == "C" and t:
                                c = sum(1 for q_ in HEAD_LIST[:w] if q_[1] == "C" and q_[0])
                                src, scale = nbs[:, c % 2, 0:nk], 1.0
                            else:
                                src, scale = bank(it)[:, 0:nk], (MQK if kind == "B" else 64) ** -0.5
                            ins = nc.scalar.activation(PB[:, r % P_BUFS, 0:nk], src, ACT.Exp, bias=stat[:, 64 + r:65 + r],
                                                       scale=scale, accum_out=stat[:, 112 + r:113 + r])
                            ins.then_inc(sems["probs_ready"], 1)
                        elif it[0] == "pt":
                            full(act, it)
                            if w >= 2:
                                full(act, ("o", w - 2))
                            taken(nc.scalar.copy(PT[:, w % 2, 0:nk // P, :],
                                                 bank(it)[:, 0:nk].rearrange("p (b n) -> p b n", n=P)))
                    full(act, ("o", len(HEAD_LIST) - 1))
                    act.dma_start(lnrows, a["rows"][lay, R_L1G:R_L2G].broadcast_to([P, 2 * D])).then_inc(loaded, 16)
                    square_roots(NT * HEADS, 1.0 / DV)
                    for it in branch_items(3):
                        if it[0] != "br":
                            branch_item(it)
                    take_gains((0, 1))
                    take_gains((2, 3))
                    square_roots(NT, 1.0)
                    square_roots(NT, 1.0)
                    for t in range(NT):
                        shift_scale("h2T", t, 0, 24, 32)
                    for t in range(NT):
                        full(act, ("h2", t, 0))
                        taken(nc.scalar.copy(h2[:, t, 0:512], bank(("h2", t, 0))))
                    for c in range(0, 16, 2):
                        full(act, ("pq", c))
                        taken(nc.scalar.copy(qT[:, c, :], bank(("pq", c))[:, 0:NTOK]))
                    for t in range(NT):
                        for q in (0, 2):
                            full(act, ("ps", t, q))
                            taken(nc.scalar.copy(S[:, t, 4 * q:4 * q + 4, :],
                                                 bank(("ps", t, q)).rearrange("p (c n) -> p c n", n=P)))
                    for t in range(NT):
                        act.wait_ge(sems["best_ready"], t + 1)
                        gt = gates[:, t * KSEL:(t + 1) * KSEL]
                        nc.scalar.activation(gt, gt, ACT.Exp).then_inc(sems["gate_exp"], 1)
                    for t in range(NT):
                        with act.Fori(0, STEPS) as i:
                            for g in range(2):
                                act.wait_ge(sems["dots_ready"], GROUP * (i * 2 + (2 * STEPS * t + g + 1)))
                                nc.scalar.activation(acts[:, GROUP * g:GROUP * (g + 1)], dots[:, GROUP * g:GROUP * (g + 1)],
                                                     ACT.Gelu).then_inc(sems["gelu_ready"], 1)
                        square_roots(1, 1.0)

                @block.vector
                def _(dve):
                    cond = [0, 1, 1]
                    steps = [0]
                    dve_step = sems["dve_step"]

                    def step(ins):
                        steps[0] += 1
                        ins.then_inc(dve_step, 1)

                    def sync():
                        dve.wait_ge(dve_step, steps[0])

                    def link(ins):
                        step(ins)
                        sync()

                    def taken(ins):
                        return ins.then_inc(dve_evac, 1)

                    sq = [0]

                    def roots(width):
                        sync()
                        sq[0] += 1
                        dve.sem_inc(sems["sqin"], 1)
                        dve.wait_ge(sems["sqout"], sq[0])
                        link(nc.vector.reciprocal(stat[:, 32:32 + width], stat[:, 16:16 + width]))

                    bn = stat[:, 160:256]

                    def mean_var(slot_, src, width):
                        nb = (width + 511) // 512
                        part = bn[:, 12 * (slot_ % 3):12 * (slot_ % 3) + 6 * nb]
                        for i in range(nb):
                            step(nc.vector.bn_stats(part[:, 6 * i:6 * i + 6], src[:, i * (width // nb):(i + 1) * (width // nb)]))
                        sync()
                        link(nc.vector.bn_aggr(bn[:, 36 + 2 * slot_:38 + 2 * slot_], part))
                        step(nc.vector.tensor_copy(stat[:, slot_:slot_ + 1], bn[:, 37 + 2 * slot_:38 + 2 * slot_]))

                    def normalised(dst, ready):
                        for t in range(NT):
                            nc.vector.tensor_scalar(dst[:, t, :], x[:, t, :], bn[:, 36 + 2 * t:37 + 2 * t], stat[:, 32 + t:33 + t],
                                                    ALU.subtract, ALU.mult).then_inc(ready, 1)

                    dve.wait_ge(loaded, 64)
                    for lo in (8, 32):
                        step(nc.vector.tensor_scalar(cols[:, C_BM + lo:C_BM + lo + 8], cols[:, C_BM + lo:C_BM + lo + 8], 1.0, None, ALU.add))
                    nc.vector.tensor_scalar(cols[:, C_BG:C_BG + 32], cols[:, C_BG:C_BG + 32], -1.0, None, ALU.mult)\
                        .then_inc(sems["bias_ready"], 1)
                    sync()

                    def mod_item(it):
                        j = it[1]
                        full(dve, it)
                        if it[0] == "mod":
                            if j:
                                full(dve, ("modt", j - 1))
                            taken(nc.vector.tensor_copy(diag[0:2, :], bank(it)[0:2, :]))
                        else:
                            taken(nc.vector.tensor_tensor(modT[:, 4 * j:4 * j + 4, :],
                                                          bank(it)[:, 0:8].rearrange("p (n c) -> p n c", c=2),
                                                          spread(cols[:, C_BM + 4 * j:C_BM + 4 * j + 4].unsqueeze(2), 2, 2), ALU.add))

                    for it in MOD_FIRST:
                        mod_item(it)

                    def diagonals(pair):
                        for i in pair:
                            for q in range(2):
                                if i == 0 and q == 0:
                                    evacuated(dve, ("modt", 11))
                                else:
                                    full(dve, ("gb", (2 * i + q - 1) // 2, (2 * i + q - 1) % 2))
                                base = 16 if i < 2 else 40
                                for k in range(4):
                                    last = nc.vector.tensor_scalar(diag[:, k * P:(k + 1) * P], ident,
                                                                   modT[:, base + 4 * q + k, i % 2:i % 2 + 1], None, ALU.mult)
                                last.then_inc(sems["diag_ready"], 1)

                    for t in range(2):
                        for h in range(HEADS):
                            step(nc.vector.tensor_tensor(bias[:, t, h, :], bias[:, t, h, :], consts[:, K_MA:K_MA + 256], ALU.add))
                    for t in range(NT):
                        mean_var(t, x[:, t, :], D)
                    roots(NT)
                    normalised(xn, sems["xn_ready"])

                    def shift_scale(kind, t, sh, sc):
                        full(dve, (kind, t, 1))
                        evacuated(dve, ("modt", 3 if kind == "hT" else 11))
                        for k in range(4):
                            n = 4 + k
                            last = nc.vector.tensor_scalar(hT[:, n, t * P:(t + 1) * P], bank((kind, t, 1))[:, k * P:(k + 1) * P],
                                                           modT[:, sc + n, cond[t]:cond[t] + 1],
                                                           modT[:, sh + n, cond[t]:cond[t] + 1], ALU.mult, ALU.add)
                        taken(last)

                    for t in range(NT):
                        shift_scale("hT", t, 0, 8)
                    for j in range(7):
                        width = min(512, IN_W - 512 * j)
                        for t in range(NT):
                            name = ("proj", j, t)
                            if EVAC_BY[INDEX[name]] == "v":
                                full(dve, name)
                                taken(nc.vector.tensor_copy(proj[:, t, 512 * j:512 * j + width], bank(name)[:, 0:width]))
                    all_evacuated(dve, [("proj", j, t) for j in range(7) for t in range(NT)])
                    for t in range(NT):
                        mean_var(t, proj[:, t, AV:AV + 256], 256)
                        for i, (c, width) in enumerate([(CQ, 256), (CKV, 128)]):
                            n = 3 + 3 * i + t
                            mean_var(n, proj[:, t, c:c + width], width)
                            sync()
                            link(nc.vector.scalar_tensor_tensor(out=stat[:, n:n + 1], in0=bn[:, 36 + 2 * n:37 + 2 * n],
                                                                scalar=bn[:, 36 + 2 * n:37 + 2 * n],
                                                                in1=bn[:, 37 + 2 * n:38 + 2 * n], op0=ALU.mult, op1=ALU.add))
                    roots(3 * NT)
                    for t in range(NT):
                        av = proj[:, t, AV:AV + 256]
                        step(nc.vector.tensor_scalar(av, av, bn[:, 36 + 2 * t:37 + 2 * t], stat[:, 32 + t:33 + t], ALU.subtract, ALU.mult))
                        cq = proj[:, t, CQ:CQ + 256]
                        step(nc.vector.tensor_scalar(cq, cq, stat[:, 35 + t:36 + t], None, ALU.mult))
                        ck = proj[:, t, CKV:CKV + P]
                        step(nc.vector.scalar_tensor_tensor(out=ck, in0=ck, scalar=stat[:, 38 + t:39 + t],
                                                            in1=rows[:, R_KVG:R_KVG + P], op0=ALU.mult, op1=ALU.mult))
                    sync()
                    for t in range(NT):
                        av = proj[:, t, AV:AV + 256]
                        step(nc.vector.tensor_tensor(av, av, rows[:, R_SG:R_SG + 256], ALU.mult))
                    sync()
                    dve.sem_inc(sems["new_ready"], 1)

                    def rotate(dst, src, t, groups, half, kc, ks):
                        cs = spread(consts[:, kc + (t - 1) * half:kc + t * half].unsqueeze(1), 1, groups)
                        sn = spread(consts[:, ks + (t - 1) * half:ks + t * half].unsqueeze(1), 1, groups)
                        x1, x2 = src[:, :, 0:half], src[:, :, half:2 * half]
                        bufs = [hold[:, i * groups * half:(i + 1) * groups * half].rearrange("p (g n) -> p g n", g=groups)
                                for i in range(4)]
                        for b_, (u, v) in zip(bufs, [(x1, cs), (x2, sn), (x2, cs), (x1, sn)]):
                            step(nc.vector.tensor_tensor(b_, u, v, ALU.mult))
                        sync()
                        step(nc.vector.tensor_tensor(dst[:, :, 0:half], bufs[0], bufs[1], ALU.subtract))
                        return nc.vector.tensor_tensor(dst[:, :, half:2 * half], bufs[2], bufs[3], ALU.add)

                    hold = TT[:, B_DQ:B_DQ + 4, :].rearrange("p b n -> p (b n)")
                    for t in (1, 2):
                        step(rotate(proj[:, t, DQ:DQ + 1024].rearrange("p (g n) -> p g n", g=16),
                                    proj[:, t, DQ:DQ + 1024].rearrange("p (g n) -> p g n", g=16), t, 16, 32, K_C32, K_S32))
                        sync()
                        step(rotate(proj[:, t, KR:KR + 32].rearrange("p (g n) -> p g n", g=1),
                                    proj[:, t, KR:KR + 32].rearrange("p (g n) -> p g n", g=1), t, 1, 16, K_C16, K_S16))
                        sync()
                    dve.sem_inc(sems["norms_ready"], 1)
                    for i in range(2):
                        q1 = rows[:, R_LAM + 128 * i:R_LAM + 128 * i + 64]
                        k1 = rows[:, R_LAM + 128 * i + 64:R_LAM + 128 * i + 128]
                        step(nc.vector.tensor_tensor(q1, q1, k1, ALU.mult))
                    sync()
                    step(nc.vector.tensor_reduce(stat[:, 46:48], rows[:, R_LAM:R_LAM + 256].rearrange("p (i n) -> p i n", i=2)[:, :, 0:64],
                                                 AX.X, ALU.add))
                    sync()
                    dve.sem_inc(sems["lam_in"], 1)
                    dve.wait_ge(sems["lam_out"], 1)
                    link(nc.vector.tensor_tensor(stat[:, 50:51], stat[:, 49:50], stat[:, 48:49], ALU.subtract))
                    link(nc.vector.tensor_tensor(stat[:, 51:52], stat[:, 50:51], cols[:, C_LI:C_LI + 1], ALU.subtract))
                    step(nc.vector.tensor_scalar(rows[:, R_DG:R_DG + P], rows[:, R_DG:R_DG + P], cols[:, C_LI + 1:C_LI + 2], None, ALU.mult))
                    neglam = stat[:, 51:52]
                    for t in range(NT):
                        full(dve, ("sgu", t))
                        for g in range(4):
                            u = proj[:, t, AU + 64 * g:AU + 64 * (g + 1)]
                            last = nc.vector.scalar_tensor_tensor(out=u, in0=bank(("sgu", t))[:, 64 * g:64 * (g + 1)],
                                                                  scalar=cols[:, C_SB + g:C_SB + g + 1], in1=u,
                                                                  op0=ALU.add, op1=ALU.mult)
                        taken(last)
                    for t in range(4):
                        name = ("tt", t, 0)
                        full(dve, name)
                        if t < NT:
                            for k in range(2):
                                nc.vector.tensor_scalar(TT[:, k, t * P:(t + 1) * P], bank(name)[:, k * P:(k + 1) * P],
                                                        cols[:, C_QG + k:C_QG + k + 1], None, ALU.mult)
                        taken(nc.vector.tensor_copy(TT[:, 2, t * P:(t + 1) * P], bank(name)[:, 2 * P:3 * P]))
                    for b in range(4):
                        src = spread((cache[:, C_KR:C_KR + 32] if b == NT else proj[:, b, KR:KR + 32]).unsqueeze(1), 1, HEADS)
                        step(nc.vector.tensor_copy(KB[:, b, :, NOPE:MQK], src))
                    sync()
                    dve.sem_inc(sems["kb_ready"], 1)
                    hold = nbs.rearrange("p r n -> p (r n)")
                    for t in range(NT):
                        full(dve, ("mq", t))
                        src = bank(("mq", t))[:, 0:384].rearrange("p (h n) -> p h n", h=HEADS)
                        dst = MQ[:, t, :].rearrange("p (h n) -> p h n", h=HEADS)
                        if t == 0:
                            taken(nc.vector.tensor_copy(dst, src))
                        else:
                            sync()
                            step(nc.vector.tensor_copy(dst[:, :, 0:NOPE], src[:, :, 0:NOPE]))
                            taken(rotate(dst[:, :, NOPE:MQK], src[:, :, NOPE:MQK], t, HEADS, 16, K_C16, K_S16))
                            evacuated(dve, ("mq", t))
                    for t in range(NT):
                        full(dve, ("mqt", t))
                        taken(nc.vector.tensor_copy(MQT[0:MQK, :, t * P:(t + 1) * P],
                                                    bank(("mqt", t))[0:MQK, :].rearrange("p (h n) -> p h n", h=HEADS)))

                    negmax = sems["negmax_ready"]
                    def branch_item(it):
                        b, n = it[1:]
                        evacuated(dve, ("gate", b, n))
                        link(nc.vector.reciprocal(sg[:, n % 4, :], sg[:, n % 4, :]))
                        full(dve, it)
                        dst = mergedT[:, n, :] if b == 0 else sg[:, n % 4, :]
                        taken(nc.vector.tensor_tensor(dst, bank(it)[:, 0:NTOK], sg[:, n % 4, :], ALU.mult))
                        if b:
                            evacuated(dve, it)
                            nc.vector.tensor_tensor(mergedT[:, n, :], mergedT[:, n, :], sg[:, n % 4, :], ALU.add)\
                                .then_inc(sems["merge_done"], 1)

                    for it in middle_order():
                        if it[0] in ("mod", "modt"):
                            mod_item(it)
                            continue
                        if it[0] == "br":
                            branch_item(it)
                            continue
                        if it[0] in ("ot", "gate"):
                            continue
                        w = it[1]
                        t, kind, h = HEAD_LIST[w]
                        nk = P * len(key_blocks(t))
                        if it[0] == "s":
                            r = ROW_OF[(w, it[2])]
                            full(dve, it)
                            nm = stat[:, 64 + r:65 + r]
                            if kind == "C" and t:
                                c = sum(1 for q_ in HEAD_LIST[:w] if q_[1] == "C" and q_[0])
                                if c >= 2:
                                    dve.wait_ge(sems["probs_ready"], ROW_OF[(HEAD_LIST.index((1 + (c - 2) // 4, "C", (c - 2) % 4)), 0)] + 1)
                                step(nc.vector.scalar_tensor_tensor(out=nbs[:, c % 2, 0:256], in0=bank(it)[:, 0:256], scalar=NA_D ** -0.5,
                                                                    in1=bias[:, t - 1, h, :], op0=ALU.mult, op1=ALU.add))
                                taken(nc.vector.tensor_scalar(nbs[:, c % 2, 256:384], bank(it)[:, 256:384], NA_D ** -0.5, None, ALU.mult))
                                evacuated(dve, it)
                                nc.vector.tensor_reduce(nm, nbs[:, c % 2, :], AX.X, ALU.max, negate=True).then_inc(negmax, 1)
                            else:
                                link(nc.vector.tensor_reduce(nm, bank(it)[:, 0:nk], AX.X, ALU.max, negate=True))
                                nc.vector.tensor_scalar(nm, nm, (MQK if kind == "B" else 64) ** -0.5, None, ALU.mult).then_inc(negmax, 1)
                        elif it[0] == "pt":
                            r = ROW_OF[(w, 0)]
                            nr = 2 if kind == "D" else 1
                            dve.wait_ge(sems["probs_ready"], r + nr)
                            rr = stat[:, 112 + r:112 + r + nr]
                            link(nc.vector.reciprocal(rr, rr))
                            if kind == "D":
                                link(nc.vector.tensor_tensor(stat[:, 113 + r:114 + r], stat[:, 113 + r:114 + r], neglam, ALU.mult))
                                p1, p2 = PB[:, r % P_BUFS, 0:nk], PB[:, (r + 1) % P_BUFS, 0:nk]
                                link(nc.vector.tensor_scalar(p2, p2, stat[:, 113 + r:114 + r], None, ALU.mult))
                                nc.vector.scalar_tensor_tensor(out=p1, in0=p1, scalar=stat[:, 112 + r:113 + r], in1=p2,
                                                               op0=ALU.mult, op1=ALU.add).then_inc(sems["weights_ready"], 1)
                        else:
                            r = ROW_OF[(w, 0)]
                            full(dve, it)
                            if w == 0:
                                dve.wait_ge(sems["stored"], 16 * 6)
                            if kind == "D":
                                taken(nc.vector.tensor_copy(proj[:, t, OUT_D + P * h:OUT_D + P * (h + 1)], bank(it)[:, 0:P]))
                            else:
                                c = (OUT_B if kind == "B" else OUT_C) + 64 * h
                                taken(nc.vector.tensor_scalar(proj[:, t, c:c + 64], bank(it)[:, 0:64], stat[:, 112 + r:113 + r], None, ALU.mult))
                    evacuated(dve, ("o", len(HEAD_LIST) - 1))
                    full(dve, ("o", len(HEAD_LIST) - 1))
                    for t in range(NT):
                        for h in range(HEADS):
                            n = HEADS * t + h
                            od = proj[:, t, OUT_D + P * h:OUT_D + P * (h + 1)]
                            step(nc.vector.tensor_tensor_reduce(TT[:, n, 0:P], od, od, 1.0, 0.0, ALU.mult, ALU.add, stat[:, n:n + 1]))
                    roots(NT * HEADS)
                    for t in range(NT):
                        for h in range(HEADS):
                            n = HEADS * t + h
                            od = proj[:, t, OUT_D + P * h:OUT_D + P * (h + 1)]
                            step(nc.vector.scalar_tensor_tensor(out=od, in0=od, scalar=stat[:, 32 + n:33 + n], in1=rows[:, R_DG:R_DG + P],
                                                                op0=ALU.mult, op1=ALU.mult))
                    sync()
                    dve.sem_inc(sems["outs_ready"], 1)
                    for it in branch_items(3):
                        if it[0] == "br":
                            branch_item(it)
                    dve.wait_ge(sems["merge_done"], 3 * KD)
                    dve.sem_inc(sems["merged_ready"], 1)
                    diagonals((0, 1))

                    def residual(t, j, src, gain):
                        xs = x[:, t, 512 * j:512 * (j + 1)]
                        tb = tmp if gain < 2 else y[:, 1, 512 * j:512 * (j + 1)]
                        first = nc.vector.tensor_tensor(tb, src, gains[:, gain % 2, 512 * j:512 * (j + 1)], ALU.mult)
                        return first, (lambda: nc.vector.scalar_tensor_tensor(out=xs, in0=xs, scalar=ALPHA, in1=tb,
                                                                              op0=ALU.mult, op1=ALU.add))

                    all_evacuated(dve, [("gb", i, q) for i in (0, 1) for q in range(2)])
                    for j in range(2):
                        for t in range(NT):
                            full(dve, ("mix", j, t))
                            first, second = residual(t, j, bank(("mix", j, t)), cond[t])
                            taken(first)
                            evacuated(dve, ("mix", j, t))
                            link(second())

                    diagonals((2, 3))

                    def affine(ts, ready):
                        for t in ts:
                            step(nc.vector.tensor_tensor(x[:, t, :], x[:, t, :], lnrows[:, 0:D], ALU.mult))
                        sync()
                        for t in ts:
                            ins = nc.vector.tensor_tensor(x[:, t, :], x[:, t, :], lnrows[:, D:2 * D], ALU.add)
                            if ready is None:
                                step(ins)
                            else:
                                ins.then_inc(ready, 1)

                    def layer_norm(ts):
                        for i, t in enumerate(ts):
                            mean_var(i, x[:, t, :], D)
                        roots(len(ts))
                        for i, t in enumerate(ts):
                            step(nc.vector.tensor_scalar(x[:, t, :], x[:, t, :], bn[:, 36 + 2 * i:37 + 2 * i], stat[:, 32 + i:33 + i],
                                                         ALU.subtract, ALU.mult))
                        sync()

                    layer_norm(range(NT))
                    dve.wait_ge(loaded, 80)
                    affine(range(NT), None)
                    sync()
                    dve.sem_inc(sems["ln1_done"], 1)
                    for t in range(NT):
                        mean_var(t, x[:, t, :], D)
                    roots(NT)
                    normalised(xn2, sems["xn_ready"])
                    for t in range(NT):
                        shift_scale("h2T", t, 24, 32)
                    for t in range(NT):
                        full(dve, ("h2", t, 1))
                        taken(nc.vector.tensor_copy(h2[:, t, 512:1024], bank(("h2", t, 1))))
                    for c in range(1, 16, 2):
                        full(dve, ("pq", c))
                        taken(nc.vector.tensor_copy(qT[:, c, :], bank(("pq", c))[:, 0:NTOK]))
                    for t in range(NT):
                        for q in (1, 3):
                            full(dve, ("ps", t, q))
                            taken(nc.vector.tensor_copy(S[:, t, 4 * q:4 * q + 4, :],
                                                        bank(("ps", t, q)).rearrange("p (c n) -> p c n", n=P)))

                    def top16(n, src, vals, idxs):
                        for c in range(n):
                            step(nc.vector.max(vals(c)[:, 0:8], src(c)))
                        sync()
                        for c in range(n):
                            step(nc.vector.max_index(idxs(c)[:, 0:8], vals(c)[:, 0:8], src(c)))
                        sync()
                        for c in range(n):
                            step(nc.vector.match_replace(src(c), vals(c)[:, 0:8], src(c), LOWEST))
                        sync()
                        for c in range(n):
                            step(nc.vector.max(vals(c)[:, 8:16], src(c)))
                        sync()
                        for c in range(n):
                            step(nc.vector.max_index(idxs(c)[:, 8:16], vals(c)[:, 8:16], src(c)))
                        sync()

                    for t in range(NT):
                        all_evacuated(dve, [("ps", t, q) for q in range(4)])
                        top16(16, lambda c: S[:, t, c, :], lambda c: v16[:, c, :], lambda c: i16[:, c, :])
                        step(nc.vector.tensor_copy(i16f, i16))
                        vv = v16.rearrange("p (h m) k -> p h m k", m=2)
                        for h in range(PH):
                            step(nc.vector.tensor_tensor(cand[:, 256 * h:256 * (h + 1)].rearrange("p (a b) -> p a b", a=16),
                                                         spread(vv[:, h, 0, :].unsqueeze(2), 2, 16),
                                                         spread(vv[:, h, 1, :].unsqueeze(1), 1, 16), ALU.add))
                        sync()
                        bv = bi[:, 0, :].rearrange("p (h k) -> p h k", h=PH)
                        top16(PH, lambda h: cand[:, 256 * h:256 * (h + 1)], lambda h: best[:, h, :], lambda h: bv[:, h, :])
                        gt = gates[:, t * KSEL:(t + 1) * KSEL].rearrange("p (h k) -> p h k", h=PH)
                        nc.vector.tensor_tensor(gt, best, spread(best[:, :, 0:1], 2, TOPK), ALU.subtract)\
                            .then_inc(sems["best_ready"], 1)
                        step(nc.vector.tensor_scalar(bi[:, 1, :], bi[:, 0, :], 4, None, ALU.logical_shift_right))
                        sync()
                        step(nc.vector.tensor_copy(selA, bi[:, 1, :]))
                        sync()
                        step(nc.vector.tensor_scalar(bi[:, 1, :], bi[:, 0, :], 15, None, ALU.bitwise_and))
                        sync()
                        step(nc.vector.tensor_copy(selB, bi[:, 1, :]))
                        sync()
                        iota = spread(consts[:, K_IO:K_IO + 16].unsqueeze(1), 1, KSEL)
                        ii = i16f.rearrange("p (h m) k -> p h m k", m=2)
                        for m, sel in ((0, selA), (1, selB)):
                            e3 = eq.rearrange("p (n k) -> p n k", n=KSEL)
                            step(nc.vector.tensor_tensor(e3, spread(sel.unsqueeze(2), 2, 16), iota, ALU.is_equal))
                            sync()
                            for h in range(PH):
                                eh = eq[:, 256 * h:256 * (h + 1)].rearrange("p (n k) -> p n k", n=TOPK)
                                step(nc.vector.tensor_tensor(eh, eh, spread(ii[:, h, m, :].unsqueeze(1), 1, TOPK), ALU.mult))
                            sync()
                            step(nc.vector.tensor_reduce(sel, e3, AX.X, ALU.add))
                            sync()
                        step(nc.vector.scalar_tensor_tensor(out=selA, in0=selA, scalar=float(NKEYS), in1=selB, op0=ALU.mult, op1=ALU.add))
                        sync()
                        step(nc.vector.tensor_scalar(selA, selA, cols[:, C_LO:C_LO + 1], None, ALU.add))
                        sync()
                        step(nc.vector.tensor_copy(experts[:, t * KSEL:(t + 1) * KSEL], selA))
                        dve.wait_ge(sems["gate_exp"], t + 1)
                        step(nc.vector.tensor_reduce(stat[:, 0:PH], gt, AX.X, ALU.add))
                        sync()
                        step(nc.vector.reciprocal(stat[:, 32:32 + PH], stat[:, 0:PH]))
                        sync()
                        step(nc.vector.tensor_tensor(gt, gt, spread(stat[:, 32:32 + PH].unsqueeze(2), 2, TOPK), ALU.mult))
                        sync()

                    for g in range(2):
                        nc.vector.tensor_copy(exslot[:, GROUP * g:GROUP * (g + 1)], experts[:, GROUP * g:GROUP * (g + 1)])\
                            .then_inc(sems["experts_ready"], 1)
                    per_layer = 16 * NT * STEPS
                    acc_done = sems["acc_done"]
                    dve.sem_inc(acc_done, 10)
                    for t in range(NT):
                        step(nc.vector.memset(y.rearrange("p r d -> p (r d)"), 0.0))
                        sync()
                        with dve.Fori(0, STEPS) as i:
                            for g in range(2):
                                for j in range(GROUP * g, GROUP * (g + 1)):
                                    dve.wait_ge(gotU[j], l * per_layer + i * 16 + 16 * (STEPS * t + 1))
                                    nc.vector.tensor_tensor_reduce(ringU[:, j, :], ringU[:, j, :], h2[:, t, :], 1.0, 0.0,
                                                                   ALU.mult, ALU.add, dots[:, j:j + 1]).then_inc(sems["dots_ready"], 1)
                            for g in range(2):
                                dve.wait_ge(sems["gelu_ready"], i * 2 + (2 * STEPS * t + g + 1))
                                nc.vector.tensor_tensor(wts[:, GROUP * g:GROUP * (g + 1)], acts[:, GROUP * g:GROUP * (g + 1)],
                                                        gates[:, bass.ds(i * 2 * GROUP + (t * KSEL + GROUP * g), GROUP)],
                                                        ALU.mult).then_inc(acc_done, 1)
                                for j in range(GROUP * g, GROUP * (g + 1)):
                                    dve.wait_ge(gotV[j], l * per_layer + i * 16 + 16 * (STEPS * t + 1))
                                nc.vector.tensor_copy(exslot[:, GROUP * g:GROUP * (g + 1)],
                                                      experts[:, bass.ds(i * 2 * GROUP + (t * KSEL + 2 * GROUP + GROUP * g), GROUP)])\
                                    .then_inc(sems["experts_ready"], 1)
                                for j in range(GROUP * g, GROUP * (g + 1)):
                                    dve.wait_ge(acc_done, i * 10 + (10 * STEPS * t + 10 + 5 * g + 1 + j - GROUP * g))
                                    nc.vector.scalar_tensor_tensor(out=y[:, 0, :], in0=ringV[:, j, :], scalar=wts[:, j:j + 1],
                                                                   in1=y[:, 0, :], op0=ALU.mult, op1=ALU.add).then_inc(acc_done, 1)
                        dve.wait_ge(acc_done, 10 * STEPS * (t + 1) + 10)
                        all_evacuated(dve, [("gb", i, q) for i in (2, 3) for q in range(2)])
                        for j in range(2):
                            first, second = residual(t, j, y[:, 0, 512 * j:512 * (j + 1)], 2 + cond[t])
                            link(first)
                            link(second())
                        layer_norm([t])
                        dve.wait_ge(loaded, 96)
                        affine([t], sems["x_ready"])
                    dve.wait_ge(sems["x_ready"], NT)

                @block.gpsimd
                def _(pool):
                    for t in range(NT):
                        with pool.Fori(0, STEPS) as i:
                            for g in range(2):
                                for ring, table, got in ((ringU, "peer_u", gotU), (ringV, "peer_v", gotV)):
                                    if table == "peer_u":
                                        pool.wait_ge(sems["experts_ready"], i * 2 + (2 * STEPS * t + g + 1))
                                    else:
                                        pool.wait_ge(sems["acc_done"], i * 10 + (10 * STEPS * t + 5 * (g + 1)))
                                    pool.sem_inc(gather_gate, 1)
                                    for j in range(GROUP * g, GROUP * (g + 1)):
                                        pool.indirect_dma_start(ring[:, j, :], None, a[table],
                                                                bass.IndirectOffsetOnAxis(ap=exslot[:, j:j + 1], axis=0))\
                                            .then_inc(got[j], 16)
            nc.all_engine_barrier()
            for s in list(sems.values()) + w_ready:
                nc.gpsimd.sem_clear(s)
            nc.all_engine_barrier()


_OUTS = [(1, 128, 1024), (1, 256, 1024), (2, 128, 128), (2, 128, 32), (2, 128, 256), (2, 128, 256), (2, 128, 512), (2, 128, 512)]
_SHAPES = [(1, 128, 1024), (1, 256, 1024), (1, 2, 128, 128), (1, 2, 128, 32), (1, 2, 128, 4, 64), (1, 2, 128, 4, 64),
           (1, 2, 128, 4, 128), (1, 2, 128, 4, 128)]


def shape_constants():
    c = np.zeros((P, K_W), np.float32)
    c[:, K_ID:K_ID + P] = np.eye(P)
    c[:, K_ON:K_ON + P] = 1
    col = np.arange(GRID_W)
    start = np.clip(col - 8, 0, GRID_W - 16)
    inside = (col[None] >= start[:, None]) & (col[None] < start[:, None] + 16)
    c[:, K_MA:K_MA + 256] = np.tile(np.where(inside, 0.0, NEG_BIG), (2, 4))
    c[:, K_IO:K_IO + 16] = np.arange(16)
    tok = np.arange(256)
    for half, kc, ks in ((16, K_C16, K_S16), (32, K_C32, K_S32)):
        nf = half // 2
        inv = (np.float32(10000.0) ** (-np.arange(nf, dtype=np.float32) / nf)).astype(np.float32)
        row, cc = (tok // GRID_W).astype(np.float32), (tok % GRID_W).astype(np.float32)
        ang = np.concatenate([row[:, None] * inv, cc[:, None] * inv], 1).astype(np.float32)
        for t in range(2):
            c[:, kc + t * half:kc + (t + 1) * half] = np.cos(ang[t * P:(t + 1) * P])
            c[:, ks + t * half:ks + (t + 1) * half] = np.sin(ang[t * P:(t + 1) * P])
    return c


def layouts(v):
    cat = np.concatenate
    lam = cat([v[n] for n in ("diff_lambda_q1", "diff_lambda_k1", "diff_lambda_q2", "diff_lambda_k2")], 1)
    rows = cat([v["sgu_norm_g"], v["mla_kv_norm_g"], v["diff_norm_g"], lam, v["ln1_g"], v["ln1_b"], v["ln2_g"], v["ln2_b"]], 1)
    colT = lambda w, n: w.reshape(DEPTH, n, P).transpose(0, 2, 1)
    init = [0.8 - 0.6 * math.exp(-0.3 * l) for l in range(DEPTH)]
    fixed = np.zeros((DEPTH, P, 4), np.float32)
    for l in range(DEPTH):
        fixed[l] = [init[l], 1 - init[l], EPS, l * NEXP]
    cols = cat([colT(v["b_mod"], 48), colT(v["b_gate"], 32), v["sgu_b"].transpose(0, 2, 1), colT(v["mla_q_norm_g"], 2), fixed], 2)
    flat = lambda w: w[0].reshape(DEPTH, P, -1)
    cache = cat([flat(v[n]) for n in ("cache_mla_ckv", "cache_mla_krope", "cache_na_k", "cache_na_v", "cache_diff_k", "cache_diff_v")], 2)
    q = np.arange(2 * P)
    r, c = q // GRID_W, q % GRID_W
    dr = r[None, :] - r[:, None] + 7
    dc = np.clip(c[None, :] - c[:, None], -15, 15) + 15
    rpb = v["na_rpb"][:, :, dr, dc].reshape(DEPTH, HEADS, 2, P, 256).transpose(0, 3, 2, 1, 4).reshape(DEPTH, P, -1)
    uq = v["mla_w_uq"].reshape(DEPTH, 2, P, 384).transpose(0, 2, 1, 3).reshape(DEPTH, P, 768)
    sgw = v["sgu_w"].transpose(0, 3, 1, 2).reshape(DEPTH, P, 512)
    small = cat([uq, v["mla_w_ukv"], sgw], 2)
    subT = v["peer_subkeys"].reshape(DEPTH, 16, P, P).transpose(0, 3, 1, 2).reshape(DEPTH, P, 2048)
    cond = np.stack([v["c_ctx"].reshape(KD, P).T, v["c"][0].reshape(KD, P).T], 2)
    out = dict(rows=rows, cols=cols, cache=cache, rpb=rpb, small=small, subT=subT, cond=cond, consts=shape_constants())
    for n in ("x_prompt", "x_sample", "w_mod", "w_in", "w_gate", "w_out", "peer_w_q", "w_branch_a", "w_branch_b", "w_branch_c", "w_branch_d"):
        out[n] = v[n]
    for n in ("peer_u", "peer_v"):
        out[n] = v[n].reshape(DEPTH * NEXP, D)
    return {n: np.ascontiguousarray(w) for n, w in out.items()}


def kernel(**inputs):
    import concourse.bacc as _bacc
    from concourse.bass_utils import run_bass_kernel_spmd as _run

    nc = _bacc.Bacc("TRN2", target_bir_lowering=False, num_devices=1)
    arrays = {f"in_{n}": w for n, w in layouts({k: np.asarray(w) for k, w in inputs.items()}).items()}
    a = {n[3:]: nc.dram_tensor(n, w.shape, F32, kind="ExternalInput").ap() for n, w in arrays.items()}
    outs = [nc.dram_tensor(f"out_{i}", s, F32, kind="ExternalOutput").ap() for i, s in enumerate(_OUTS)]
    build(nc, a, outs)
    r = _run(nc, [arrays], core_ids=[0])
    return tuple(r.results[0][f"out_{i}"].reshape(s) for i, s in enumerate(_SHAPES))
```

```python
from contextlib import ExitStack
import math

import numpy as np
import concourse.bass as bass
from concourse import mybir

F32 = mybir.dt.float32
I32 = mybir.dt.int32
U32 = mybir.dt.uint32
ALU = mybir.AluOpType
ACT = mybir.ActivationFunctionType
AX = mybir.AxisListType

P = 128
D = 1024
KD = D // P
DEPTH = 2
NT = 3
NTOK = NT * P
GRID_W = 64
EPS = 1e-6
ALPHA = (2 * DEPTH) ** 0.25
HEADS = 4
NOPE, ROPE, MV = 64, 32, 64
MQK = NOPE + ROPE
NA_D = 64
DQK, DV = 64, 128
PH, TOPK, NKEYS = 8, 16, 128
NEXP = NKEYS * NKEYS
KSEL = PH * TOPK
GROUP = 4
STEPS = KSEL // (2 * GROUP)
NEG_BIG = -1e30
LOWEST = -3.0e38

IN_W = 3232
AU, AV, CQ, CKV, KR, NQ, NK, NV, DQ, DK, DVO = 0, 256, 512, 768, 896, 928, 1184, 1440, 1696, 2208, 2720
C_CKV, C_KR, C_NK, C_NV, C_DK, C_DV, C_W = 0, 128, 160, 416, 672, 1184, 1696
OUT_A, OUT_B, OUT_C, OUT_D, OUT_W = 0, 256, 512, 768, 1280
R_SG, R_KVG, R_DG, R_LAM, R_L1G, R_L1B, R_L2G, R_L2B, R_W = 0, 256, 384, 512, 768, 1792, 2816, 3840, 4864
C_BM, C_BG, C_SB, C_QG, C_LI, C_LO, COLS = 0, 48, 80, 84, 86, 88, 89
K_ID, K_ON, K_MA, K_IO, K_C16, K_S16, K_C32, K_S32, K_EPS, K_W = 0, 128, 256, 512, 528, 560, 592, 656, 720, 721

W_SLOT = 4 * 512
W_RING = 4

TT_FIRST = [0, 3, 7, 11]
B_NQ, B_NK, B_DQ, B_DK, TT_BLOCKS = 3, 5, 7, 11, 15
TT_SRC = [[CQ, CQ + 128, CKV], [NQ, NQ + 128, NK, NK + 128],
          [DQ + 128 * i for i in range(4)], [DK + 128 * i for i in range(4)]]
TT_CACHE = {0: [(2, C_CKV)], 1: [(2, C_NK), (3, C_NK + 128)], 3: [(i, C_DK + 128 * i) for i in range(4)]}

HEAD_LIST = [(t, kind, h) for kind in "BCD" for t in range(NT) for h in range(HEADS)]
BRANCH_K = [2, 2, 2, 4]
ROWS = [(w, m) for w, (t, kind, h) in enumerate(HEAD_LIST) for m in range(2 if kind == "D" else 1)]
ROW_OF = {wm: r for r, wm in enumerate(ROWS)}
P_BUFS = 6
HEAD_LAG = 2


def key_blocks(t):
    return [0] if t == 0 else [1, 2, 3]


def spread(ap, axis, n):
    shape = list(ap.shape)
    shape[axis] = n
    return ap.broadcast_to(shape)


def head_step(w):
    scores = [("s", w, m) for m in range(2 if HEAD_LIST[w][1] == "D" else 1)] if w < len(HEAD_LIST) else []
    pt = [("pt", w - HEAD_LAG)] if 0 <= w - HEAD_LAG < len(HEAD_LIST) else []
    o = [("o", w - HEAD_LAG - 1)] if w > HEAD_LAG else []
    return scores, pt + o


GATES_FIRST = [("gate", 0, n) for n in range(4)]


def branch_items(b):
    ot = [("ot", b, k) for k in range(BRANCH_K[b])]
    out = []
    for half in range(2):
        gates = [("gate", b, 4 * half + n) for n in range(4)]
        products = [("br", b, 4 * half + n) for n in range(4)]
        if half == 0:
            out += {0: ot, 3: gates + ot}.get(b, ot + gates) + products
        else:
            out += gates + products
    if b == 3:
        out[len(out) // 2:len(out) // 2] = [("gb", i, q) for i in (0, 1) for q in range(2)]
    return out


def middle_order():
    per = len(HEAD_LIST) // 3
    for w in range(len(HEAD_LIST) + HEAD_LAG + 1):
        p = min(w // per, 2)
        i = w - p * per
        scores, rest = head_step(w)
        if i == 0:
            wait = HEAD_LAG + 1 if p else 0
            steps = per if p < 2 else per + HEAD_LAG + 1
            late = [x for x in branch_items(p) if x not in GATES_FIRST]
            share = [[] for _ in range(steps)]
            for n, x in enumerate(late):
                share[wait + n * (steps - wait) // len(late)].append(x)
        yield from scores
        yield from share[i]
        yield from rest


MOD_FIRST = [("mod", 0)] + [x for j in range(1, 4) for x in (("mod", j), ("modt", j - 1))] + [("modt", 3)]


PROJ_ORDER = []
for _j in range(7):
    PROJ_ORDER += [("proj", _j, t) for t in range(NT)]
    if _j < 6:
        PROJ_ORDER += [("macc", 4 + _j, 0), ("macc", 4 + _j, 1), ("modt", 4 + _j)]

MOD_LAST = [[("mod", 10)], [("mod", 11), ("modt", 10)], [("modt", 11)]]


def plan_items():
    out = [(x, "v") for x in MOD_FIRST]
    out += [(("hT", t, q), "av"[q]) for t in range(NT) for q in range(2)]
    out += [(x, "v" if x[0] == "modt" else "a") for x in PROJ_ORDER if x[0] != "macc"]
    out += [(x, "a") for x in GATES_FIRST]
    out += [(("sgu", t), "v") for t in range(NT)]
    out += [(("tt", t, g), "v" if g == 0 else "a") for t in range(4) for g in range(4) if t < NT or g in TT_CACHE]
    out += [(("mq", t), "v") for t in range(NT)]
    out += [(("kv", b), "a") for b in range(4)]
    out += [(("mqt", t), "v") for t in range(NT)]
    out += [(("mkt", b), "a") for b in range(4)]
    for it in list(middle_order()) + branch_items(3):
        if it[0] == "s":
            t, kind, h = HEAD_LIST[it[1]]
            out.append((it, "v" if kind == "C" and t else "p"))
        else:
            out.append((it, "v" if it[0] in ("o", "br", "mod", "modt") else "a"))
    out += [(("mix", j, t), "v") for j in range(2) for t in range(NT)]
    for t in range(NT):
        out += [(("h2T", t, q), "av"[q]) for q in range(2)] + [(x, "a") for x in MOD_LAST[t]]
    out += [(("h2", t, q), "av"[q]) for t in range(NT) for q in range(2)]
    out += [(("gb", i, q), "a") for i in (2, 3) for q in range(2)]
    out += [(("pq", c), "av"[c % 2]) for c in range(16)]
    out += [(("ps", t, q), "av"[q % 2]) for t in range(NT) for q in range(4)]
    return out


ITEMS = plan_items()
INDEX = {name: n for n, (name, _) in enumerate(ITEMS)}
EVAC_BY = [who for _, who in ITEMS]
EVAC_COUNT = [sum(w == who for w in EVAC_BY[:n + 1]) for n, who in enumerate(EVAC_BY)]

TOPK_PIECES = 15
BEST_PIECE = 11
STEP_PIECES = [[(1 + n // TOPK_PIECES, n % TOPK_PIECES) for n in range(2 * TOPK_PIECES)
                if n * STEPS // (2 * TOPK_PIECES) == i] for i in range(STEPS)]

SLOTS = []
for _name in (MOD_FIRST + PROJ_ORDER + [x for x, _ in ITEMS[INDEX[("modt", 9)] + 1:INDEX[("mix", 0, 0)]]]):
    if _name[0] == "mod":
        SLOTS += [("mod", _name[1], k) for k in range(2)]
    elif _name[0] == "macc":
        SLOTS += [("mod", _name[1], _name[2])]
    elif _name[0] == "proj" and _name[2] == 0:
        SLOTS += [("in", _name[1], k) for k in range(2)]
    elif _name == ("sgu", 0):
        SLOTS += [("small",)]
    elif _name[0] == "gate" and _name[2] % 4 == 0:
        SLOTS += [("gate", _name[1], _name[2] // 4, k) for k in range(2)]
    elif _name[0] == "br" and _name[2] % 4 == 0:
        SLOTS += [("branch", _name[1], _name[2] // 4)]
SLOTS += [("out", j, k) for j in range(2) for k in range(2)]
SLOTS += [("mod", j, k) for j in (10, 11) for k in range(2)]
SLOTS += [("pq", j, k) for j in range(4) for k in range(2)] + [("sub",)]
SLOT_OF = {s: n for n, s in enumerate(SLOTS)}
def last_item(s):
    return {"mod": lambda: ("modt" if 4 <= s[1] < 10 else "mod", s[1]), "in": lambda: ("proj", s[1], NT - 1), "small": lambda: ("kv", 3),
            "gate": lambda: ("gate", s[1], 4 * s[2] + 3), "branch": lambda: ("br", s[1], 4 * s[2] + 3),
            "out": lambda: ("mix", s[1], NT - 1), "pq": lambda: ("pq", 4 * s[1] + 3), "sub": lambda: ("ps", NT - 1, 3)}[s[0]]()


S_UQ, S_UKV, S_SW, S_W = 0, 768, 1280, 1792


def build(nc, a, outs):
    with ExitStack() as ctx:
        def sb(name, words, dt=F32):
            return ctx.enter_context(nc.sbuf_tensor(name, [P, words], dt))

        def sem(name):
            s = ctx.enter_context(nc.semaphore(name))
            return s

        x = sb("x", NT * D)[:, :].rearrange("p (t d) -> p t d", t=NT)
        hT = sb("hT", KD * NTOK)[:, :].rearrange("p (k n) -> p k n", k=KD)
        rows = sb("rows", R_L1G)
        bias = sb("bias", 2 * HEADS * 256)[:, :].rearrange("p (t h n) -> p t h n", t=2, h=HEADS)
        cols = sb("cols", COLS)
        consts = sb("consts", K_W)
        modacc = sb("modacc", 1024)[:, :].rearrange("p (c n) -> p c n", c=2)
        modrow = diag = modacc[:, 0, :]
        modrow2 = modacc[:, 1, :]
        modT = sb("modT", 96)[:, :].rearrange("p (n c) -> p n c", c=2)
        silu = sb("silu", 16)[:, :].rearrange("p (k c) -> p k c", c=2)
        wring = sb("wring", W_RING * W_SLOT)
        stat = sb("stat", 256)
        psum = ctx.enter_context(nc.psum_tensor("psum", [P, 8, 512], F32))
        ident = consts[:, K_ID:K_ID + P]
        ones = consts[:, K_ON:K_ON + P]

        WORK = 31744
        work = sb("work", WORK)

        def region(at, words):
            assert at + words <= WORK
            return work[:, at:at + words]

        proj = region(0, NT * IN_W).rearrange("p (t n) -> p t n", t=NT)
        TTO = NT * IN_W
        TT = region(TTO, TT_BLOCKS * 512).rearrange("p (b n) -> p b n", b=TT_BLOCKS)
        outT = [region(TTO + at, n * NTOK).rearrange("p (k n) -> p k n", k=n)
                for at, n in ((0, 2), (2 * NTOK, 2), (B_NQ * 512, 2), (B_DQ * 512, 4))]
        o = TTO + TT_BLOCKS * 512
        VB = region(o, 4 * 256).rearrange("p (b n) -> p b n", b=4)
        o += 4 * 256
        MQT = region(o, HEADS * NTOK).rearrange("p (h n) -> p h n", h=HEADS)
        o += HEADS * NTOK
        MKT = region(o, HEADS * 512).rearrange("p (h n) -> p h n", h=HEADS)
        o += HEADS * 512
        cache = region(o, C_W)
        o += C_W
        MQ = region(o, NT * 384).rearrange("p (t n) -> p t n", t=NT)
        KB = region(o + NT * 384, 4 * 384).rearrange("p (b h n) -> p b h n", b=4, h=HEADS)
        PB = region(o, P_BUFS * 384).rearrange("p (r n) -> p r n", r=P_BUFS)
        o += (NT + 4) * 384
        PT = region(o, 2 * 384).rearrange("p (r b n) -> p r b n", r=2, b=3)
        o += 2 * 384
        xn = region(o, NT * D).rearrange("p (t d) -> p t d", t=NT)
        mergedT = region(o, KD * NTOK).rearrange("p (k n) -> p k n", k=KD)
        o += KD * NTOK
        sg = region(o, 4 * NTOK).rearrange("p (n q) -> p n q", n=4)
        tmp = region(o, 512)
        nbs = sb("nbs", 2 * 384)[:, :].rearrange("p (r n) -> p r n", r=2)

        ringU = region(0, 8 * D).rearrange("p (r d) -> p r d", r=8)
        ringV = region(8 * D, 8 * D).rearrange("p (r d) -> p r d", r=8)
        S = [region(at, 2048).rearrange("p (c n) -> p c n", c=16) for at in (0, WORK - 4096, WORK - 2048)]
        qT = region(8 * D, 16 * NTOK).rearrange("p (c n) -> p c n", c=16)
        o = 16 * D
        h2 = region(o, NT * D).rearrange("p (t d) -> p t d", t=NT)
        o += NT * D
        y = region(o, 2 * D).rearrange("p (r d) -> p r d", r=2)
        o += 2 * D
        spare = [(SLOT_OF[("sub",)] + i) % W_RING * W_SLOT for i in (1, 2, 3)]
        cand, eq = (wring[:, at:at + 2048] for at in spare[:2])
        wdiag = wring[:, spare[2]:spare[2] + 8 * P].rearrange("p (j n) -> p j n", j=8)
        xn2 = region(0, NT * D).rearrange("p (t d) -> p t d", t=NT)
        v16 = region(o, 256).rearrange("p (c k) -> p c k", c=16)
        i16f = region(o + 256, 256).rearrange("p (c k) -> p c k", c=16)
        best = region(o + 512, 128).rearrange("p (h k) -> p h k", h=PH)
        selA = region(o + 640, 128)
        selB = region(o + 768, 128)
        o += 896
        lnrows = region(o, 2 * D)
        gains = region(o + 2 * D, 2 * D).rearrange("p (i d) -> p i d", i=2)
        assert o + 4 * D <= WORK - 4096
        i16 = sb("i16", 256, U32)[:, :].rearrange("p (c k) -> p c k", c=16)
        bi = sb("bi", 256, U32)[:, :].rearrange("p (r n) -> p r n", r=2)
        gates = sb("gates", NT * KSEL)
        experts = sb("experts", NT * KSEL + 8, I32)
        exslot = sb("exslot", 8, I32)
        dots = sb("dots", 8)
        acts = sb("acts", 8)
        wts = sb("wts", 8)

        names = ["loaded", "psum_full", "dve_evac", "act_evac", "dve_step", "ln1_done", "merge_done",
                 "diag_ready", "bias_ready", "half_used", "macc_ready", "sigmoid_exp", "xn_ready", "norms_ready", "kb_ready",
                 "negmax_ready", "probs_ready", "nbs_ready", "weights_ready", "outs_ready", "merged_ready",
                 "h2_ready", "best_ready", "gate_exp", "experts_ready", "dots_ready", "gelu_ready", "stored",
                 "new_ready", "x_ready", "sqin", "sqout", "lam_in", "lam_out", "zeros_ready", "wts_ready", "diags_made", "rows_added", "sum_ready"]
        sems = {n: sem(n) for n in names}
        w_ready = [sem(f"w_ready{i}") for i in range(W_RING)]
        gotU = [sem(f"gotU{i}") for i in range(8)]
        gotV = [sem(f"gotV{i}") for i in range(8)]
        setup_loaded = sem("setup_loaded")
        setup_done = sem("setup_done")
        gather_gate = sem("gather_gate")
        loaded, psum_full, dve_evac, act_evac = (sems[n] for n in names[:4])

        def bank(name):
            return psum[:, INDEX[name] % 8, :]

        def full(eng, name):
            eng.wait_ge(psum_full, INDEX[name] + 1)

        def evacuated(eng, name):
            n = INDEX[name]
            if EVAC_BY[n] == "p":
                eng.wait_ge(sems["probs_ready"], ROW_OF[name[1:]] + 1)
            else:
                eng.wait_ge(dve_evac if EVAC_BY[n] == "v" else act_evac, EVAC_COUNT[n])

        def all_evacuated(eng, names_):
            for who in "va":
                last = [n for n in names_ if EVAC_BY[INDEX[n]] == who]
                if last:
                    evacuated(eng, max(last, key=lambda n: INDEX[n]))

        with nc.Block() as block:
            @block.sync
            def _(sp):
                for t in range(NT):
                    src = a["x_prompt"][0] if t == 0 else a["x_sample"][0, (t - 1) * P:t * P, :]
                    sp.dma_start(x[:, t, :], src).then_inc(setup_loaded, 16)
                sp.dma_start(consts[:, :], a["consts"]).then_inc(setup_loaded, 16)
                sp.dma_start(silu, a["cond"]).then_inc(setup_loaded, 16)
                sp.wait_ge(setup_loaded, 80)

            @block.scalar
            def _(act):
                act.wait_ge(setup_loaded, 80)
                nc.scalar.activation(silu, silu, ACT.Silu).then_inc(setup_done, 1)

            @block.tensor
            def _(pe):
                pe.wait_ge(setup_done, 2)

            @block.vector
            def _(dve):
                nc.vector.memset(experts[:, NT * KSEL:], 0).then_inc(setup_done, 1)
                dve.wait_ge(setup_done, 2)

            @block.gpsimd
            def _(pool):
                pool.wait_ge(setup_done, 2)
        nc.all_engine_barrier()

        per_layer = 16 * NT * STEPS
        with nc.Fori(0, DEPTH) as l:
            with nc.Block() as block:
                @block.sync
                def _(sp):
                    lay = bass.ds(l, 1)
                    def cols_of(name, j, width, k0, nk):
                        w = a[name][lay].rearrange("a (k p) n -> p (a k) n", p=P)
                        return w[:, k0:k0 + nk, j:j + width]

                    for n, s in enumerate(SLOTS):
                        if n >= W_RING:
                            before = SLOTS[n - W_RING]
                            if before[0] == "in" and before[2] == 0:
                                sp.wait_ge(sems["half_used"], before[1] + 1)
                            else:
                                full(sp, last_item(before))
                        base = (n % W_RING) * W_SLOT
                        ready = w_ready[n % W_RING]
                        kind = s[0]
                        if kind == "small":
                            sp.dma_start(wring[:, base:base + S_W],
                                         a["small"][lay].rearrange("a p n -> p (a n)")).then_inc(ready, 16)
                        elif kind == "sub":
                            sp.dma_start(wring[:, base:base + W_SLOT],
                                         a["subT"][lay].rearrange("a p n -> p (a n)")).then_inc(ready, 16)
                        elif kind == "branch":
                            dst = wring[:, base:base + W_SLOT].rearrange("p (k n) -> p k n", k=4)[:, 0:BRANCH_K[s[1]], :]
                            sp.dma_start(dst, cols_of("w_branch_" + "abcd"[s[1]], 512 * s[2], 512, 0, BRANCH_K[s[1]])).then_inc(ready, 16)
                        else:
                            name = {"mod": "w_mod", "in": "w_in", "gate": "w_gate", "out": "w_out", "pq": "peer_w_q"}[kind]
                            col = (s[1] * 2 + s[2]) * 512 if kind == "gate" else s[1] * 512
                            width = min(512, IN_W - col) if kind == "in" else 512
                            dst = wring[:, base:base + W_SLOT].rearrange("p (k n) -> p k n", k=4)[:, :, 0:width]
                            sp.dma_start(dst, cols_of(name, col, width, 4 * s[-1], 4)).then_inc(ready, 16)
                    sp.wait_ge(sems["ln1_done"], 1)
                    sp.dma_start(lnrows, a["rows"][lay, R_L2G:R_W].broadcast_to([P, 2 * D])).then_inc(loaded, 16)
                    for t in range(NT):
                        sp.wait_ge(sems["x_ready"], t + 1)
                        dst = outs[0][0] if t == 0 else outs[1][0, (t - 1) * P:t * P, :]
                        sp.dma_start(dst, x[:, t, :]).then_inc(sems["stored"], 16)
                    sp.wait_ge(sems["stored"], 16 * (NT + 6))

                @block.tensor
                def _(pe):
                    def slot(s, k):
                        n = SLOT_OF[s]
                        pe.wait_ge(w_ready[n % W_RING], 16 * (n // W_RING + 1))
                        base = (n % W_RING) * W_SLOT
                        return wring[:, base:base + W_SLOT].rearrange("p (k n) -> p k n", k=k)

                    def room(name):
                        if INDEX[name] >= 8:
                            evacuated(pe, ITEMS[INDEX[name] - 8][0])
                        return bank(name)

                    def mod_item(it):
                        j = it[1]
                        out = room(it)
                        if it[0] == "mod":
                            w = [slot(("mod", j, k), 4) for k in range(2)]
                            for k in range(KD):
                                last = nc.tensor.matmul(out[0:2, :], silu[:, k, :], w[k // 4][:, k % 4, :],
                                                        start=(k == 0), stop=(k == KD - 1))
                        else:
                            if j < 4 or j >= 10:
                                evacuated(pe, ("mod", j))
                            else:
                                pe.wait_ge(sems["macc_ready"], j - 3)
                            for n in range(4):
                                if j < 4 or j >= 10:
                                    last = nc.tensor.transpose(out[:, 2 * n:2 * n + 2], (modrow2 if j == 11 else modrow)[0:2, n * P:(n + 1) * P], ident[0:2, 0:2])
                                else:
                                    for c in range(2):
                                        last = nc.tensor.matmul(out[:, 2 * n + c:2 * n + c + 1], modacc[:, c, n * P:(n + 1) * P],
                                                                ones[:, 0:1], start=True, stop=True)
                        last.then_inc(psum_full, 1)

                    for it in MOD_FIRST:
                        mod_item(it)

                    def spread_gains(i, q):
                        out = room(("gb", i, q))
                        pe.wait_ge(sems["diag_ready"], 2 * i + q + 1)
                        nc.tensor.matmul(out, ones, diag[:, :], start=True, stop=True).then_inc(psum_full, 1)

                    def transposed(kind, src, ready, count, ts):
                        for t in ts:
                            pe.wait_ge(ready, count + t)
                            for q in range(2):
                                out = room((kind, t, q))
                                for k in range(4):
                                    last = nc.tensor.transpose(out[:, k * P:(k + 1) * P],
                                                               src[:, t, (4 * q + k) * P:(4 * q + k + 1) * P], ident)
                                last.then_inc(psum_full, 1)

                    transposed("hT", xn, sems["xn_ready"], 1, range(NT))

                    all_evacuated(pe, [("hT", t, q) for t in range(NT) for q in range(2)])
                    for it in PROJ_ORDER:
                        if it[0] == "modt":
                            mod_item(it)
                        if it[0] != "proj" or it[2]:
                            continue
                        j = it[1]
                        width = min(512, IN_W - 512 * j)
                        outb = [room(("proj", j, t)) for t in range(NT)]
                        for half in range(2):
                            w = slot(("in", j, half), 4)
                            for t in range(NT):
                                for k in range(4):
                                    kk = 4 * half + k
                                    last = nc.tensor.matmul(outb[t][:, 0:width], hT[:, kk, t * P:(t + 1) * P],
                                                            w[:, k, 0:width], start=(kk == 0), stop=(kk == KD - 1))
                                if half == 1:
                                    last.then_inc(psum_full, 1)
                            if half == 0:
                                last.then_inc(sems["half_used"], 1)

                    def branch_item(it):
                        b, n = it[1:]
                        if it[0] == "gb":
                            spread_gains(b, n)
                            return
                        out = room(it)
                        if it[0] == "ot":
                            if b in (1, 2):
                                evacuated(pe, ("o", 12 * b - 1))
                            elif b == 3:
                                pe.wait_ge(sems["outs_ready"], 1)
                            else:
                                evacuated(pe, ("sgu", NT - 1))
                            c = [OUT_A, OUT_B, OUT_C, OUT_D][b] + n * P
                            for t in range(NT):
                                last = nc.tensor.transpose(out[:, t * P:(t + 1) * P], proj[:, t, c:c + P], ident)
                        elif it[0] == "gate":
                            w = [slot(("gate", b, n // 4, k), 4) for k in range(2)]
                            for k in range(KD):
                                last = nc.tensor.matmul(out[:, 0:NTOK], w[k // 4][:, k % 4, n % 4 * P:(n % 4 + 1) * P], hT[:, k, :],
                                                        start=(k == 0), stop=(k == KD - 1))
                        else:
                            w = slot(("branch", b, n // 4), 4)
                            all_evacuated(pe, [("ot", b, k) for k in range(BRANCH_K[b])])
                            for k in range(BRANCH_K[b]):
                                last = nc.tensor.matmul(out[:, 0:NTOK], w[:, k, n % 4 * P:(n % 4 + 1) * P], outT[b][:, k, :],
                                                        start=(k == 0), stop=(k == BRANCH_K[b] - 1))
                        last.then_inc(psum_full, 1)

                    for it in GATES_FIRST:
                        branch_item(it)
                    small = slot(("small",), 1)[:, 0, :]
                    pe.wait_ge(sems["norms_ready"], 1)
                    for t in range(NT):
                        out = room(("sgu", t))
                        for g in range(4):
                            last = nc.tensor.matmul(out[:, g * 64:(g + 1) * 64], small[:, S_SW + g * P:S_SW + (g + 1) * P],
                                                    proj[:, t, AV + 64 * g:AV + 64 * (g + 1)], start=True, stop=True)
                        last.then_inc(psum_full, 1)
                    for t in range(4):
                        for g in range(4):
                            if t == NT and g not in TT_CACHE:
                                continue
                            out = room(("tt", t, g))
                            blocks = TT_CACHE[g] if t == NT else list(enumerate(TT_SRC[g]))
                            for i, c in blocks:
                                src = cache[:, c:c + P] if t == NT else proj[:, t, c:c + P]
                                last = nc.tensor.transpose(out[:, i * P:(i + 1) * P], src, ident)
                            last.then_inc(psum_full, 1)
                    all_evacuated(pe, [("tt", 3, 0), ("tt", 2, 0)])
                    for t in range(NT):
                        out = room(("mq", t))
                        for k in range(2):
                            last = nc.tensor.matmul(out[:, 0:384], TT[:, k, t * P:(t + 1) * P],
                                                    small[:, S_UQ + 384 * k:S_UQ + 384 * (k + 1)],
                                                    start=(k == 0), stop=(k == 1))
                        last.then_inc(psum_full, 1)
                    for b in range(4):
                        nc.tensor.matmul(room(("kv", b)), TT[:, 2, b * P:(b + 1) * P], small[:, S_UKV:S_UKV + 512],
                                         start=True, stop=True).then_inc(psum_full, 1)
                    for t in range(NT):
                        out = room(("mqt", t))
                        evacuated(pe, ("mq", t))
                        for h in range(HEADS):
                            last = nc.tensor.transpose(out[0:MQK, h * P:(h + 1) * P], MQ[:, t, h * MQK:(h + 1) * MQK], ident)
                        last.then_inc(psum_full, 1)
                    for b in range(4):
                        out = room(("mkt", b))
                        evacuated(pe, ("kv", b))
                        pe.wait_ge(sems["kb_ready"], 1)
                        for h in range(HEADS):
                            last = nc.tensor.transpose(out[0:MQK, h * P:(h + 1) * P], KB[:, b, h, :], ident)
                        last.then_inc(psum_full, 1)

                    all_evacuated(pe, [("mqt", 2), ("mkt", 3)])
                    all_evacuated(pe, [("tt", t, g) for t in range(4) for g in range(4) if t < NT or g in TT_CACHE])
                    for it in middle_order():
                        if it[0] in ("ot", "gate", "br"):
                            branch_item(it)
                            continue
                        w = it[1]
                        t, kind, h = HEAD_LIST[w]
                        out = room(it)
                        blocks = key_blocks(t)
                        nk = P * len(blocks)
                        k0 = P * blocks[0]
                        if it[0] == "s":
                            if kind == "B":
                                q, k = MQT[0:MQK, h, t * P:(t + 1) * P], MKT[0:MQK, h, k0:k0 + nk]
                            elif kind == "C":
                                lo = 64 * (h % 2)
                                q, k = TT[lo:lo + 64, B_NQ + h // 2, t * P:(t + 1) * P], TT[lo:lo + 64, B_NK + h // 2, k0:k0 + nk]
                            else:
                                lo = 64 * it[2]
                                q, k = TT[lo:lo + 64, B_DQ + h, t * P:(t + 1) * P], TT[lo:lo + 64, B_DK + h, k0:k0 + nk]
                            nc.tensor.matmul(out[:, 0:nk], q, k, start=True, stop=True).then_inc(psum_full, 1)
                        elif it[0] == "pt":
                            r = ROW_OF[(w, 0)]
                            if kind == "D":
                                pe.wait_ge(sems["weights_ready"], sum(1 for q_ in HEAD_LIST[:w + 1] if q_[1] == "D"))
                            else:
                                pe.wait_ge(sems["probs_ready"], r + 1)
                            for i in range(len(blocks)):
                                last = nc.tensor.transpose(out[:, i * P:(i + 1) * P], PB[:, r % P_BUFS, i * P:(i + 1) * P], ident)
                            last.then_inc(psum_full, 1)
                        else:
                            evacuated(pe, ("pt", w))
                            for i, b in enumerate(blocks):
                                if kind == "B":
                                    v = VB[:, b, 64 * h:64 * (h + 1)]
                                elif kind == "C":
                                    v = proj[:, b, NV + 64 * h:NV + 64 * (h + 1)] if b < NT else cache[:, C_NV + 64 * h:C_NV + 64 * (h + 1)]
                                else:
                                    v = proj[:, b, DVO + P * h:DVO + P * (h + 1)] if b < NT else cache[:, C_DV + P * h:C_DV + P * (h + 1)]
                                last = nc.tensor.matmul(out[:, 0:P if kind == "D" else 64], PT[:, w % 2, i, :], v,
                                                        start=(i == 0), stop=(i == len(blocks) - 1))
                            last.then_inc(psum_full, 1)

                    for it in branch_items(3):
                        branch_item(it)
                    pe.wait_ge(sems["merged_ready"], 1)
                    for j in range(2):
                        outb = [room(("mix", j, t)) for t in range(NT)]
                        for half in range(2):
                            w = slot(("out", j, half), 4)
                            for t in range(NT):
                                for k in range(4):
                                    kk = 4 * half + k
                                    last = nc.tensor.matmul(outb[t], mergedT[:, kk, t * P:(t + 1) * P], w[:, k, :],
                                                            start=(kk == 0), stop=(kk == KD - 1))
                                if half == 1:
                                    last.then_inc(psum_full, 1)
                    for t in range(NT):
                        transposed("h2T", xn2, sems["xn_ready"], NT + 1, [t])
                        for it in MOD_LAST[t]:
                            mod_item(it)
                    for t in range(NT):
                        all_evacuated(pe, [("h2T", t, 0), ("h2T", t, 1)])
                        for q in range(2):
                            out = room(("h2", t, q))
                            for k in range(4):
                                last = nc.tensor.transpose(out[:, k * P:(k + 1) * P], hT[:, 4 * q + k, t * P:(t + 1) * P], ident)
                            last.then_inc(psum_full, 1)
                    for i in (2, 3):
                        for q in range(2):
                            spread_gains(i, q)
                    for j in range(4):
                        outb = [room(("pq", 4 * j + n)) for n in range(4)]
                        for kh in range(2):
                            w = slot(("pq", j, kh), 4)
                            for n in range(4):
                                for k in range(4):
                                    kk = 4 * kh + k
                                    last = nc.tensor.matmul(outb[n][:, 0:NTOK], w[:, k, n * P:(n + 1) * P], hT[:, kk, :],
                                                            start=(kk == 0), stop=(kk == KD - 1))
                                if kh == 1:
                                    last.then_inc(psum_full, 1)
                    sub = slot(("sub",), 16)
                    all_evacuated(pe, [("pq", c) for c in range(16)])
                    for t in range(NT):
                        for q in range(4):
                            out = room(("ps", t, q))
                            for i in range(4):
                                c = 4 * q + i
                                last = nc.tensor.matmul(out[:, i * P:(i + 1) * P], qT[:, c, t * P:(t + 1) * P], sub[:, c, :],
                                                        start=True, stop=True)
                            last.then_inc(psum_full, 1)

                    all_evacuated(pe, [("ps", t, q) for t in range(NT) for q in range(4)])
                    pe.wait_ge(sems["zeros_ready"], 1)
                    rows_added, diags_made = sems["rows_added"], sems["diags_made"]
                    pe.sem_inc(rows_added, 2)
                    for t in range(NT):
                        for q in range(2):
                            nc.tensor.matmul(psum[:, 2 * t + q, :], ident, y[:, 0, 0:512], start=True, stop=False)
                        with pe.Fori(0, STEPS) as i:
                            for j in range(2 * GROUP):
                                pe.wait_ge(gotV[j], l * per_layer + i * 16 + 16 * (STEPS * t + 1))
                                pe.wait_ge(diags_made, i * (2 * GROUP) + (2 * GROUP * (STEPS * t + 1) + j + 1))
                                for q in range(2):
                                    last = nc.tensor.matmul(psum[:, 2 * t + q, :], wdiag[:, j, :], ringV[:, j, 512 * q:512 * (q + 1)],
                                                            start=False, stop=False)
                                if j % GROUP == GROUP - 1:
                                    last.then_inc(rows_added, 1)
                        for q in range(2):
                            nc.tensor.matmul(psum[:, 2 * t + q, :], ident, y[:, 0, 0:512], start=False, stop=True)\
                                .then_inc(sems["sum_ready"], 1)

                @block.scalar
                def _(act):
                    cond = [0, 1, 1]

                    def taken(ins):
                        return ins.then_inc(act_evac, 1)

                    lay = bass.ds(l, 1)
                    act.dma_start(cols[:, :], a["cols"][lay].rearrange("a p n -> p (a n)")).then_inc(loaded, 16)
                    act.dma_start(rows[:, :], a["rows"][lay, 0:R_L1G].broadcast_to([P, R_L1G])).then_inc(loaded, 16)
                    act.dma_start(cache, a["cache"][lay].rearrange("a p n -> p (a n)")).then_inc(loaded, 16)
                    act.dma_start(bias.rearrange("p t h n -> p (t h n)"),
                                 a["rpb"][lay].rearrange("a p n -> p (a n)")).then_inc(loaded, 16)

                    def take_gains(i, q):
                        full(act, ("gb", i, q))
                        taken(nc.scalar.copy(gains[:, i % 2, q * 512:(q + 1) * 512], bank(("gb", i, q))))


                    def shift_scale(kind, t, q, sh, sc):
                        full(act, (kind, t, q))
                        evacuated(act, ("modt", 3 if kind == "hT" else 9))
                        for k in range(4):
                            n = 4 * q + k
                            last = nc.scalar.activation(hT[:, n, t * P:(t + 1) * P], bank((kind, t, q))[:, k * P:(k + 1) * P],
                                                        ACT.Identity, bias=modT[:, sh + n, cond[t]:cond[t] + 1],
                                                        scale=modT[:, sc + n, cond[t]:cond[t] + 1])
                        taken(last)

                    sq = [0]

                    def square_roots(width, scale):
                        sq[0] += 1
                        act.wait_ge(sems["sqin"], sq[0])
                        nc.scalar.activation(stat[:, 16:16 + width], stat[:, 0:width], ACT.Sqrt,
                                             bias=consts[:, K_EPS:K_EPS + 1], scale=scale).then_inc(sems["sqout"], 1)

                    square_roots(NT, 1.0)
                    for t in range(NT):
                        shift_scale("hT", t, 0, 0, 8)
                    for j in range(7):
                        width = min(512, IN_W - 512 * j)
                        for t in range(NT):
                            name = ("proj", j, t)
                            if EVAC_BY[INDEX[name]] != "a":
                                continue
                            full(act, name)
                            taken(nc.scalar.activation(proj[:, t, 512 * j:512 * j + width], bank(name)[:, 0:width],
                                                       ACT.Gelu if j == 0 else ACT.Copy))
                    square_roots(3 * NT, 1.0)
                    def branch_item(it):
                        b, n = it[1:]
                        if it[0] == "gb":
                            take_gains(b, n)
                            return
                        full(act, it)
                        if it[0] == "ot":
                            if n == 0 and b >= 2:
                                full(act, ("o", 12 * b - 1))
                            taken(nc.scalar.copy(outT[b][:, n, :], bank(it)[:, 0:NTOK]))
                        elif it[0] == "gate":
                            i = 8 * b + n
                            if 4 <= i < 12:
                                evacuated(act, ("br", 0, i - 4))
                            elif i >= 12:
                                act.wait_ge(sems["merge_done"], i - 11)
                            else:
                                act.wait_ge(sems["bias_ready"], 1)
                            nc.scalar.activation(sg[:, n % 4, :], bank(it)[:, 0:NTOK], ACT.Exp, scale=-1.0,
                                                 bias=cols[:, C_BG + i:C_BG + i + 1]).then_inc(sems["sigmoid_exp"], 1)
                            act.wait_ge(sems["sigmoid_exp"], i + 1)
                            taken(nc.scalar.add(sg[:, n % 4, :], sg[:, n % 4, :], 1.0))

                    for it in GATES_FIRST:
                        branch_item(it)
                    act.wait_ge(sems["lam_in"], 1)
                    nc.scalar.activation(stat[:, 48:50], stat[:, 46:48], ACT.Exp).then_inc(sems["lam_out"], 1)
                    act.wait_ge(sems["new_ready"], 1)
                    for i, (c, width) in enumerate([(CKV, 128), (KR, 32), (NK, 256), (NV, 256), (DK, 512), (DVO, 512)]):
                        act.dma_start(outs[2 + i][lay].rearrange("a p n -> p (a n)"), proj[:, 0, c:c + width])\
                           .then_inc(sems["stored"], 16)
                    for t in range(4):
                        for g in range(1, 4):
                            if t == NT and g not in TT_CACHE:
                                continue
                            name = ("tt", t, g)
                            full(act, name)
                            lo = 2 if (t == NT and g == 1) else 0
                            b0 = TT_FIRST[g]
                            taken(nc.scalar.copy(TT[:, b0 + lo:b0 + 4, t * P:(t + 1) * P],
                                                 bank(name)[:, lo * P:512].rearrange("p (b n) -> p b n", n=P)))
                    for b in range(4):
                        full(act, ("kv", b))
                        src = bank(("kv", b)).rearrange("p (h n) -> p h n", h=HEADS)
                        nc.scalar.copy(KB[:, b, :, 0:NOPE], src[:, :, 0:NOPE])
                        taken(nc.scalar.copy(VB[:, b, :].rearrange("p (h n) -> p h n", h=HEADS), src[:, :, NOPE:NOPE + MV]))
                    for b in range(4):
                        full(act, ("mkt", b))
                        taken(nc.scalar.copy(MKT[0:MQK, :, b * P:(b + 1) * P],
                                             bank(("mkt", b))[0:MQK, :].rearrange("p (h n) -> p h n", h=HEADS)))
                    for it in middle_order():
                        if it[0] == "br":
                            continue
                        if it[0] in ("ot", "gate"):
                            branch_item(it)
                            continue
                        w = it[1]
                        t, kind, h = HEAD_LIST[w]
                        nk = P * len(key_blocks(t))
                        if it[0] == "s":
                            r = ROW_OF[(w, it[2])]
                            if r >= P_BUFS:
                                full(act, ("pt", ROWS[r - P_BUFS][0]))
                            act.wait_ge(sems["negmax_ready"], r + 1)
                            if kind == "C" and t:
                                c = sum(1 for q_ in HEAD_LIST[:w] if q_[1] == "C" and q_[0])
                                src, scale = nbs[:, c % 2, 0:nk], 1.0
                            else:
                                src, scale = bank(it)[:, 0:nk], (MQK if kind == "B" else 64) ** -0.5
                            ins = nc.scalar.activation(PB[:, r % P_BUFS, 0:nk], src, ACT.Exp, bias=stat[:, 64 + r:65 + r],
                                                       scale=scale, accum_out=stat[:, 112 + r:113 + r])
                            ins.then_inc(sems["probs_ready"], 1)
                        elif it[0] == "pt":
                            full(act, it)
                            if w >= 2:
                                full(act, ("o", w - 2))
                            taken(nc.scalar.copy(PT[:, w % 2, 0:nk // P, :],
                                                 bank(it)[:, 0:nk].rearrange("p (b n) -> p b n", n=P)))
                    full(act, ("o", len(HEAD_LIST) - 1))
                    act.dma_start(lnrows, a["rows"][lay, R_L1G:R_L2G].broadcast_to([P, 2 * D])).then_inc(loaded, 16)
                    square_roots(NT * HEADS, 1.0 / DV)
                    for it in branch_items(3):
                        if it[0] != "br":
                            branch_item(it)
                    def last_mods(t):
                        for it in MOD_LAST[t]:
                            j = it[1]
                            full(act, it)
                            if it[0] == "mod":
                                full(act, ("gb", 1, 1))
                                taken(nc.scalar.copy((modrow2 if j == 11 else modrow)[0:2, :], bank(it)[0:2, :]))
                            else:
                                for n in range(4):
                                    last = nc.scalar.activation(modT[:, 4 * j + n, :], bank(it)[:, 2 * n:2 * n + 2], ACT.Identity,
                                                                bias=cols[:, C_BM + 4 * j + n:C_BM + 4 * j + n + 1])
                                taken(last)

                    for t in range(NT):
                        square_roots(1, 1.0)
                        square_roots(1, 1.0)
                        if t:
                            shift_scale("h2T", t - 1, 0, 24, 32)
                            last_mods(t - 1)
                    shift_scale("h2T", NT - 1, 0, 24, 32)
                    last_mods(NT - 1)
                    for t in range(NT):
                        full(act, ("h2", t, 0))
                        taken(nc.scalar.copy(h2[:, t, 0:512], bank(("h2", t, 0))))
                    for i in (2, 3):
                        for q in range(2):
                            take_gains(i, q)
                    for c in range(0, 16, 2):
                        full(act, ("pq", c))
                        taken(nc.scalar.copy(qT[:, c, :], bank(("pq", c))[:, 0:NTOK]))
                    for t in range(NT):
                        for q in (0, 2):
                            full(act, ("ps", t, q))
                            taken(nc.scalar.copy(S[t][:, 4 * q:4 * q + 4, :],
                                                 bank(("ps", t, q)).rearrange("p (c n) -> p c n", n=P)))
                    def softmax_exp(t):
                        act.wait_ge(sems["best_ready"], t + 1)
                        gt = gates[:, t * KSEL:(t + 1) * KSEL]
                        nc.scalar.activation(gt, gt, ACT.Exp).then_inc(sems["gate_exp"], 1)

                    act.sem_inc(sems["diags_made"], 2 * GROUP)

                    def expert_gelus(t, i):
                        for g in range(2):
                            act.wait_ge(sems["dots_ready"], i * (2 * GROUP) + GROUP * (2 * STEPS * t + g + 1))
                            nc.scalar.activation(acts[:, GROUP * g:GROUP * (g + 1)], dots[:, GROUP * g:GROUP * (g + 1)],
                                                 ACT.Gelu).then_inc(sems["gelu_ready"], 1)
                            act.wait_ge(sems["rows_added"], i * 2 + (2 * STEPS * t + g + 1))
                            act.wait_ge(sems["wts_ready"], i * 2 + (2 * STEPS * t + g + 1))
                            for j in range(GROUP * g, GROUP * (g + 1)):
                                nc.scalar.activation(wdiag[:, j, :], ident, ACT.Identity, scale=wts[:, j:j + 1])\
                                    .then_inc(sems["diags_made"], 1)

                    softmax_exp(0)
                    for i in range(STEPS):
                        expert_gelus(0, i)
                        for t, piece in STEP_PIECES[i]:
                            if piece == BEST_PIECE:
                                softmax_exp(t)
                    square_roots(1, 1.0)
                    for t in range(1, NT):
                        with act.Fori(0, STEPS) as i:
                            expert_gelus(t, i)
                        square_roots(1, 1.0)

                @block.vector
                def _(dve):
                    cond = [0, 1, 1]
                    steps = [0]
                    dve_step = sems["dve_step"]

                    def step(ins):
                        steps[0] += 1
                        ins.then_inc(dve_step, 1)

                    def sync():
                        dve.wait_ge(dve_step, steps[0])

                    def link(ins):
                        step(ins)
                        sync()

                    def taken(ins):
                        return ins.then_inc(dve_evac, 1)

                    sq = [0]

                    def roots(width):
                        sync()
                        sq[0] += 1
                        dve.sem_inc(sems["sqin"], 1)
                        dve.wait_ge(sems["sqout"], sq[0])
                        link(nc.vector.reciprocal(stat[:, 32:32 + width], stat[:, 16:16 + width]))

                    bn = stat[:, 160:256]

                    def mean_var(slot_, src, width):
                        nb = (width + 511) // 512
                        part = bn[:, 12 * (slot_ % 3):12 * (slot_ % 3) + 6 * nb]
                        for i in range(nb):
                            step(nc.vector.bn_stats(part[:, 6 * i:6 * i + 6], src[:, i * (width // nb):(i + 1) * (width // nb)]))
                        sync()
                        link(nc.vector.bn_aggr(bn[:, 36 + 2 * slot_:38 + 2 * slot_], part))
                        step(nc.vector.tensor_copy(stat[:, slot_:slot_ + 1], bn[:, 37 + 2 * slot_:38 + 2 * slot_]))

                    def normalised(dst, ts, ready):
                        for i, t in enumerate(ts):
                            nc.vector.tensor_scalar(dst[:, t, :], x[:, t, :], bn[:, 36 + 2 * i:37 + 2 * i], stat[:, 32 + i:33 + i],
                                                    ALU.subtract, ALU.mult).then_inc(ready, 1)

                    def diagonals(pair):
                        for i in pair:
                            for q in range(2):
                                if (i, q) == (0, 0):
                                    evacuated(dve, ("modt", 9))
                                elif (i, q) == (2, 0):
                                    evacuated(dve, ("modt", 11))
                                else:
                                    full(dve, ("gb", (2 * i + q - 1) // 2, (2 * i + q - 1) % 2))
                                base = 16 if i < 2 else 40
                                for k in range(4):
                                    last = nc.vector.tensor_scalar(diag[:, k * P:(k + 1) * P], ident,
                                                                   modT[:, base + 4 * q + k, i % 2:i % 2 + 1], None, ALU.mult)
                                last.then_inc(sems["diag_ready"], 1)

                    for t in range(NT):
                        mean_var(t, x[:, t, :], D)
                    roots(NT)
                    normalised(xn, range(NT), sems["xn_ready"])
                    dve.wait_ge(loaded, 64)
                    for lo in (8, 32):
                        step(nc.vector.tensor_scalar(cols[:, C_BM + lo:C_BM + lo + 8], cols[:, C_BM + lo:C_BM + lo + 8], 1.0, None, ALU.add))
                    nc.vector.tensor_scalar(cols[:, C_BG:C_BG + 32], cols[:, C_BG:C_BG + 32], -1.0, None, ALU.mult)\
                        .then_inc(sems["bias_ready"], 1)
                    sync()

                    def mod_products(j, half):
                        if half == 0:
                            full(dve, ("modt", j - 1))
                        n = SLOT_OF[("mod", j, half)]
                        dve.wait_ge(w_ready[n % W_RING], 16 * (n // W_RING + 1))
                        w = wring[:, n % W_RING * W_SLOT:(n % W_RING + 1) * W_SLOT].rearrange("p (k n) -> p k n", k=4)
                        for k in range(4):
                            for c in range(2):
                                s_ = silu[:, 4 * half + k, c:c + 1]
                                if half == 0 and k == 0:
                                    ins = nc.vector.tensor_scalar(modacc[:, c, :], w[:, k, :], s_, None, ALU.mult)
                                else:
                                    dve.wait_ge(dve_step, steps[0] - 1)
                                    ins = nc.vector.scalar_tensor_tensor(out=modacc[:, c, :], in0=w[:, k, :], scalar=s_,
                                                                         in1=modacc[:, c, :], op0=ALU.mult, op1=ALU.add)
                                step(ins)
                        if half == 1:
                            sync()
                            dve.sem_inc(sems["macc_ready"], 1)

                    def mod_item(it):
                        j = it[1]
                        full(dve, it)
                        if it[0] == "mod":
                            if j:
                                full(dve, ("modt", j - 1))
                            taken(nc.vector.tensor_copy(modrow[0:2, :], bank(it)[0:2, :]))
                        else:
                            taken(nc.vector.tensor_tensor(modT[:, 4 * j:4 * j + 4, :],
                                                          bank(it)[:, 0:8].rearrange("p (n c) -> p n c", c=2),
                                                          spread(cols[:, C_BM + 4 * j:C_BM + 4 * j + 4].unsqueeze(2), 2, 2), ALU.add))

                    for it in MOD_FIRST:
                        mod_item(it)


                    def shift_scale(kind, t, sh, sc):
                        full(dve, (kind, t, 1))
                        evacuated(dve, ("modt", 3 if kind == "hT" else 9))
                        for k in range(4):
                            n = 4 + k
                            last = nc.vector.tensor_scalar(hT[:, n, t * P:(t + 1) * P], bank((kind, t, 1))[:, k * P:(k + 1) * P],
                                                           modT[:, sc + n, cond[t]:cond[t] + 1],
                                                           modT[:, sh + n, cond[t]:cond[t] + 1], ALU.mult, ALU.add)
                        taken(last)

                    for t in range(NT):
                        shift_scale("hT", t, 0, 8)
                    for t in range(2):
                        for h in range(HEADS):
                            step(nc.vector.tensor_tensor(bias[:, t, h, :], bias[:, t, h, :], consts[:, K_MA:K_MA + 256], ALU.add))
                    for it in PROJ_ORDER:
                        if it[0] == "macc":
                            mod_products(it[1], it[2])
                        elif it[0] == "modt":
                            mod_item(it)
                    all_evacuated(dve, [("proj", j, t) for j in range(7) for t in range(NT)])
                    for t in range(NT):
                        mean_var(t, proj[:, t, AV:AV + 256], 256)
                        for i, (c, width) in enumerate([(CQ, 256), (CKV, 128)]):
                            n = 3 + 3 * i + t
                            mean_var(n, proj[:, t, c:c + width], width)
                            sync()
                            link(nc.vector.scalar_tensor_tensor(out=stat[:, n:n + 1], in0=bn[:, 36 + 2 * n:37 + 2 * n],
                                                                scalar=bn[:, 36 + 2 * n:37 + 2 * n],
                                                                in1=bn[:, 37 + 2 * n:38 + 2 * n], op0=ALU.mult, op1=ALU.add))
                    roots(3 * NT)
                    for t in range(NT):
                        av = proj[:, t, AV:AV + 256]
                        step(nc.vector.tensor_scalar(av, av, bn[:, 36 + 2 * t:37 + 2 * t], stat[:, 32 + t:33 + t], ALU.subtract, ALU.mult))
                        cq = proj[:, t, CQ:CQ + 256]
                        step(nc.vector.tensor_scalar(cq, cq, stat[:, 35 + t:36 + t], None, ALU.mult))
                        ck = proj[:, t, CKV:CKV + P]
                        step(nc.vector.scalar_tensor_tensor(out=ck, in0=ck, scalar=stat[:, 38 + t:39 + t],
                                                            in1=rows[:, R_KVG:R_KVG + P], op0=ALU.mult, op1=ALU.mult))
                    sync()
                    for t in range(NT):
                        av = proj[:, t, AV:AV + 256]
                        step(nc.vector.tensor_tensor(av, av, rows[:, R_SG:R_SG + 256], ALU.mult))
                    sync()
                    dve.sem_inc(sems["new_ready"], 1)

                    def rotate(dst, src, t, groups, half, kc, ks):
                        cs = spread(consts[:, kc + (t - 1) * half:kc + t * half].unsqueeze(1), 1, groups)
                        sn = spread(consts[:, ks + (t - 1) * half:ks + t * half].unsqueeze(1), 1, groups)
                        x1, x2 = src[:, :, 0:half], src[:, :, half:2 * half]
                        bufs = [hold[:, i * groups * half:(i + 1) * groups * half].rearrange("p (g n) -> p g n", g=groups)
                                for i in range(4)]
                        for b_, (u, v) in zip(bufs, [(x1, cs), (x2, sn), (x2, cs), (x1, sn)]):
                            step(nc.vector.tensor_tensor(b_, u, v, ALU.mult))
                        sync()
                        step(nc.vector.tensor_tensor(dst[:, :, 0:half], bufs[0], bufs[1], ALU.subtract))
                        return nc.vector.tensor_tensor(dst[:, :, half:2 * half], bufs[2], bufs[3], ALU.add)

                    hold = TT[:, B_DQ:B_DQ + 4, :].rearrange("p b n -> p (b n)")
                    for t in (1, 2):
                        step(rotate(proj[:, t, DQ:DQ + 1024].rearrange("p (g n) -> p g n", g=16),
                                    proj[:, t, DQ:DQ + 1024].rearrange("p (g n) -> p g n", g=16), t, 16, 32, K_C32, K_S32))
                        sync()
                        step(rotate(proj[:, t, KR:KR + 32].rearrange("p (g n) -> p g n", g=1),
                                    proj[:, t, KR:KR + 32].rearrange("p (g n) -> p g n", g=1), t, 1, 16, K_C16, K_S16))
                        sync()
                    dve.sem_inc(sems["norms_ready"], 1)
                    for i in range(2):
                        q1 = rows[:, R_LAM + 128 * i:R_LAM + 128 * i + 64]
                        k1 = rows[:, R_LAM + 128 * i + 64:R_LAM + 128 * i + 128]
                        step(nc.vector.tensor_tensor(q1, q1, k1, ALU.mult))
                    sync()
                    step(nc.vector.tensor_reduce(stat[:, 46:48], rows[:, R_LAM:R_LAM + 256].rearrange("p (i n) -> p i n", i=2)[:, :, 0:64],
                                                 AX.X, ALU.add))
                    sync()
                    dve.sem_inc(sems["lam_in"], 1)
                    dve.wait_ge(sems["lam_out"], 1)
                    link(nc.vector.tensor_tensor(stat[:, 50:51], stat[:, 49:50], stat[:, 48:49], ALU.subtract))
                    link(nc.vector.tensor_tensor(stat[:, 51:52], stat[:, 50:51], cols[:, C_LI:C_LI + 1], ALU.subtract))
                    step(nc.vector.tensor_scalar(rows[:, R_DG:R_DG + P], rows[:, R_DG:R_DG + P], cols[:, C_LI + 1:C_LI + 2], None, ALU.mult))
                    neglam = stat[:, 51:52]
                    for t in range(NT):
                        full(dve, ("sgu", t))
                        for g in range(4):
                            u = proj[:, t, AU + 64 * g:AU + 64 * (g + 1)]
                            last = nc.vector.scalar_tensor_tensor(out=u, in0=bank(("sgu", t))[:, 64 * g:64 * (g + 1)],
                                                                  scalar=cols[:, C_SB + g:C_SB + g + 1], in1=u,
                                                                  op0=ALU.add, op1=ALU.mult)
                        taken(last)
                    for t in range(4):
                        name = ("tt", t, 0)
                        full(dve, name)
                        if t < NT:
                            for k in range(2):
                                nc.vector.tensor_scalar(TT[:, k, t * P:(t + 1) * P], bank(name)[:, k * P:(k + 1) * P],
                                                        cols[:, C_QG + k:C_QG + k + 1], None, ALU.mult)
                        taken(nc.vector.tensor_copy(TT[:, 2, t * P:(t + 1) * P], bank(name)[:, 2 * P:3 * P]))
                    for b in range(4):
                        src = spread((cache[:, C_KR:C_KR + 32] if b == NT else proj[:, b, KR:KR + 32]).unsqueeze(1), 1, HEADS)
                        step(nc.vector.tensor_copy(KB[:, b, :, NOPE:MQK], src))
                    sync()
                    dve.sem_inc(sems["kb_ready"], 1)
                    hold = nbs.rearrange("p r n -> p (r n)")
                    for t in range(NT):
                        full(dve, ("mq", t))
                        src = bank(("mq", t))[:, 0:384].rearrange("p (h n) -> p h n", h=HEADS)
                        dst = MQ[:, t, :].rearrange("p (h n) -> p h n", h=HEADS)
                        if t == 0:
                            taken(nc.vector.tensor_copy(dst, src))
                        else:
                            sync()
                            step(nc.vector.tensor_copy(dst[:, :, 0:NOPE], src[:, :, 0:NOPE]))
                            taken(rotate(dst[:, :, NOPE:MQK], src[:, :, NOPE:MQK], t, HEADS, 16, K_C16, K_S16))
                            evacuated(dve, ("mq", t))
                    for t in range(NT):
                        full(dve, ("mqt", t))
                        taken(nc.vector.tensor_copy(MQT[0:MQK, :, t * P:(t + 1) * P],
                                                    bank(("mqt", t))[0:MQK, :].rearrange("p (h n) -> p h n", h=HEADS)))

                    negmax = sems["negmax_ready"]
                    def branch_item(it):
                        b, n = it[1:]
                        evacuated(dve, ("gate", b, n))
                        link(nc.vector.reciprocal(sg[:, n % 4, :], sg[:, n % 4, :]))
                        full(dve, it)
                        dst = mergedT[:, n, :] if b == 0 else sg[:, n % 4, :]
                        taken(nc.vector.tensor_tensor(dst, bank(it)[:, 0:NTOK], sg[:, n % 4, :], ALU.mult))
                        if b:
                            evacuated(dve, it)
                            nc.vector.tensor_tensor(mergedT[:, n, :], mergedT[:, n, :], sg[:, n % 4, :], ALU.add)\
                                .then_inc(sems["merge_done"], 1)

                    for it in middle_order():
                        if it[0] == "br":
                            branch_item(it)
                            continue
                        if it[0] in ("ot", "gate"):
                            continue
                        w = it[1]
                        t, kind, h = HEAD_LIST[w]
                        nk = P * len(key_blocks(t))
                        if it[0] == "s":
                            r = ROW_OF[(w, it[2])]
                            full(dve, it)
                            nm = stat[:, 64 + r:65 + r]
                            if kind == "C" and t:
                                c = sum(1 for q_ in HEAD_LIST[:w] if q_[1] == "C" and q_[0])
                                if c >= 2:
                                    dve.wait_ge(sems["probs_ready"], ROW_OF[(HEAD_LIST.index((1 + (c - 2) // 4, "C", (c - 2) % 4)), 0)] + 1)
                                step(nc.vector.scalar_tensor_tensor(out=nbs[:, c % 2, 0:256], in0=bank(it)[:, 0:256], scalar=NA_D ** -0.5,
                                                                    in1=bias[:, t - 1, h, :], op0=ALU.mult, op1=ALU.add))
                                taken(nc.vector.tensor_scalar(nbs[:, c % 2, 256:384], bank(it)[:, 256:384], NA_D ** -0.5, None, ALU.mult))
                                evacuated(dve, it)
                                nc.vector.tensor_reduce(nm, nbs[:, c % 2, :], AX.X, ALU.max, negate=True).then_inc(negmax, 1)
                            else:
                                link(nc.vector.tensor_reduce(nm, bank(it)[:, 0:nk], AX.X, ALU.max, negate=True))
                                nc.vector.tensor_scalar(nm, nm, (MQK if kind == "B" else 64) ** -0.5, None, ALU.mult).then_inc(negmax, 1)
                        elif it[0] == "pt":
                            r = ROW_OF[(w, 0)]
                            nr = 2 if kind == "D" else 1
                            dve.wait_ge(sems["probs_ready"], r + nr)
                            rr = stat[:, 112 + r:112 + r + nr]
                            link(nc.vector.reciprocal(rr, rr))
                            if kind == "D":
                                link(nc.vector.tensor_tensor(stat[:, 113 + r:114 + r], stat[:, 113 + r:114 + r], neglam, ALU.mult))
                                p1, p2 = PB[:, r % P_BUFS, 0:nk], PB[:, (r + 1) % P_BUFS, 0:nk]
                                link(nc.vector.tensor_scalar(p2, p2, stat[:, 113 + r:114 + r], None, ALU.mult))
                                nc.vector.scalar_tensor_tensor(out=p1, in0=p1, scalar=stat[:, 112 + r:113 + r], in1=p2,
                                                               op0=ALU.mult, op1=ALU.add).then_inc(sems["weights_ready"], 1)
                        else:
                            r = ROW_OF[(w, 0)]
                            full(dve, it)
                            if w == 0:
                                dve.wait_ge(sems["stored"], 16 * 6)
                            if kind == "D":
                                taken(nc.vector.tensor_copy(proj[:, t, OUT_D + P * h:OUT_D + P * (h + 1)], bank(it)[:, 0:P]))
                            else:
                                c = (OUT_B if kind == "B" else OUT_C) + 64 * h
                                taken(nc.vector.tensor_scalar(proj[:, t, c:c + 64], bank(it)[:, 0:64], stat[:, 112 + r:113 + r], None, ALU.mult))
                    evacuated(dve, ("o", len(HEAD_LIST) - 1))
                    full(dve, ("o", len(HEAD_LIST) - 1))
                    for t in range(NT):
                        for h in range(HEADS):
                            n = HEADS * t + h
                            od = proj[:, t, OUT_D + P * h:OUT_D + P * (h + 1)]
                            step(nc.vector.tensor_tensor_reduce(TT[:, n, 0:P], od, od, 1.0, 0.0, ALU.mult, ALU.add, stat[:, n:n + 1]))
                    roots(NT * HEADS)
                    for t in range(NT):
                        for h in range(HEADS):
                            n = HEADS * t + h
                            od = proj[:, t, OUT_D + P * h:OUT_D + P * (h + 1)]
                            step(nc.vector.scalar_tensor_tensor(out=od, in0=od, scalar=stat[:, 32 + n:33 + n], in1=rows[:, R_DG:R_DG + P],
                                                                op0=ALU.mult, op1=ALU.mult))
                    sync()
                    dve.sem_inc(sems["outs_ready"], 1)
                    diagonals((0, 1))
                    for it in branch_items(3):
                        if it[0] == "br":
                            branch_item(it)
                    dve.wait_ge(sems["merge_done"], 3 * KD)
                    dve.sem_inc(sems["merged_ready"], 1)

                    def residual(t, j, src, gain):
                        xs = x[:, t, 512 * j:512 * (j + 1)]
                        tb = tmp if gain < 2 else y[:, 1, 512 * j:512 * (j + 1)]
                        first = nc.vector.tensor_tensor(tb, src, gains[:, gain % 2, 512 * j:512 * (j + 1)], ALU.mult)
                        return first, (lambda: nc.vector.scalar_tensor_tensor(out=xs, in0=xs, scalar=ALPHA, in1=tb,
                                                                              op0=ALU.mult, op1=ALU.add))

                    all_evacuated(dve, [("gb", i, q) for i in (0, 1) for q in range(2)])
                    def take_mix(j, t):
                        full(dve, ("mix", j, t))
                        first, second = residual(t, j, bank(("mix", j, t)), cond[t])
                        taken(first)
                        evacuated(dve, ("mix", j, t))
                        link(second())

                    for j in range(2):
                        for t in range(NT):
                            take_mix(j, t)

                    def affine(ts, ready):
                        for i, t in enumerate(ts):
                            ins = nc.vector.scalar_tensor_tensor(out=x[:, t, :], in0=x[:, t, :], scalar=stat[:, 32 + i:33 + i],
                                                                 in1=lnrows[:, D:2 * D], op0=ALU.mult, op1=ALU.add)
                            if ready is None:
                                step(ins)
                            else:
                                ins.then_inc(ready, 1)

                    def layer_norm(ts):
                        for i, t in enumerate(ts):
                            mean_var(i, x[:, t, :], D)
                        roots(len(ts))
                        for i, t in enumerate(ts):
                            step(nc.vector.scalar_tensor_tensor(out=x[:, t, :], in0=x[:, t, :], scalar=bn[:, 36 + 2 * i:37 + 2 * i],
                                                                in1=lnrows[:, 0:D], op0=ALU.subtract, op1=ALU.mult))
                        sync()

                    dve.wait_ge(loaded, 80)
                    for t in range(NT):
                        layer_norm([t])
                        affine([t], None)
                        sync()
                        mean_var(0, x[:, t, :], D)
                        roots(1)
                        normalised(xn2, [t], sems["xn_ready"])
                        if t:
                            shift_scale("h2T", t - 1, 24, 32)
                    dve.sem_inc(sems["ln1_done"], 1)
                    shift_scale("h2T", NT - 1, 24, 32)
                    diagonals((2, 3))
                    for t in range(NT):
                        full(dve, ("h2", t, 1))
                        taken(nc.vector.tensor_copy(h2[:, t, 512:1024], bank(("h2", t, 1))))
                    for c in range(1, 16, 2):
                        full(dve, ("pq", c))
                        taken(nc.vector.tensor_copy(qT[:, c, :], bank(("pq", c))[:, 0:NTOK]))
                    for t in range(NT):
                        for q in (1, 3):
                            full(dve, ("ps", t, q))
                            taken(nc.vector.tensor_copy(S[t][:, 4 * q:4 * q + 4, :],
                                                        bank(("ps", t, q)).rearrange("p (c n) -> p c n", n=P)))

                    def top16(n, src, vals, idxs):
                        for c in range(n):
                            step(nc.vector.max(vals(c)[:, 0:8], src(c)))
                        sync()
                        yield
                        for c in range(n):
                            step(nc.vector.max_index(idxs(c)[:, 0:8], vals(c)[:, 0:8], src(c)))
                        sync()
                        yield
                        for c in range(n):
                            step(nc.vector.match_replace(src(c), vals(c)[:, 0:8], src(c), LOWEST))
                        sync()
                        yield
                        for c in range(n):
                            step(nc.vector.max(vals(c)[:, 8:16], src(c)))
                        sync()
                        yield
                        for c in range(n):
                            step(nc.vector.max_index(idxs(c)[:, 8:16], vals(c)[:, 8:16], src(c)))
                        sync()

                    def top_experts(t):
                        all_evacuated(dve, [("ps", t, q) for q in range(4)])
                        yield from top16(16, lambda c: S[t][:, c, :], lambda c: v16[:, c, :], lambda c: i16[:, c, :])
                        yield
                        step(nc.vector.tensor_copy(i16f, i16))
                        vv = v16.rearrange("p (h m) k -> p h m k", m=2)
                        for h in range(PH):
                            step(nc.vector.tensor_tensor(cand[:, 256 * h:256 * (h + 1)].rearrange("p (a b) -> p a b", a=16),
                                                         spread(vv[:, h, 0, :].unsqueeze(2), 2, 16),
                                                         spread(vv[:, h, 1, :].unsqueeze(1), 1, 16), ALU.add))
                        sync()
                        yield
                        bv = bi[:, 0, :].rearrange("p (h k) -> p h k", h=PH)
                        yield from top16(PH, lambda h: cand[:, 256 * h:256 * (h + 1)], lambda h: best[:, h, :], lambda h: bv[:, h, :])
                        yield
                        gt = gates[:, t * KSEL:(t + 1) * KSEL].rearrange("p (h k) -> p h k", h=PH)
                        nc.vector.tensor_tensor(gt, best, spread(best[:, :, 0:1], 2, TOPK), ALU.subtract)\
                            .then_inc(sems["best_ready"], 1)
                        step(nc.vector.tensor_scalar(bi[:, 1, :], bi[:, 0, :], 4, None, ALU.logical_shift_right))
                        sync()
                        step(nc.vector.tensor_copy(selA, bi[:, 1, :]))
                        sync()
                        step(nc.vector.tensor_scalar(bi[:, 1, :], bi[:, 0, :], 15, None, ALU.bitwise_and))
                        sync()
                        step(nc.vector.tensor_copy(selB, bi[:, 1, :]))
                        sync()
                        yield
                        iota = spread(consts[:, K_IO:K_IO + 16].unsqueeze(1), 1, KSEL)
                        ii = i16f.rearrange("p (h m) k -> p h m k", m=2)
                        for m, sel in ((0, selA), (1, selB)):
                            e3 = eq.rearrange("p (n k) -> p n k", n=KSEL)
                            step(nc.vector.tensor_tensor(e3, spread(sel.unsqueeze(2), 2, 16), iota, ALU.is_equal))
                            sync()
                            for h in range(PH):
                                eh = eq[:, 256 * h:256 * (h + 1)].rearrange("p (n k) -> p n k", n=TOPK)
                                step(nc.vector.tensor_tensor(eh, eh, spread(ii[:, h, m, :].unsqueeze(1), 1, TOPK), ALU.mult))
                            sync()
                            step(nc.vector.tensor_reduce(sel, e3, AX.X, ALU.add))
                            sync()
                            yield
                        step(nc.vector.scalar_tensor_tensor(out=selA, in0=selA, scalar=float(NKEYS), in1=selB, op0=ALU.mult, op1=ALU.add))
                        sync()
                        step(nc.vector.tensor_scalar(selA, selA, cols[:, C_LO:C_LO + 1], None, ALU.add))
                        sync()
                        step(nc.vector.tensor_copy(experts[:, t * KSEL:(t + 1) * KSEL], selA))
                        dve.wait_ge(sems["gate_exp"], t + 1)
                        step(nc.vector.tensor_reduce(stat[:, 0:PH], gt, AX.X, ALU.add))
                        sync()
                        step(nc.vector.reciprocal(stat[:, 32:32 + PH], stat[:, 0:PH]))
                        sync()
                        step(nc.vector.tensor_tensor(gt, gt, spread(stat[:, 32:32 + PH].unsqueeze(2), 2, TOPK), ALU.mult))
                        sync()
                        yield

                    nc.vector.memset(y[:, 0, 0:512], 0.0).then_inc(sems["zeros_ready"], 1)
                    pieces = [top_experts(t) for t in range(NT)]
                    for _ in range(TOPK_PIECES):
                        next(pieces[0])

                    for g in range(2):
                        nc.vector.tensor_copy(exslot[:, GROUP * g:GROUP * (g + 1)], experts[:, GROUP * g:GROUP * (g + 1)])\
                            .then_inc(sems["experts_ready"], 1)
                    def expert_step(t, i):
                        for g in range(2):
                            for j in range(GROUP * g, GROUP * (g + 1)):
                                dve.wait_ge(gotU[j], l * per_layer + i * 16 + 16 * (STEPS * t + 1))
                                nc.vector.tensor_tensor_reduce(ringU[:, j, :], ringU[:, j, :], h2[:, t, :], 1.0, 0.0,
                                                               ALU.mult, ALU.add, dots[:, j:j + 1]).then_inc(sems["dots_ready"], 1)
                            for j in range(GROUP * g, GROUP * (g + 1)):
                                dve.wait_ge(gotV[j], l * per_layer + i * 16 + 16 * (STEPS * t + 1))
                            dve.wait_ge(sems["dots_ready"], i * (2 * GROUP) + GROUP * (2 * STEPS * t + g + 1))
                            nc.vector.tensor_copy(exslot[:, GROUP * g:GROUP * (g + 1)],
                                                  experts[:, bass.ds(i * 2 * GROUP + (t * KSEL + 2 * GROUP + GROUP * g), GROUP)])\
                                .then_inc(sems["experts_ready"], 1)
                            dve.wait_ge(sems["gelu_ready"], i * 2 + (2 * STEPS * t + g + 1))
                            dve.wait_ge(sems["diags_made"], i * (2 * GROUP) + (2 * GROUP * STEPS * t + GROUP * (g + 1)))
                            nc.vector.tensor_tensor(wts[:, GROUP * g:GROUP * (g + 1)], acts[:, GROUP * g:GROUP * (g + 1)],
                                                    gates[:, bass.ds(i * 2 * GROUP + (t * KSEL + GROUP * g), GROUP)],
                                                    ALU.mult).then_inc(sems["wts_ready"], 1)

                    for t in range(NT):
                        if t == 0:
                            for i in range(STEPS):
                                expert_step(t, i)
                                for tile, _ in STEP_PIECES[i]:
                                    next(pieces[tile])
                        else:
                            with dve.Fori(0, STEPS) as i:
                                expert_step(t, i)
                        dve.wait_ge(sems["sum_ready"], 2 * (t + 1))
                        all_evacuated(dve, [("gb", i, q) for i in (2, 3) for q in range(2)])
                        for j in range(2):
                            first, second = residual(t, j, psum[:, 2 * t + j, :], 2 + cond[t])
                            link(first)
                            link(second())
                        dve.wait_ge(loaded, 96)
                        layer_norm([t])
                        affine([t], sems["x_ready"])
                    dve.wait_ge(sems["x_ready"], NT)

                @block.gpsimd
                def _(pool):
                    for t in range(NT):
                        with pool.Fori(0, STEPS) as i:
                            for g in range(2):
                                for ring, table, got in ((ringU, "peer_u", gotU), (ringV, "peer_v", gotV)):
                                    if table == "peer_u":
                                        pool.wait_ge(sems["experts_ready"], i * 2 + (2 * STEPS * t + g + 1))
                                    else:
                                        pool.wait_ge(sems["rows_added"], i * 2 + (2 * STEPS * t + g + 1))
                                    pool.sem_inc(gather_gate, 1)
                                    for j in range(GROUP * g, GROUP * (g + 1)):
                                        pool.indirect_dma_start(ring[:, j, :], None, a[table],
                                                                bass.IndirectOffsetOnAxis(ap=exslot[:, j:j + 1], axis=0))\
                                            .then_inc(got[j], 16)
            nc.all_engine_barrier()
            for s in list(sems.values()) + w_ready:
                nc.gpsimd.sem_clear(s)
            nc.all_engine_barrier()


_OUTS = [(1, 128, 1024), (1, 256, 1024), (2, 128, 128), (2, 128, 32), (2, 128, 256), (2, 128, 256), (2, 128, 512), (2, 128, 512)]
_SHAPES = [(1, 128, 1024), (1, 256, 1024), (1, 2, 128, 128), (1, 2, 128, 32), (1, 2, 128, 4, 64), (1, 2, 128, 4, 64),
           (1, 2, 128, 4, 128), (1, 2, 128, 4, 128)]


def shape_constants():
    c = np.zeros((P, K_W), np.float32)
    c[:, K_ID:K_ID + P] = np.eye(P)
    c[:, K_ON:K_ON + P] = 1
    col = np.arange(GRID_W)
    start = np.clip(col - 8, 0, GRID_W - 16)
    inside = (col[None] >= start[:, None]) & (col[None] < start[:, None] + 16)
    c[:, K_MA:K_MA + 256] = np.tile(np.where(inside, 0.0, NEG_BIG), (2, 4))
    c[:, K_IO:K_IO + 16] = np.arange(16)
    c[:, K_EPS] = EPS
    tok = np.arange(256)
    for half, kc, ks in ((16, K_C16, K_S16), (32, K_C32, K_S32)):
        nf = half // 2
        inv = (np.float32(10000.0) ** (-np.arange(nf, dtype=np.float32) / nf)).astype(np.float32)
        row, cc = (tok // GRID_W).astype(np.float32), (tok % GRID_W).astype(np.float32)
        ang = np.concatenate([row[:, None] * inv, cc[:, None] * inv], 1).astype(np.float32)
        for t in range(2):
            c[:, kc + t * half:kc + (t + 1) * half] = np.cos(ang[t * P:(t + 1) * P])
            c[:, ks + t * half:ks + (t + 1) * half] = np.sin(ang[t * P:(t + 1) * P])
    return c


def layouts(v):
    cat = np.concatenate
    lam = cat([v[n] for n in ("diff_lambda_q1", "diff_lambda_k1", "diff_lambda_q2", "diff_lambda_k2")], 1)
    rows = cat([v["sgu_norm_g"], v["mla_kv_norm_g"], v["diff_norm_g"], lam, v["ln1_g"], v["ln1_b"], v["ln2_g"], v["ln2_b"]], 1)
    colT = lambda w, n: w.reshape(DEPTH, n, P).transpose(0, 2, 1)
    init = [0.8 - 0.6 * math.exp(-0.3 * l) for l in range(DEPTH)]
    fixed = np.zeros((DEPTH, P, 3), np.float32)
    for l in range(DEPTH):
        fixed[l] = [init[l], 1 - init[l], l * NEXP]
    cols = cat([colT(v["b_mod"], 48), colT(v["b_gate"], 32), v["sgu_b"].transpose(0, 2, 1), colT(v["mla_q_norm_g"], 2), fixed], 2)
    flat = lambda w: w[0].reshape(DEPTH, P, -1)
    cache = cat([flat(v[n]) for n in ("cache_mla_ckv", "cache_mla_krope", "cache_na_k", "cache_na_v", "cache_diff_k", "cache_diff_v")], 2)
    q = np.arange(2 * P)
    r, c = q // GRID_W, q % GRID_W
    dr = r[None, :] - r[:, None] + 7
    dc = np.clip(c[None, :] - c[:, None], -15, 15) + 15
    rpb = v["na_rpb"][:, :, dr, dc].reshape(DEPTH, HEADS, 2, P, 256).transpose(0, 3, 2, 1, 4).reshape(DEPTH, P, -1)
    uq = v["mla_w_uq"].reshape(DEPTH, 2, P, 384).transpose(0, 2, 1, 3).reshape(DEPTH, P, 768)
    sgw = v["sgu_w"].transpose(0, 3, 1, 2).reshape(DEPTH, P, 512)
    small = cat([uq, v["mla_w_ukv"], sgw], 2)
    subT = v["peer_subkeys"].reshape(DEPTH, 16, P, P).transpose(0, 3, 1, 2).reshape(DEPTH, P, 2048)
    cond = np.stack([v["c_ctx"].reshape(KD, P).T, v["c"][0].reshape(KD, P).T], 2)
    out = dict(rows=rows, cols=cols, cache=cache, rpb=rpb, small=small, subT=subT, cond=cond, consts=shape_constants())
    for n in ("x_prompt", "x_sample", "w_mod", "w_in", "w_gate", "w_out", "peer_w_q", "w_branch_a", "w_branch_b", "w_branch_c", "w_branch_d"):
        out[n] = v[n]
    for n in ("peer_u", "peer_v"):
        out[n] = v[n].reshape(DEPTH * NEXP, D)
    return {n: np.ascontiguousarray(w) for n, w in out.items()}


def kernel(**inputs):
    import concourse.bacc as _bacc
    from concourse.bass_utils import run_bass_kernel_spmd as _run

    nc = _bacc.Bacc("TRN2", target_bir_lowering=False, num_devices=1)
    arrays = {f"in_{n}": w for n, w in layouts({k: np.asarray(w) for k, w in inputs.items()}).items()}
    a = {n[3:]: nc.dram_tensor(n, w.shape, F32, kind="ExternalInput").ap() for n, w in arrays.items()}
    outs = [nc.dram_tensor(f"out_{i}", s, F32, kind="ExternalOutput").ap() for i, s in enumerate(_OUTS)]
    build(nc, a, outs)
    r = _run(nc, [arrays], core_ids=[0])
    return tuple(r.results[0][f"out_{i}"].reshape(s) for i, s in enumerate(_SHAPES))
```
